# Optimizing a Trainium2 kernel written in Bass

```python
import math
import jax, jax.numpy as jnp
from jax import lax
import numpy as np

D_MODEL = 1024
BATCH = 1
SEQ = 1024
DEPTH = 1
DEC_BATCH = 8
DEC_SEQ = 1
PAST_LEN = 1024
PAGE_SIZE = 128

D_RNN = D_MODEL
N_LRU_BLOCKS = 16
LRU_BLOCK = D_RNN // N_LRU_BLOCKS
CONV_WIDTH = 4
LRU_C = 8.0
HEAD_DIM = 64
HEADS_PER_GROUP = 8
DILATED_GROUPS = ((128, 1), (512, 4), (2048, 16))
N_GROUPS = len(DILATED_GROUPS)
N_ATT_HEADS = N_GROUPS * HEADS_PER_GROUP
ATT_WIDTH = N_ATT_HEADS * HEAD_DIM
ATT_OUT = HEADS_PER_GROUP * HEAD_DIM
BAND_BLOCK = 128
NUM_BUCKETS = 32
MAX_DISTANCE = 2048
D_FF = -(-8 * D_MODEL // (3 * 256)) * 256
EPS = 1e-6
D_IN = 2 * D_RNN + 3 * ATT_WIDTH
SPLITS = (D_RNN, 2 * D_RNN, 2 * D_RNN + ATT_WIDTH, 2 * D_RNN + 2 * ATT_WIDTH)

kernel_name = "hawk_dilated_hybrid_step"

def rmsnorm(x, g):
    xf = x.astype(jnp.float32)
    y = xf * lax.rsqrt(jnp.mean(xf * xf, axis=-1, keepdims=True) + EPS)
    return (y * g.astype(jnp.float32)).astype(x.dtype)

def t5_bucket(dist):
    max_exact = NUM_BUCKETS // 2
    d_f = jnp.maximum(dist, 1).astype(jnp.float32)
    large = max_exact + (jnp.log(d_f / max_exact) / math.log(MAX_DISTANCE / max_exact)
                         * (NUM_BUCKETS - max_exact)).astype(jnp.int32)
    large = jnp.minimum(large, NUM_BUCKETS - 1)
    return jnp.where(dist < max_exact, dist, large)

def causal_conv(x_ext, w, b):
    T = x_ext.shape[1] - (CONV_WIDTH - 1)
    out = b
    for k in range(CONV_WIDTH):
        out = out + w[k] * x_ext[:, k:k + T]
    return out

def rg_lru(x, pos, h0, w_a, b_a, w_x, b_x, lam):
    B, T, _ = x.shape
    xb = x.reshape(B, T, N_LRU_BLOCKS, LRU_BLOCK)
    gate_a = jnp.einsum('btni,nij->btnj', xb, w_a).reshape(B, T, D_RNN) + b_a
    gate_x = jnp.einsum('btni,nij->btnj', xb, w_x).reshape(B, T, D_RNN) + b_x
    r = jax.nn.sigmoid(gate_a.astype(jnp.float32))
    i = jax.nn.sigmoid(gate_x.astype(jnp.float32))
    log_a = -LRU_C * r * jax.nn.softplus(-lam.astype(jnp.float32))
    a = jnp.exp(log_a)
    mult = jnp.sqrt(-jnp.expm1(2.0 * log_a))
    mult = jnp.where((pos == 0)[None, :, None], 1.0, mult)
    u = mult * i * x.astype(jnp.float32)

    def step(h, au):
        a_t, u_t = au
        h = a_t * h + u_t
        return h, h

    h_T, hs = lax.scan(step, h0.astype(jnp.float32),
                       (jnp.swapaxes(a, 0, 1), jnp.swapaxes(u, 0, 1)))
    return jnp.swapaxes(hs, 0, 1).astype(x.dtype), h_T

def dilated_attn_prompt(q, k, v, tab, window, dil):
    B, S, H, E = q.shape
    BB = BAND_BLOCK
    band = window // dil
    n = S // dil
    nb = -(-n // BB)
    n_pad = nb * BB

    def to_res(t):
        t = jnp.swapaxes(t.reshape(B, n, dil, H, E), 1, 2)
        return jnp.pad(t, ((0, 0), (0, 0), (0, n_pad - n), (0, 0), (0, 0)))

    def key_blocks(t):
        tp = jnp.pad(t, ((0, 0), (0, 0), (BB, 0), (0, 0), (0, 0))).reshape(B, dil, nb + 1, BB, H, E)
        return jnp.concatenate([tp[:, :, :-1], tp[:, :, 1:]], axis=3)

    qb = to_res(q).reshape(B, dil, nb, BB, H, E)
    kb = key_blocks(to_res(k))
    vb = key_blocks(to_res(v))
    s = jnp.einsum('brcqhe,brckhe->brchqk', qb, kb,
                   preferred_element_type=jnp.float32) * (HEAD_DIM ** -0.5)
    qi = jnp.arange(BB)[:, None]
    ki = jnp.arange(2 * BB)[None, :]
    sub_dist = qi + BB - ki
    in_band = (sub_dist >= 0) & (sub_dist <= band)
    bias = tab[t5_bucket(jnp.clip(sub_dist, 0, band) * dil)].astype(jnp.float32)
    bias = jnp.transpose(bias, (2, 0, 1))
    key_sub = jnp.arange(nb)[:, None, None] * BB - BB + ki[None]
    valid = in_band[None] & (key_sub >= 0)
    s = jnp.where(valid[:, None], s + bias, -jnp.inf)
    m = jnp.max(s, axis=-1)
    p = jnp.exp(s - m[..., None])
    l = jnp.sum(p, axis=-1)
    o = jnp.einsum('brchqk,brckhe->brcqhe', p, vb.astype(jnp.float32))
    m = jnp.swapaxes(m, 3, 4)
    l = jnp.swapaxes(l, 3, 4)
    o = o / l[..., None]

    def from_res(t):
        t = t.reshape((B, dil, n_pad) + t.shape[4:])[:, :, :n]
        t = jnp.swapaxes(t, 1, 2)
        return t.reshape((B, S) + t.shape[3:])

    return from_res(o), from_res(m), from_res(l)

def dilated_attn_sample(q, k_all, v_all, tab, window, dil):
    B, T, H, E = q.shape
    L = k_all.shape[1] - T
    kk = jnp.arange(window // dil + 1)
    idx = L + jnp.arange(T)[:, None] - kk[None, :] * dil
    valid = idx >= 0
    idx_c = jnp.maximum(idx, 0)
    kg = k_all[:, idx_c]
    vg = v_all[:, idx_c]
    s = jnp.einsum('bthe,btkhe->bthk', q, kg,
                   preferred_element_type=jnp.float32) * (HEAD_DIM ** -0.5)
    bias = tab[t5_bucket(kk * dil)].astype(jnp.float32).T
    s = jnp.where(valid[:, None, :], s + bias, -jnp.inf)
    m = jnp.max(s, axis=-1)
    p = jnp.exp(s - m[..., None])
    l = jnp.sum(p, axis=-1)
    o = jnp.einsum('bthk,btkhe->bthe', p, vg.astype(jnp.float32)) / l[..., None]
    return o, m, l

def combine_groups(outs):
    m_max = jnp.max(jnp.stack([m for _, m, _ in outs]), axis=0)
    num = 0.0
    den = 0.0
    for o, m, l in outs:
        z = l * jnp.exp(m - m_max)
        num = num + z[..., None] * o
        den = den + z
    return num / den[..., None]

def trunk_layer(x, pos, conv_prefix, h0, kv_bufs, rel_bias, norm_mix, w_in, w_conv, b_conv,
                w_rg_a, b_rg_a, w_rg_x, b_rg_x, lru_lambda, q_gain, k_gain, w_merge, b_merge,
                w_branch_lru, w_branch_att, w_o, norm_ffn, w_ffn_in, w_ffn_out):
    B, T, _ = x.shape
    xn = rmsnorm(x, norm_mix)
    lru_x, lru_g, q, k, v = jnp.split(xn @ w_in, SPLITS, axis=-1)

    if conv_prefix is None:
        conv_prefix = jnp.zeros((B, CONV_WIDTH - 1, D_RNN), lru_x.dtype)
    x_ext = jnp.concatenate([conv_prefix.astype(lru_x.dtype), lru_x], axis=1)
    new_conv = x_ext[:, -(CONV_WIDTH - 1):]
    xc = causal_conv(x_ext, w_conv, b_conv)
    hs, h_T = rg_lru(xc, pos, h0, w_rg_a, b_rg_a, w_rg_x, b_rg_x, lru_lambda)
    y_lru = (hs * jax.nn.gelu(lru_g)) @ w_branch_lru

    q = rmsnorm(q.reshape(B, T, N_ATT_HEADS, HEAD_DIM), q_gain)
    k = rmsnorm(k.reshape(B, T, N_ATT_HEADS, HEAD_DIM), k_gain)
    v = v.reshape(B, T, N_ATT_HEADS, HEAD_DIM)
    outs, new_kv = [], []
    for g, (window, dil) in enumerate(DILATED_GROUPS):
        hsl = slice(g * HEADS_PER_GROUP, (g + 1) * HEADS_PER_GROUP)
        qg, kg, vg = q[:, :, hsl], k[:, :, hsl], v[:, :, hsl]
        tab = rel_bias[:, hsl]
        if kv_bufs is None:
            outs.append(dilated_attn_prompt(qg, kg, vg, tab, window, dil))
            keep = min(window, T)
            new_kv.append(jnp.stack([kg[:, T - keep:], vg[:, T - keep:]], axis=2))
        else:
            buf = kv_bufs[g].astype(kg.dtype)
            k_all = jnp.concatenate([buf[:, :, 0], kg], axis=1)
            v_all = jnp.concatenate([buf[:, :, 1], vg], axis=1)
            outs.append(dilated_attn_sample(qg, k_all, v_all, tab, window, dil))
            new_kv.append(jnp.stack([kg, vg], axis=2))
    o = combine_groups(outs).astype(x.dtype).reshape(B, T, ATT_OUT)
    y_att = o @ w_branch_att

    g_lru, g_att = jnp.split(jax.nn.sigmoid(xn @ w_merge + b_merge), 2, axis=-1)
    x = x + (g_lru * y_lru + g_att * y_att) @ w_o

    gate, up = jnp.split(rmsnorm(x, norm_ffn) @ w_ffn_in, 2, axis=-1)
    x = x + (jax.nn.silu(gate) * up) @ w_ffn_out
    return x, new_conv, h_T, new_kv

def setup_inputs(seed: int = 0) -> dict:
    key = jax.random.key(seed)
    ks = iter(jax.random.split(key, 40))
    nrm = lambda shape, scale: jax.random.normal(next(ks), shape, jnp.float32) * scale
    inp = {}
    inp["x_prompt"] = nrm((BATCH, SEQ, D_MODEL), 1.0)
    inp["x_sample"] = nrm((DEC_BATCH, DEC_SEQ, D_MODEL), 1.0)
    for g, (window, dil) in enumerate(DILATED_GROUPS):
        L = min(window, PAST_LEN)
        inp["cache_kv_g%d" % g] = nrm((DEPTH, DEC_BATCH, L, 2, HEADS_PER_GROUP, HEAD_DIM), 1.0)
    inp["state_conv"] = nrm((DEPTH, DEC_BATCH, CONV_WIDTH - 1, D_RNN), 1.0)
    inp["state_h"] = nrm((DEPTH, DEC_BATCH, D_RNN), 0.5)
    inp["rel_bias"] = nrm((NUM_BUCKETS, N_ATT_HEADS), 0.5)
    inp["norm_mix"] = 1.0 + nrm((DEPTH, D_MODEL), 0.01)
    inp["w_in"] = nrm((DEPTH, D_MODEL, D_IN), D_MODEL ** -0.5)
    inp["w_conv"] = nrm((DEPTH, CONV_WIDTH, D_RNN), CONV_WIDTH ** -0.5)
    inp["b_conv"] = nrm((DEPTH, D_RNN), 0.01)
    inp["w_rg_a"] = nrm((DEPTH, N_LRU_BLOCKS, LRU_BLOCK, LRU_BLOCK), LRU_BLOCK ** -0.5)
    inp["b_rg_a"] = nrm((DEPTH, D_RNN), 0.01)
    inp["w_rg_x"] = nrm((DEPTH, N_LRU_BLOCKS, LRU_BLOCK, LRU_BLOCK), LRU_BLOCK ** -0.5)
    inp["b_rg_x"] = nrm((DEPTH, D_RNN), 0.01)
    a_c = jax.random.uniform(next(ks), (DEPTH, D_RNN), jnp.float32, 0.9, 0.999)
    a = a_c ** (1.0 / LRU_C)
    inp["lru_lambda"] = jnp.log(a) - jnp.log1p(-a)
    inp["q_gain"] = 1.0 + nrm((DEPTH, HEAD_DIM), 0.01)
    inp["k_gain"] = 1.0 + nrm((DEPTH, HEAD_DIM), 0.01)
    inp["w_merge"] = nrm((DEPTH, D_MODEL, 2 * D_MODEL), D_MODEL ** -0.5)
    inp["b_merge"] = nrm((DEPTH, 2 * D_MODEL), 0.01)
    inp["w_branch_lru"] = nrm((DEPTH, D_RNN, D_MODEL), D_RNN ** -0.5)
    inp["w_branch_att"] = nrm((DEPTH, ATT_OUT, D_MODEL), ATT_OUT ** -0.5)
    inp["w_o"] = nrm((DEPTH, D_MODEL, D_MODEL), D_MODEL ** -0.5)
    inp["norm_ffn"] = 1.0 + nrm((DEPTH, D_MODEL), 0.01)
    inp["w_ffn_in"] = nrm((DEPTH, D_MODEL, 2 * D_FF), D_MODEL ** -0.5)
    inp["w_ffn_out"] = nrm((DEPTH, D_FF, D_MODEL), D_FF ** -0.5)
    return inp

def reference(x_prompt, x_sample, cache_kv_g0, cache_kv_g1, cache_kv_g2, state_conv, state_h,
              rel_bias, norm_mix, w_in, w_conv, b_conv, w_rg_a, b_rg_a, w_rg_x, b_rg_x, lru_lambda,
              q_gain, k_gain, w_merge, b_merge, w_branch_lru, w_branch_att, w_o, norm_ffn,
              w_ffn_in, w_ffn_out):
    pos_p = jnp.arange(x_prompt.shape[1])
    pos_s = PAST_LEN + jnp.arange(x_sample.shape[1])

    def layer_weights(l):
        return (norm_mix[l], w_in[l], w_conv[l], b_conv[l], w_rg_a[l], b_rg_a[l], w_rg_x[l],
                b_rg_x[l], lru_lambda[l], q_gain[l], k_gain[l], w_merge[l], b_merge[l],
                w_branch_lru[l], w_branch_att[l], w_o[l], norm_ffn[l], w_ffn_in[l], w_ffn_out[l])

    yp, ys = x_prompt, x_sample
    kvp = [[], [], []]
    kvs = [[], [], []]
    conv_p, h_p, conv_s, h_s = [], [], [], []
    for l in range(DEPTH):
        lw = layer_weights(l)
        h0 = jnp.zeros((x_prompt.shape[0], D_RNN), jnp.float32)
        yp, c_p, hp_l, kv_p = trunk_layer(yp, pos_p, None, h0, None, rel_bias, *lw)
        ys, c_s, hs_l, kv_s = trunk_layer(ys, pos_s, state_conv[l], state_h[l],
                                          (cache_kv_g0[l], cache_kv_g1[l], cache_kv_g2[l]),
                                          rel_bias, *lw)
        for g in range(N_GROUPS):
            kvp[g].append(kv_p[g])
            kvs[g].append(kv_s[g])
        conv_p.append(c_p)
        h_p.append(hp_l)
        conv_s.append(c_s)
        h_s.append(hs_l)
    kv_g0_p, kv_g1_p, kv_g2_p = (jnp.stack(kvp[0]), jnp.stack(kvp[1]), jnp.stack(kvp[2]))
    kv_g0_s, kv_g1_s, kv_g2_s = (jnp.stack(kvs[0]), jnp.stack(kvs[1]), jnp.stack(kvs[2]))
    conv_p_out = jnp.stack(conv_p)
    h_p_out = jnp.stack(h_p)
    conv_s_out = jnp.stack(conv_s)
    h_s_out = jnp.stack(h_s)
    return (yp, ys, kv_g0_p, kv_g1_p, kv_g2_p, conv_p_out, h_p_out,
            kv_g0_s, kv_g1_s, kv_g2_s, conv_s_out, h_s_out)


_drawn_inputs = setup_inputs


def setup_inputs(seed=0):
    import zlib

    import numpy as np

    out = dict(_drawn_inputs(seed))
    spreads = {}
    factors = {'norm_mix': 5.857,
     'b_rg_a': 35.173,
     'b_rg_x': 32.905,
     'q_gain': 8.0,
     'k_gain': 7.896,
     'b_merge': 26.532,
     'norm_ffn': 30.788,
     'b_conv': 5.203}
    for name, (base, spread) in spreads.items():
        noise = np.random.default_rng([zlib.crc32(name.encode()), seed]).standard_normal(out[name].shape)
        drawn = base * np.exp(spread * noise) if base else spread * noise
        out[name] = __import__('jax').numpy.asarray(drawn.astype(out[name].dtype))
    for name, factor in factors.items():
        out[name] = (out[name] * factor).astype(out[name].dtype)
    return out
```

```python
import math
from contextlib import ExitStack

import numpy as np

import concourse.bass as bass
from concourse import mybir

F32 = mybir.dt.float32
F32R = mybir.dt.float32r
ALU = mybir.AluOpType
ACT = mybir.ActivationFunctionType
AX_X = mybir.AxisListType.X
ds = bass.ds

P = 128
D = 1024
SEQ = 1024
NB = 8
NT = SEQ + NB
NCH = 3
CH = NT // NCH
KT = D // P
HD = 64
HG = 8
NG = 3
DIL = (1, 4, 16)
NKEY = (128, 128, 64)
ATT = NG * HG * HD
DFF = 2816
FT = DFF // P
PARTS = ((0, 8), (8, 8), (16, 6))
EPS = 1e-6
NEG = -1e30
SCALE = HD ** -0.5
NBK = 32
UL = 384


def bucket_lines():
    out = np.zeros((NG, NBK + 1, UL), np.float32)
    out[:, NBK] = NEG
    for g in range(NG):
        skip = 2 if g == 2 else 1
        at = np.arange(127, 256, skip)
        dist = np.arange(len(at)) * DIL[g]
        d_f = np.maximum(dist, 1).astype(np.float32)
        large = 16 + (np.log(d_f / np.float32(16)) / np.float32(math.log(2048 / 16)) * np.float32(16)).astype(np.int32)
        bucket = np.where(dist < 16, dist, np.minimum(large, NBK - 1))
        out[g, NBK, at] = 0.0
        out[g, bucket, at] = 1.0
    return out


class Chain:

    def __init__(self, eng, sem):
        self.eng, self.sem, self.base, self.n, self.i, self.per = eng, sem, 0, 0, 0, 0

    def loop(self, i, per):
        self.base += self.n
        self.i, self.per, self.n = i, per, 0

    def end(self, iterations):
        assert self.n == self.per, (self.n, self.per)
        self.base += self.per * iterations
        self.i = self.per = self.n = 0

    def step(self, ins):
        self.n += 1
        ins.then_inc(self.sem, 1)
        self.eng.wait_ge(self.sem, self.i * self.per + (self.base + self.n) if self.per else self.base + self.n)


def build(nc, A, O):
    with ExitStack() as ctx:
        def sb(name, shape, dt=F32):
            return ctx.enter_context(nc.sbuf_tensor(name, shape, dt))

        def sem(name):
            return ctx.enter_context(nc.semaphore(name))

        def dram(name, shape):
            return nc.dram_tensor(name, shape, F32, kind="Internal").ap()

        big1 = sb("big1", [P, 2, KT, NT], F32R)
        big2 = sb("big2", [P, 2, KT, NT], F32R)
        x1 = sb("x1", [P, KT, NT])
        wraw = sb("wraw", [P, 2, KT, P])
        wsp = sb("wsp", [P, 2, 2, KT, P], F32R)
        ext = sb("ext", [P, 4, NT + 3])
        ident = sb("ident", [P, P])
        hsel = sb("hsel", [P, 2])
        ones = sb("ones", [P, 1])
        esel = sb("esel", [P, 2 * NB - 1])
        par = sb("par", [P, KT, 8])
        cdec = sb("cdec", [P, 2, KT])
        lamt = sb("lamt", [P, 4, KT])
        gmix = sb("gmix", [P, KT])
        gffn = sb("gffn", [P, KT])
        bones = sb("bones", [P, P])
        rsd = sb("rsd", [P, 3, 9])
        gq2 = sb("gq2", [P, 2])
        relx = sb("relx", [NBK + 1, NG * HG])
        gqk = sb("gqk", [P, 12])
        bmrg = sb("bmrg", [P, 16])
        bd = sb("bd", [P, 2, P])
        sqkv = sb("sqkv", [P, 36, NB])
        stc = sb("stc", [P, KT, 4 * NB])
        sout = sb("sout", [P, KT, 20])
        st = sb("st", [P, 2, 32])
        epst = sb("epst", [P, 1])
        u_lines = ext[0:HG, 0:2, :].rearrange("p a n -> p (a n)")[:, 0:NG * UL].rearrange("p (g n) -> p g n", g=NG)

        def tmp(n):
            return x1[:, n, :]

        ups = ctx.enter_context(nc.psum_tensor("ups", [P, 2, NCH, 512], F32))
        aux = ctx.enter_context(nc.psum_tensor("aux", [P, 2, 512], F32))

        qkv_s = O["qkv"]
        gate_s = dram("gate_s", [24, P, NT])
        o_s = dram("o_s", [NG, SEQ, HG, HD + 2])
        u_s = dram("u_s", [NG * HG, UL])
        bt_s = dram("bt_s", [NG * HG, P, 2 * P])

        stream = [
            ("lru", 8, KT, A["w_in"], 0, 8, 1, 0),
            ("qk", 12, KT, A["w_in"], 16, 17, 2, 0),
            ("v", 6, KT, A["w_in"], 40, 41, 2, 0),
            ("att0", 4, KT, A["w_merge"], 0, 1, 2, 0),
            ("att1", 4, KT, A["w_merge"], 8, 9, 2, 0),
            ("att2", 4, KT, A["w_branch_lru"], 0, 1, 2, 0),
            ("merge", 4, 4, A["w_branch_att"], 0, 1, 2, 0),
            ("wo", 4, KT, A["w_o"], 0, 1, 2, 0),
        ]
        for n, (f0, nf) in enumerate(PARTS):
            stream.append((f"up{n}", nf, KT, A["w_ffn_in"], f0, FT + f0, 1, 0))
            stream.append((f"down{n}", 4, nf, A["w_ffn_out"], 0, 1, 2, f0))
        T0, t = {}, 0
        for s in stream:
            T0[s[0]] = t
            t += s[1]

        def two(name):
            return [sem(f"{name}{j}") for j in range(2)]

        w_loaded, w_split, unit_done, ps_free = two("w_loaded"), two("w_split"), two("unit_done"), two("ps_free")
        w_hi, ticks = sem("w_hi"), sem("ticks")
        s_dve, s_act, s_pool = sem("s_dve"), sem("s_act"), sem("s_pool")
        const_ld = sem("const_ld")
        bd_zero = sem("bd_zero")
        x_loaded = [sem(f"x_loaded{k}") for k in range(KT)]
        nsq_done, nst_mm, nst_done, nrt_done, nex_done, nbc_done, nrb_done = (
            sem(n) for n in ("nsq_done", "nst_mm", "nst_done", "nrt_done", "nex_done", "nbc_done", "nrb_done"))
        nf_done, nhi_done, nlo_done = sem("nf_done"), sem("nhi_done"), sem("nlo_done")
        u_ps, u_sb, u_stored = sem("u_ps"), sem("u_sb"), sem("u_stored")
        lam_act, lam_dve = sem("lam_act"), sem("lam_dve")

        bd_loaded, xc0_done, xc_done = sem("bd_loaded"), sem("xc0_done"), sem("xc_done")
        conv_done, u_done, z_done = sem("conv_done"), sem("u_done"), sem("z_done")
        gate_mm, gate_ev, ath_done, m2_done, sqrt_done = sem("gate_mm"), sem("gate_ev"), sem("ath_done"), sem("m2_done"), sem("sqrt_done")
        out_done = sem("out_done")
        qsq_done, st_done, sd_done, ex_done, bc_done, qn_done = two("qsq_done"), two("st_done"), two("sd_done"), two("ex_done"), two("bc_done"), two("qn_done")
        qn_stored = two("qn_stored")
        sqc_done = sem("sqc_done")
        v_stored = two("v_stored")

        bt_fill = sem("bt_fill")
        sm_ld, sm_dve, sm_pe, sm_act, sm_max, sm_v = sem("sm_ld"), sem("sm_dve"), sem("sm_pe"), sem("sm_act"), sem("sm_max"), two("sm_v")
        qkv_ld, att_free, au_ev, g_stored, o_stored = sem("qkv_ld"), sem("att_free"), sem("au_ev"), two("g_stored"), sem("o_stored")
        vt_mm, vt_ev, s_mm, sa_done, nm_done, exp_done, pt_mm, pt_ev, pv_mm, o_ev = (
            sem(n) for n in ("vt_mm", "vt_ev", "s_mm", "sa_done", "nm_done", "exp_done", "pt_mm", "pt_ev", "pv_mm", "o_ev"))
        ol_ld, cb_free, dm_done, ce_done, on_done, ot_mm, ot_done = (
            two("ol_ld"), two("cb_free"), sem("dm_done"), sem("ce_done"), sem("on_done"), sem("ot_mm"), sem("ot_done"))
        side_ld, mrg_sum, mrg_hi, mrg_done = two("side_ld"), two("mrg_sum"), two("mrg_hi"), two("mrg_done")
        xr_ld, xr_free, wo_done = two("xr_ld"), two("xr_free"), sem("wo_done")
        sg_free, h_done, y_stored = sem("sg_free"), sem("h_done"), sem("y_stored")

        kc = [x1[:, 0:4, :], x1[:, 4:8, :], ext[:, 0:2, :]]
        kc = [t.rearrange("p a n -> p (a n)")[:, 0:NB * 4 * n].rearrange("p (b f n) -> p b f n", b=NB, f=4) for t, n in zip(kc, NKEY)]
        vc = [x1[:, 0:4, :], x1[:, 4:8, :], x1[0:64, 0:4, :]]
        vc = [t.rearrange("p a n -> p (a n)")[:, 0:NB * 512].rearrange("p (b f) -> p b f", b=NB) for t in vc]
        small = ext[:, 2:4, :].rearrange("p a n -> p (a n)")
        ROWS = NB * HG

        def part(a, n, p=P):
            return small[0:p, a:a + n]

        qm, pm, sqs, rms = (part(192 * n, 192) for n in range(4))
        srow, sbias = part(768, 323, ROWS), part(1091, 387, ROWS)
        pts, hm, dsel = part(1478, 192), part(1670, P, ROWS), part(1798, 32, ROWS)
        r3, rsel, ul8 = part(1830, 96, ROWS), part(1926, ROWS, HG), part(768, 387, HG)
        osum = part(1990, 32)
        sstat = st[0:ROWS, 0, 0:4]
        osam = stc[:, 0:4, 0:NB]

        QT, KTT, VT = tmp(0)[:, 0:SEQ], tmp(1)[:, 0:SEQ], tmp(2)[:, 0:SEQ]
        SB = [tmp(3)[:, 512 * n:512 * n + 512] for n in range(2)]
        PTS = [tmp(4)[:, 512 * n:512 * n + 512] for n in range(2)]
        OT = x1[:, 5:7, :].rearrange("p a n -> p (a n)")[:, 0:16 * (HD + 2)].rearrange("p (b h e) -> p b h e", b=8, h=2)
        VTOK = ext[:, 1:3, :].rearrange("p a n -> p (a n)")[:, 0:16 * (HD + 1)].rearrange("p (b h e) -> p b h e", b=8, h=2)
        BT = ext[:, 0, 0:512].rearrange("p (h n) -> p h n", h=2)
        NM = ext[:, 0, 512:516]
        GT = [tmp(7), ext[:, 3, 0:NT]]
        s_bank = [ups[:, 1, 0, :], ups[:, 1, 1, :]]
        pt_bank = [ups[:, 1, 2, :], aux[:, 0, :]]
        o_bank = aux[:, 1, :]

        def toks(ap, g, b, n=1):
            if g == 0:
                return ap[:, (b + 1 - n) * P:(b + 1) * P]
            if g == 1:
                return ap.rearrange("p (m d) -> p d m", d=4)[:, b // 2, (b % 2 + 1 - n) * P:(b % 2 + 1) * P]
            return ap.rearrange("p (m d) -> p d m", d=8)[:, b]

        def nkeys(g, b):
            return (2 if b else 1, 1 + b % 2, 1)[g]

        OL = [x1[:, 2 * n:2 * n + 2, :].rearrange("p a n -> p (a n)")[:, 0:NG * HG * (HD + 2)]
              .rearrange("p (g h e) -> p g h e", g=NG, h=HG) for n in range(2)]
        mt = tmp(4)[:, 0:8]
        ce, cl, cc = (tmp(4)[:, 32 * n:32 * n + 24].rearrange("p (g h) -> p g h", g=NG) for n in range(1, 4))
        den = tmp(4)[:, 128:136]
        oacc, oprod = (tmp(5 + n)[:, 0:512].rearrange("p (h e) -> p h e", h=HG) for n in range(2))

        ups_v = [ups[:, j, :, 0:CH] for j in range(2)]

        def apart(eng):
            eng.sem_inc(ticks, 1)

        def chunks(ap):
            return ap.rearrange("p (c n) -> p c n", c=NCH)

        consts = [
            (ident[:], A["c_ident"]), (hsel[:], A["c_hsel"]), (relx[0:NBK, :], A["rel_bias"]),
            (relx[NBK:NBK + 1, :], A["c_one"]),
            (ext[0:NBK + 1, 2:4, :].rearrange("p a n -> p (a n)")[:, 0:NG * UL].rearrange("p (g n) -> p g n", g=NG),
             A["c_lines"].rearrange("g b n -> b g n")),
            (stc[:], A["c_state"]), (bones[:], A["c_bones"]),
            (gmix[:], A["c_norm_mix"]), (gffn[:], A["c_norm_ffn"]), (bmrg[:], A["c_b_merge"]),
            (par[:], A["c_par"]), (gq2[:], A["c_gains"]),
        ]
        CONSTS = 16 * len(consts)
        sm_loads = [(kc[g], A[f"kc{g}"]) for g in range(NG)]
        sm_loads += [(hm, A["c_hm"]), (dsel, A["c_dsel"]), (rsel, A["c_rsel"]),
                     (ul8.rearrange("h (g n) -> h g n", g=NG), u_s.rearrange("(g h) n -> h g n", g=NG)[:, :, 127:256])]
        SM_LD = 16 * len(sm_loads)
        O_STORES = 16 * (1 + 4 + 8 + 4)
        block = ctx.enter_context(nc.Block())

        @block.sync
        def _(sp):
            for k in range(KT):
                sp.dma_start(tmp(k), A["x_T"][k]).then_inc(x_loaded[k], 16)
            for name, iters, nk, src, f0, f1, step, k0 in stream:
                if name == "att0":
                    for j in range(2):
                        sp.wait_ge(qn_stored[j], 16 * 13)
                        sp.wait_ge(v_stored[j], 16 * 7)
                    sp.wait_ge(bt_fill, 16)
                if name == "merge":
                    for n in range(8):
                        if n >= 2:
                            sp.wait_ge(cb_free[n % 2], n // 2)
                        else:
                            sp.wait_ge(o_stored, O_STORES)
                        sp.dma_start(OL[n % 2], o_s[:, n * P:(n + 1) * P].rearrange("g t h e -> t g h e")).then_inc(ol_ld[n % 2], 16)
                    for j in range(2):
                        sp.wait_ge(g_stored[j], 16 * 13)
                with sp.Fori(0, iters) as i:
                    for slot, f in ((0, f0), (1, f1)):
                        sp.wait_ge(w_split[slot], i + (T0[name] + 1))
                        sp.dma_start(wraw[:, slot, 0:nk, :],
                                     src[ds(i * step + f, 1), :, k0:k0 + nk, :].rearrange("a p k n -> p (a k) n")).then_inc(w_loaded[slot], 16)
                    if name.startswith("att"):
                        g = int(name[3])
                        sp.wait_ge(att_free, i + (4 * g + 1))
                        for n, t in enumerate((QT, KTT, VT)):
                            sp.dma_start(t, qkv_s[ds(i + (12 * n + 4 * g), 1)].rearrange("a p t -> p (a t)")).then_inc(qkv_ld, 16)
                        sp.dma_start(BT, bt_s[ds(i * 2 + 8 * g, 2)].rearrange("h p n -> p h n")).then_inc(qkv_ld, 16)
                    if name == "merge":
                        for j in range(2):
                            sp.wait_ge(mrg_done[j], i + 1)
                            for n in range(3):
                                sp.dma_start(tmp(3 * j + n), gate_s[ds(i * 2 + (8 * n + j), 1)].rearrange("a p t -> p (a t)"))\
                                    .then_inc(side_ld[j], 16)
                    if name == "wo":
                        for j in range(2):
                            sp.wait_ge(xr_free[j], i + 1)
                            sp.dma_start(ext[:, 3 * j, 0:NT], A["x_T"][ds(i * 2 + j, 1)].rearrange("a p t -> p (a t)")).then_inc(xr_ld[j], 16)

        @block.gpsimd
        def _(pool):
            nc.gpsimd.memset(bd[:], 0.0).then_inc(bd_zero, 1)
            for j in range(2):
                pool.sem_inc(w_split[j], 1)

            def norm_low(r):
                for k in range(KT):
                    pool.wait_ge(nhi_done, KT * r + k + 1)
                    nc.gpsimd.tensor_tensor(big1[:, 1, k, :], ext[:, 1 + k % 2, 0:NT], big1[:, 0, k, :].bitcast(F32),
                                            ALU.subtract).then_inc(nlo_done, 1)

            norm_low(0)
            for name, iters, nk, *_ in stream:
                if name == "up0":
                    norm_low(1)
                with pool.Fori(0, iters) as i:
                    for slot in range(2):
                        pool.wait_ge(w_loaded[slot], i * 16 + 16 * (T0[name] + 1))
                        pool.wait_ge(unit_done[slot], i + (T0[name] + 1))
                        apart(pool)
                        raw, hi, lo = wraw[:, slot, 0:nk, :], wsp[:, slot, 0, 0:nk, :], wsp[:, slot, 1, 0:nk, :]
                        nc.gpsimd.tensor_copy(hi, raw).then_inc(w_hi, 1)
                        pool.wait_ge(w_hi, i * 2 + (2 * T0[name] + slot + 1))
                        nc.gpsimd.tensor_tensor(lo, raw, hi.bitcast(F32), ALU.subtract).then_inc(w_split[slot], 1)

        @block.tensor
        def _(pe):
            def unit(name, i, slot, src, nk=KT, parts=(0, 1, 2)):
                if 0 in parts:
                    pe.wait_ge(w_split[slot], i + (T0[name] + 2))
                    pe.wait_ge(ps_free[slot], i + (T0[name] + 1 - (12 if T0[name] >= T0["merge"] else 0)))
                for c in parts:
                    for k in range(nk):
                        for w, a in ((0, 0), (0, 1), (1, 0)):
                            ins = nc.tensor.matmul(ups[:, slot, c, 0:CH], wsp[:, slot, w, k, :], src[:, a, k, c * CH:(c + 1) * CH],
                                                   start=(k == 0 and w + a == 0), stop=(k == nk - 1 and w == 1))
                if NCH - 1 in parts:
                    ins.then_inc(unit_done[slot], 1)

            for j in range(2):
                pe.sem_inc(unit_done[j], 1)
            pe.wait_ge(const_ld, CONSTS)
            for g in range(NG):
                lines = ext[0:NBK + 1, 2:4, :].rearrange("p a n -> p (a n)")[:, g * UL:(g + 1) * UL]
                ins = nc.tensor.matmul(ups[0:HG, 0, g, 0:UL], relx[:, g * HG:(g + 1) * HG], lines, start=True, stop=True)
            ins.then_inc(u_ps, 1)
            pe.wait_ge(u_sb, 1)
            def norm_sums(r):
                for k in range(KT):
                    pe.wait_ge(nsq_done, KT * r + k + 1)
                    for b in range(9):
                        w = P if b < 8 else NB
                        ins = nc.tensor.matmul(aux[0:w, 0, b:b + 1], ext[:, 1 + k % 2, b * P:b * P + w], ones[:],
                                               start=(k == 0 and b == 0), stop=(k == KT - 1), skip_group_check=True)
                    ins.then_inc(nst_mm, 1)

            def norm_spread(r):
                pe.wait_ge(nex_done, r + 1)
                for b in range(9):
                    w = P if b < 8 else NB
                    src = ext[0:w, 3, b * P:(b + 1) * P] if b < 8 else ext[0:w, 0, 0:P]
                    ins = nc.tensor.transpose(ups[:, 0, b // 4, (b % 4) * P:(b % 4) * P + w], src, ident[0:w, 0:w])
                ins.then_inc(nbc_done, 1)

            norm_sums(0)
            norm_spread(0)
            pe.wait_ge(nlo_done, KT)

            pe.sem_inc(gate_mm, 1)
            with pe.Fori(0, KT) as i:
                unit("lru", i, 0, big1)
                unit("lru", i, 1, big1)
                pe.wait_ge(bd_loaded, i * 64 + 64)
                pe.wait_ge(xc_done, i + 1)
                for c in range(NCH):
                    pe.wait_ge(gate_ev, i * NCH + (c + 1))
                    for a in range(2):
                        ins = nc.tensor.matmul(aux[:, a, 0:CH], bd[:, a, :], tmp(0)[:, c * CH:(c + 1) * CH], start=True, stop=True)
                    ins.then_inc(gate_mm, 1)
            pe.wait_ge(gate_ev, KT * NCH + 1)
            def stats(j, i):
                pe.wait_ge(qsq_done[j], i + 1)
                for b in range(8):
                    ins = nc.tensor.matmul(aux[:, 1, 2 * b:2 * b + 2], tmp(2 + j)[:, b * P:(b + 1) * P], hsel[:], start=True, stop=True)
                ins.then_inc(st_done[j], 1)

            def spread(j, i):
                pe.wait_ge(ex_done[j], i + 1)
                for b in range(8):
                    ins = nc.tensor.transpose(aux[:, b // 4, (b % 4) * P:(b % 4 + 1) * P], tmp(4 + j)[:, b * P:(b + 1) * P], ident[:])
                ins.then_inc(bc_done[j], 1)

            def qk(i, first):
                unit("qk", i, 0, big1, parts=(0,))
                if not first:
                    stats(1, i - 1)
                unit("qk", i, 0, big1, parts=(1, 2))
                if not first:
                    spread(1, i - 1)
                unit("qk", i, 1, big1, parts=(0,))
                if not first:
                    pe.wait_ge(qn_done[1], i + 1)
                stats(0, i)
                unit("qk", i, 1, big1, parts=(1, 2))
                spread(0, i)
                pe.wait_ge(qn_done[0], i + 2)

            qk(0, True)
            with pe.Fori(1, 12) as i:
                qk(i, False)
            stats(1, 11)
            spread(1, 11)
            with pe.Fori(0, 6) as i:
                unit("v", i, 0, big1)
                unit("v", i, 1, big1)

            pe.wait_ge(sm_dve, 1)
            nc.tensor.matmul(aux[:, 0, 0:192], bones[:], sqs, start=True, stop=True).then_inc(sm_pe, 1)
            pe.wait_ge(sm_ld, SM_LD)
            nc.tensor.matmul(aux[0:ROWS, 1, 8:395], rsel, ul8, start=True, stop=True).then_inc(sm_pe, 1)
            pe.wait_ge(sm_dve, 2)
            for g in range(NG):
                nc.tensor.matmul(aux[0:ROWS, 1, g:g + 1], pm[:, 64 * g:64 * g + 64], ones[:], start=True, stop=True)
                for f in range(4):
                    for b in range(NB):
                        at = 64 * g + 16 * f + 2 * b
                        ins = nc.tensor.matmul(aux[0:NKEY[g], 0, at:at + 2], kc[g][:, b, f, :], qm[:, at:at + 2], start=True, stop=True)
            ins.then_inc(sm_pe, 1)
            pe.wait_ge(sm_dve, 3)
            for g in range(NG):
                ins = nc.tensor.transpose(ups[0:ROWS, 0, 0, g * P:g * P + NKEY[g]], sqs[0:NKEY[g], 64 * g:64 * g + 64],
                                          ident[0:NKEY[g], 0:NKEY[g]])
            ins.then_inc(sm_pe, 1)
            pe.wait_ge(sm_dve, 4)
            for g in range(NG):
                nc.tensor.transpose(aux[0:NKEY[g], 0, 64 * g:64 * g + 64], srow[:, g * P:g * P + NKEY[g]], ident[0:ROWS, 0:ROWS])
            nc.tensor.matmul(aux[:, 1, 0:96], hm, r3, start=True, stop=True).then_inc(sm_pe, 1)
            pe.wait_ge(sm_dve, 5)
            for g in range(NG):
                pe.wait_ge(sm_v[g % 2], 16 * (g // 2 + 1))
                for f in range(4):
                    for b in range(NB):
                        at = 16 * f + 2 * b
                        ins = nc.tensor.matmul(ups[:, 1, 0, at:at + 2], vc[g][0:NKEY[g], b, f * P:(f + 1) * P],
                                               pts[0:NKEY[g], 64 * g + at:64 * g + at + 2],
                                               start=(g + f + b == 0), stop=(g == NG - 1), skip_group_check=True)
                ins.then_inc(sm_pe, 1)
            pe.wait_ge(sm_dve, 6)

            for g in range(NG):
                src = big2 if g == 2 else big1
                if g == 2:
                    pe.wait_ge(z_done, KT + 1)
                with pe.Fori(0, 4) as i:
                    def pieces(a, b):
                        for n in range(a, b):
                            slot, c, k = n // 24, n // 8 % 3, n % 8
                            if n % 24 == 0:
                                pe.wait_ge(w_split[slot], i + (T0[f"att{g}"] + 2))
                                pe.wait_ge(au_ev, i * 2 + (8 * g + slot + 1))
                            for w, a2 in ((0, 0), (0, 1), (1, 0)):
                                ins = nc.tensor.matmul(ups[:, 0, c, 0:CH], wsp[:, slot, w, k, :], src[:, a2, k, c * CH:(c + 1) * CH],
                                                       start=(k == 0 and w + a2 == 0), stop=(k == KT - 1 and w == 1))
                            if n % 24 == 23:
                                ins.then_inc(unit_done[slot], 1)

                    pieces(0, 8)
                    pe.wait_ge(qkv_ld, i * 64 + 64 * (4 * g + 1))
                    pe.wait_ge(pt_ev, i * 8 + (32 * g + 2))
                    for b in range(8):
                        ins = nc.tensor.transpose(pt_bank[b // 4][:, (b % 4) * P:(b % 4 + 1) * P], toks(VT, g, b), ident[:])
                    ins.then_inc(vt_mm, 1)
                    for n in range(10):
                        if n < 8:
                            hh, bp = n // 4, n % 4
                            hr = slice(hh * HD, (hh + 1) * HD)
                            pe.wait_ge(sa_done, i * 8 + (32 * g + n + 1))
                            for m in range(2):
                                b = 2 * bp + m
                                nk = nkeys(g, b)
                                ins = nc.tensor.matmul(s_bank[n % 2][:, 256 * m + 256 - P * nk:256 * m + 256], toks(QT, g, b)[hr],
                                                       toks(KTT, g, b, nk)[hr], start=True, stop=True)
                            ins.then_inc(s_mm, 1)
                        if 1 <= n <= 8:
                            q = n - 1
                            pe.wait_ge(exp_done, i * 8 + (32 * g + q + 1))
                            pe.wait_ge(pt_ev, i * 8 + (32 * g + q + 1))
                            if q == 0:
                                pe.wait_ge(vt_ev, i + (4 * g + 1))
                            for m in range(2):
                                for c in range(256 * m + 256 - P * nkeys(g, 2 * (q % 4) + m), 256 * m + 256, P):
                                    ins = nc.tensor.transpose(pt_bank[q % 2][:, c:c + P], SB[q % 2][:, c:c + P], ident[:])
                            ins.then_inc(pt_mm, 1)
                        if n >= 2:
                            q = n - 2
                            hh, bp = q // 4, q % 4
                            pe.wait_ge(pt_ev, i * 8 + (32 * g + q + 3))
                            pe.wait_ge(o_ev, i * 8 + (32 * g + q + 1))
                            for m in range(2):
                                b = 2 * bp + m
                                nk = nkeys(g, b)
                                for k in range(nk):
                                    c = 256 * m + 256 - P * (nk - k)
                                    ins = nc.tensor.matmul(o_bank[:, m * (HD + 1):(m + 1) * (HD + 1)], PTS[q % 2][:, c:c + P],
                                                           VTOK[:, b + 1 - nk + k, hh, :], start=(k == 0), stop=(k == nk - 1))
                            ins.then_inc(pv_mm, 1)
                        pieces(8 + 4 * n, 12 + 4 * n)

            for n in range(8):
                pe.wait_ge(on_done, n + 1)
                if n:
                    pe.wait_ge(ot_done, n)
                for k in range(4):
                    ins = nc.tensor.transpose(aux[:, 0, k * P:(k + 1) * P], tmp(5)[:, k * P:(k + 1) * P], ident[:])
                ins.then_inc(ot_mm, 1)
            pe.wait_ge(ot_done, 9)
            pe.wait_ge(au_ev, 25)
            with pe.Fori(0, 4) as i:
                unit("merge", i, 0, big2, nk=4)
                unit("merge", i, 1, big2, nk=4)
            for j in range(2):
                pe.wait_ge(mrg_done[j], 5)
            with pe.Fori(0, 4) as i:
                unit("wo", i, 0, big1)
                unit("wo", i, 1, big1)
            norm_sums(1)
            norm_spread(1)
            pe.wait_ge(nlo_done, 2 * KT)
            for n, (f0, nf) in enumerate(PARTS):
                with pe.Fori(0, nf) as i:
                    unit(f"up{n}", i, 0, big1)
                    unit(f"up{n}", i, 1, big1)
                pe.wait_ge(h_done, f0 + nf)
                with pe.Fori(0, 4) as i:
                    unit(f"down{n}", i, 0, big2, nk=nf)
                    unit(f"down{n}", i, 1, big2, nk=nf)


        @block.scalar
        def _(act):
            step = Chain(act, s_act)
            for dst, src in consts:
                act.dma_start(dst, src).then_inc(const_ld, 16)
            act.wait_ge(u_sb, 1)
            act.dma_start(u_s.rearrange("(g h) n -> h g n", g=NG), u_lines).then_inc(u_stored, 16)
            act.wait_ge(u_stored, 16)

            def norm(r):
                for k in range(KT):
                    act.wait_ge(x_loaded[k], 16) if r == 0 else act.wait_ge(wo_done, k + 1)
                    if k >= 2:
                        act.wait_ge(nst_mm, KT * r + k - 1)
                    nc.scalar.activation(ext[:, 1 + k % 2, 0:NT], tmp(k), ACT.Square).then_inc(nsq_done, 1)
                act.wait_ge(nst_mm, KT * (r + 1))
                for w, c in ((P, slice(0, 8)), (NB, slice(8, 9))):
                    ins = nc.scalar.activation(rsd[0:w, 1, c], aux[0:w, 0, c], ACT.Sqrt, scale=1.0 / D, bias=epst[0:w, :])
                ins.then_inc(nrt_done, 1)
                act.wait_ge(nbc_done, r + 1)
                nc.scalar.activation(ext[:, 0, 0:SEQ], ups[:, 0, 0:2, :].rearrange("p b n -> p (b n)"), ACT.Copy)
                nc.scalar.activation(ext[:, 0, SEQ:NT], ups[:, 0, 2, 0:NB], ACT.Copy).then_inc(nrb_done, 1)
                for k in range(KT):
                    act.wait_ge(nf_done, KT * r + k + 1)
                    nc.scalar.activation(big1[:, 0, k, :], ext[:, 1 + k % 2, 0:NT], ACT.Copy).then_inc(nhi_done, 1)

            norm(0)
            act.dma_start(bt_s, bass.AP(tensor=u_s.tensor, offset=0, ap=[[UL, NG * HG], [1, P], [1, 2 * P]])).then_inc(bt_fill, 16)
            act.wait_ge(lam_dve, 1)
            nc.scalar.activation(lamt[:, 1, :], lamt[:, 0, :], ACT.Exp, scale=-1.0).then_inc(lam_act, 1)
            act.wait_ge(lam_dve, 2)
            nc.scalar.activation(lamt[:, 3, :], lamt[:, 2, :], ACT.Ln).then_inc(lam_act, 1)

            act.wait_ge(nlo_done, KT)
            act.sem_inc(gate_ev, 1)
            XC, GE, R, I, AD, M2, U, H = (tmp(n) for n in range(8))
            LX = ext[:, 0, :]
            with act.Fori(0, KT) as i:
                act.wait_ge(gate_mm, i * NCH + 1)
                for a, wn in enumerate(("w_rg_a", "w_rg_x")):
                    src = A[wn][0].rearrange("n i j -> (n i) j")
                    for h in range(2):
                        act.dma_start(bd[h * HD:(h + 1) * HD, a, h * HD:(h + 1) * HD],
                                      src[ds(i * P + h * HD, HD), :]).then_inc(bd_loaded, 16)
                act.wait_ge(unit_done[0], i + (T0["lru"] + 2))
                act.wait_ge(conv_done, i + 1)
                nc.scalar.activation(chunks(LX[:, 3:3 + NT]), ups_v[0], ACT.Copy).then_inc(ps_free[0], 1)
                act.wait_ge(ps_free[0], i + (T0["lru"] + 2))
                act.wait_ge(u_done, i + 1)
                apart(act)
                nc.scalar.activation(XC[:, 0:SEQ], LX[:, 0:SEQ], ACT.Identity, bias=par[:, ds(i, 1), 4], scale=par[:, ds(i, 1), 0])
                nc.scalar.activation(XC[:, SEQ:NT], LX[:, SEQ + 3:NT + 3], ACT.Identity, bias=par[:, ds(i, 1), 4],
                                     scale=par[:, ds(i, 1), 3]).then_inc(xc0_done, 1)
                act.wait_ge(unit_done[1], i + (T0["lru"] + 2))
                act.wait_ge(z_done, i + 1)
                nc.scalar.activation(chunks(GE), ups_v[1], ACT.Gelu_apprx_tanh).then_inc(ps_free[1], 1)
                for c in range(NCH):
                    act.wait_ge(gate_mm, i * NCH + (c + 2))
                    apart(act)
                    nc.scalar.activation(R[:, c * CH:(c + 1) * CH], aux[:, 0, 0:CH], ACT.Sigmoid, bias=par[:, ds(i, 1), 5])
                    nc.scalar.activation(I[:, c * CH:(c + 1) * CH], aux[:, 1, 0:CH], ACT.Sigmoid, bias=par[:, ds(i, 1), 6]).then_inc(gate_ev, 1)
                act.wait_ge(gate_ev, i * NCH + (NCH + 1))
                step.loop(i, 1)
                apart(act)
                step.step(nc.scalar.activation(AD, R, ACT.Exp, scale=cdec[:, 0, ds(i, 1)]))
                apart(act)
                nc.scalar.activation(R, R, ACT.Tanh, scale=cdec[:, 1, ds(i, 1)]).then_inc(ath_done, 1)
                act.wait_ge(m2_done, i + 1)
                nc.scalar.activation(M2, M2, ACT.Sqrt).then_inc(sqrt_done, 1)
            step.end(KT)
            act.wait_ge(z_done, KT + 1)
            act.dma_start(O["lru_out"], sout[:]).then_inc(out_done, 16)
            act.dma_start(O["state_out"], stc[:]).then_inc(out_done, 16)
            for j in range(2):
                act.sem_inc(qn_stored[j], 16)
                act.sem_inc(v_stored[j], 16)

            def evac(i, j):
                act.wait_ge(unit_done[j], i + (T0["qk"] + 2))
                act.wait_ge(qn_done[j], i + 1)
                nc.scalar.activation(chunks(tmp(j)), ups_v[j], ACT.Copy).then_inc(ps_free[j], 1)
                act.wait_ge(ps_free[j], i + (T0["qk"] + 2))
                nc.scalar.activation(tmp(2 + j)[:, 0:SEQ], tmp(j)[:, 0:SEQ], ACT.Square).then_inc(qsq_done[j], 1)
                nc.scalar.activation(sqkv[:, ds(i * 2 + j, 1), :], tmp(j)[:, SEQ:NT], ACT.Copy).then_inc(sqc_done, 1)

            def store(i, j):
                act.wait_ge(qn_done[j], i + 2)
                act.dma_start(qkv_s[ds(i * 2 + j, 1), :, :].rearrange("a p t -> p a t"), tmp(6 + j)[:, 0:SEQ]).then_inc(qn_stored[j], 16)

            def root(i, j):
                act.wait_ge(st_done[j], i + 1)
                nc.scalar.activation(st[:, j, 0:16], aux[:, 1, 0:16], ACT.Sqrt, scale=1.0 / HD, bias=epst[:]).then_inc(sd_done[j], 1)

            def qk(i, first):
                evac(i, 0)
                if not first:
                    store(i - 1, 1)
                root(i, 0)
                evac(i, 1)
                store(i, 0)
                root(i, 1)

            qk(0, True)
            with act.Fori(1, 12) as i:
                qk(i, False)
            store(11, 1)
            with act.Fori(0, 6) as i:
                for j in range(2):
                    act.wait_ge(unit_done[j], i + (T0["v"] + 2))
                    act.wait_ge(v_stored[j], i * 16 + 16)
                    nc.scalar.activation(chunks(tmp(j)), ups_v[j], ACT.Copy).then_inc(ps_free[j], 1)
                    act.wait_ge(ps_free[j], i + (T0["v"] + 2))
                    nc.scalar.activation(sqkv[:, ds(i * 2 + (24 + j), 1), :], tmp(j)[:, SEQ:NT], ACT.Copy).then_inc(sqc_done, 1)
                    act.dma_start(qkv_s[ds(i * 2 + (24 + j), 1), :, :].rearrange("a p t -> p a t"), tmp(j)[:, 0:SEQ]).then_inc(v_stored[j], 16)
            for j in range(2):
                act.wait_ge(v_stored[j], 16 * 7)
                act.wait_ge(qn_stored[j], 16 * 13)
            act.wait_ge(sqc_done, 36)
            for dst, src in sm_loads:
                act.dma_start(dst, src).then_inc(sm_ld, 16)
            act.wait_ge(sm_pe, 1)
            nc.scalar.activation(rms, aux[:, 0, 0:192], ACT.Sqrt, scale=1.0 / HD, bias=epst[:]).then_inc(sm_act, 1)
            act.wait_ge(sm_dve, 2)
            act.dma_start(O["sqkv"], sqkv[:]).then_inc(out_done, 16)
            act.wait_ge(sm_pe, 3)
            for g in range(2):
                act.dma_start(vc[g], A[f"vc{g}"]).then_inc(sm_v[g], 16)
            act.wait_ge(sm_max, 1)
            nc.scalar.activation(srow, srow, ACT.Exp, bias=sstat[:, 1:2], accum_out=sstat[:, 2:3]).then_inc(sm_act, 1)
            act.wait_ge(sm_pe, 6)
            act.dma_start(vc[2], A["vc2"]).then_inc(sm_v[0], 16)
            act.wait_ge(sm_dve, 6)

            act.sem_inc(pt_ev, 2)
            act.sem_inc(au_ev, 1)
            act.sem_inc(o_stored, 16)
            for j in range(2):
                act.sem_inc(g_stored[j], 16)
            for g in range(NG):
                with act.Fori(0, 4) as i:
                    def unit_evac(j):
                        act.wait_ge(unit_done[j], i + (T0[f"att{g}"] + 2))
                        act.wait_ge(g_stored[j], i * 16 + (64 * g + 16))
                        apart(act)
                        if g < 2:
                            nc.scalar.activation(chunks(GT[j]), ups_v[0], ACT.Tanh, scale=0.5,
                                                 bias=bmrg[:, ds(i * 2 + (8 * g + j), 1)]).then_inc(au_ev, 1)
                        else:
                            nc.scalar.activation(chunks(GT[j]), ups_v[0], ACT.Copy).then_inc(au_ev, 1)
                        act.wait_ge(au_ev, i * 2 + (8 * g + j + 2))
                        act.dma_start(gate_s[ds(i * 2 + (8 * g + j), 1)].rearrange("a p t -> p (a t)"), GT[j]).then_inc(g_stored[j], 16)

                    act.wait_ge(vt_mm, i + (4 * g + 1))
                    act.wait_ge(pv_mm, i * 8 + (32 * g + 2))
                    for n in range(2):
                        ins = nc.scalar.activation(VTOK[:, 4 * n:4 * n + 4, :, 0:HD],
                                                   pt_bank[n].rearrange("p (b h e) -> p b h e", b=4, h=2), ACT.Copy)
                    ins.then_inc(vt_ev, 1)
                    for n in range(9):
                        if n >= 1:
                            q = n - 1
                            act.wait_ge(pt_mm, i * 8 + (32 * g + q + 3))
                            act.wait_ge(pv_mm, i * 8 + (32 * g + q + 1))
                            lo = 256 - P * nkeys(g, 2 * (q % 4))
                            if g < 2:
                                ins = nc.scalar.activation(PTS[q % 2][:, lo:512], pt_bank[q % 2][:, lo:512], ACT.Copy)
                            else:
                                ins = nc.scalar.activation(PTS[q % 2].rearrange("p (m c) -> p m c", m=2)[:, :, P:2 * P],
                                                           pt_bank[q % 2].rearrange("p (m c) -> p m c", m=2)[:, :, P:2 * P], ACT.Copy)
                            ins.then_inc(pt_ev, 1)
                        if n < 8:
                            act.wait_ge(nm_done, i * 8 + (32 * g + n + 1))
                            for m in range(2):
                                cols = slice(256 * m + 256 - P * nkeys(g, 2 * (n % 4) + m), 256 * m + 256)
                                ins = nc.scalar.activation(SB[n % 2][:, cols], SB[n % 2][:, cols], ACT.Exp,
                                                           bias=NM[:, 2 * (n % 2) + m:2 * (n % 2) + m + 1])
                            ins.then_inc(exp_done, 1)
                        if n == 4:
                            unit_evac(0)
                    unit_evac(1)
                    act.wait_ge(o_ev, i * 8 + (32 * g + 9))
                    pair = o_s[g].rearrange("t (f h) e -> t f h e", h=2)[:, ds(i, 1)].rearrange("t a h e -> t (a h e)")
                    if g == 0:
                        act.dma_start(pair.rearrange("(b p) e -> p b e", p=P), OT.rearrange("p b h e -> p b (h e)")).then_inc(o_stored, 16)
                    elif g == 1:
                        for c in range(2):
                            act.dma_start(pair.rearrange("(c p r) e -> c p r e", c=2, r=4)[c],
                                          OT.rearrange("p (r c) h e -> p r c (h e)", c=2)[:, :, c]).then_inc(o_stored, 16)
                    else:
                        act.dma_start(pair.rearrange("(m b) e -> m b e", b=8), OT.rearrange("p b h e -> p b (h e)")).then_inc(o_stored, 16)
            for n in range(8):
                act.wait_ge(dm_done, n + 1)
                nc.scalar.activation(ce, ce, ACT.Exp).then_inc(ce_done, 1)

            with act.Fori(0, 4) as i:
                for j in range(2):
                    act.wait_ge(mrg_sum[j], i + 1)
                    apart(act)
                    nc.scalar.activation(big1[:, 0, ds(i * 2 + j, 1), :], tmp(3 * j), ACT.Copy, scale=0.5).then_inc(mrg_hi[j], 1)
            norm(1)
            for n, (f0, nf) in enumerate(PARTS):
                with act.Fori(0, nf) as i:
                    act.wait_ge(unit_done[0], i + (T0[f"up{n}"] + 2))
                    act.wait_ge(sg_free, i + (f0 + 1))
                    nc.scalar.activation(chunks(ext[:, 0, 0:NT]), ups_v[0], ACT.Silu).then_inc(ps_free[0], 1)
            with act.Fori(0, 4) as i:
                for j in range(2):
                    act.wait_ge(ps_free[j], i + (T0["down2"] + 2 - 12))
                    act.dma_start(O["y_T"][ds(i * 2 + j, 1)].rearrange("a p t -> p (a t)"), x1[:, ds(i * 2 + j, 1), :].rearrange("p a t -> p (a t)"))\
                        .then_inc(y_stored, 16)
            act.wait_ge(y_stored, 16 * KT)
            act.wait_ge(out_done, 48)
            act.wait_ge(o_stored, O_STORES)
            for j in range(2):
                act.wait_ge(g_stored[j], 16 * 13)


        @block.vector
        def _(dve):
            step = Chain(dve, s_dve)
            nc.vector.memset(epst[:], EPS)
            nc.vector.memset(esel[:], 0.0)

            step.step(nc.vector.memset(ones[:], 1.0))
            nc.vector.memset(esel[:, NB - 1:NB], 1.0)
            dve.wait_ge(const_ld, CONSTS)
            dve.wait_ge(u_ps, 1)
            nc.vector.tensor_copy(u_lines, ups[0:HG, 0, :, 0:UL]).then_inc(u_sb, 1)
            for c in range(2):
                nc.vector.tensor_copy(gqk[:, 6 * c:6 * c + 6], gq2[:, c:c + 1].broadcast_to([P, 6]))
            step.step(nc.vector.tensor_scalar(bmrg[:], bmrg[:], 0.5, None, ALU.mult))

            def norm(r, gain):
                dve.wait_ge(nrt_done, r + 1)
                nc.vector.reciprocal(rsd[0:NB, 2, 8:9], rsd[0:NB, 1, 8:9])
                step.step(nc.vector.reciprocal(rsd[:, 2, 0:8], rsd[:, 1, 0:8]))
                nc.vector.tensor_copy(ext[0:NB, 0, 0:P], rsd[0:NB, 2, 8:9].broadcast_to([NB, P]))
                nc.vector.tensor_copy(ext[:, 3, 0:SEQ].rearrange("p (b n) -> p b n", b=8),
                                      rsd[:, 2, 0:8].unsqueeze(2).broadcast_to([P, 8, P])).then_inc(nex_done, 1)
                dve.wait_ge(nrb_done, r + 1)
                for k in range(KT):
                    if k >= 2:
                        dve.wait_ge(nlo_done, KT * r + k - 1)
                    nc.vector.scalar_tensor_tensor(ext[:, 1 + k % 2, 0:NT], tmp(k), gain[:, k:k + 1], ext[:, 0, 0:NT],
                                                   ALU.mult, ALU.mult).then_inc(nf_done, 1)

            norm(0, gmix)
            lam = par[:, :, 7]
            step.step(nc.vector.tensor_scalar(lamt[:, 0, :], lam, -1.0, None, ALU.mult))
            nc.vector.tensor_tensor(lamt[:, 0, :], lamt[:, 0, :], lam, ALU.max).then_inc(lam_dve, 1)
            dve.wait_ge(lam_act, 1)
            nc.vector.tensor_scalar(lamt[:, 2, :], lamt[:, 1, :], 1.0, None, ALU.add).then_inc(lam_dve, 1)
            dve.wait_ge(lam_act, 2)
            step.step(nc.vector.tensor_scalar(lamt[:, 2, :], lamt[:, 2, :], -1.0, None, ALU.add))
            step.step(nc.vector.tensor_scalar(cdec[:, 0, :], lamt[:, 2, :], 0.0, None, ALU.is_equal))
            step.step(nc.vector.tensor_tensor(lamt[:, 2, :], lamt[:, 2, :], cdec[:, 0, :], ALU.add))
            step.step(nc.vector.tensor_tensor(lamt[:, 3, :], lamt[:, 3, :], cdec[:, 0, :], ALU.add))
            step.step(nc.vector.reciprocal(lamt[:, 2, :], lamt[:, 2, :]))
            step.step(nc.vector.tensor_tensor(lamt[:, 3, :], lamt[:, 3, :], lamt[:, 2, :], ALU.mult))
            step.step(nc.vector.tensor_tensor(lamt[:, 3, :], lamt[:, 3, :], lamt[:, 1, :], ALU.mult))
            step.step(nc.vector.tensor_scalar(lamt[:, 0, :], lam, -1.0, 0.0, ALU.mult, ALU.max))
            step.step(nc.vector.tensor_tensor(lamt[:, 3, :], lamt[:, 3, :], lamt[:, 0, :], ALU.add))
            step.step(nc.vector.tensor_scalar(cdec[:, 0, :], lamt[:, 3, :], -8.0, None, ALU.mult))
            step.step(nc.vector.tensor_scalar(cdec[:, 1, :], lamt[:, 3, :], 8.0, None, ALU.mult))
            dve.wait_ge(nlo_done, KT)
            step.step(nc.vector.memset(ext[:, 0, 0:3], 0.0))

            for s in (ps_free[0], ps_free[1], conv_done, u_done, z_done):
                dve.sem_inc(s, 1)
            XC, GE, R, I, AD, M2, U, H = (tmp(n) for n in range(8))
            LX = ext[:, 0, :]
            with dve.Fori(0, KT) as i:
                step.loop(i, 15)
                dve.wait_ge(xc0_done, i + 1)
                for k in range(1, 4):
                    step.step(nc.vector.scalar_tensor_tensor(XC[:, 0:SEQ], LX[:, k:k + SEQ], par[:, ds(i, 1), k], XC[:, 0:SEQ], ALU.mult, ALU.add))
                for k in range(3):
                    prev = stc[:, ds(i, 1), 0:3 * NB].rearrange("p a (b c) -> p a b c", c=3)[:, :, :, k]
                    ins = nc.vector.scalar_tensor_tensor(XC[:, SEQ:NT], prev, par[:, ds(i, 1), k], XC[:, SEQ:NT], ALU.mult, ALU.add)
                    if k < 2:
                        step.step(ins)
                ins.then_inc(xc_done, 1)
                nc.vector.tensor_copy(sout[:, ds(i, 1), 0:11], LX[:, SEQ:SEQ + 11]).then_inc(conv_done, 1)
                dve.wait_ge(ath_done, i + 1)
                step.step(nc.vector.tensor_tensor(M2, AD, AD, ALU.mult))
                nc.vector.scalar_tensor_tensor(M2, M2, 1.0, R, ALU.add, ALU.mult).then_inc(m2_done, 1)
                dve.wait_ge(sqrt_done, i + 1)
                step.step(nc.vector.memset(M2[:, 0:1], 1.0))
                step.step(nc.vector.tensor_tensor(U, M2, I, ALU.mult))
                nc.vector.tensor_tensor(U, U, XC, ALU.mult).then_inc(u_done, 1)
                dve.wait_ge(u_done, i + 2)
                step.step(nc.vector.tensor_tensor_scan(H[:, 0:SEQ], AD[:, 0:SEQ], U[:, 0:SEQ], 0.0, ALU.mult, ALU.add))
                step.step(nc.vector.tensor_tensor(H[:, SEQ:NT], AD[:, SEQ:NT], stc[:, ds(i, 1), 3 * NB:4 * NB], ALU.mult))
                step.step(nc.vector.tensor_tensor(H[:, SEQ:NT], H[:, SEQ:NT], U[:, SEQ:NT], ALU.add))
                nc.vector.tensor_copy(sout[:, ds(i, 1), 11:20], H[:, SEQ - 1:NT])
                step.step(nc.vector.tensor_tensor(U, H, GE, ALU.mult))
                step.step(nc.vector.tensor_copy(big2[:, 0, ds(i, 1), :], U))
                step.step(nc.vector.tensor_tensor(big2[:, 1, ds(i, 1), :], U, big2[:, 0, ds(i, 1), :].bitcast(F32), ALU.subtract))
                step.step(nc.vector.memset(M2[:, 0:1], 0.0))
                nc.vector.memset(M2[:, 0:1], 0.0).then_inc(z_done, 1)
            step.end(KT)

            for j in range(2):
                dve.sem_inc(qn_done[j], 1)
            with dve.Fori(0, 12) as i:
                step.loop(i, 2)
                for j in range(2):
                    dve.wait_ge(sd_done[j], i + 1)
                    step.step(nc.vector.reciprocal(st[:, j, 16:32], st[:, j, 0:16]))
                    nc.vector.tensor_copy(tmp(4 + j)[:, 0:SEQ].rearrange("p (b e) -> p b e", e=HD),
                                          st[:, j, 16:32].unsqueeze(2).broadcast_to([P, 16, HD])).then_inc(ex_done[j], 1)
                    dve.wait_ge(bc_done[j], i + 1)
                    dve.wait_ge(qn_stored[j], i * 16 + 16)
                    nc.vector.scalar_tensor_tensor(tmp(6 + j)[:, 0:SEQ], tmp(j)[:, 0:SEQ], gqk[:, ds(i, 1)],
                                                   aux[:].rearrange("p b n -> p (b n)"), ALU.mult, ALU.mult).then_inc(qn_done[j], 1)
            step.end(12)

            dve.wait_ge(sqc_done, 36)
            dve.wait_ge(sm_ld, SM_LD)
            nc.vector.tensor_tensor(sqs, sqkv[:, 0:24, :].rearrange("p f b -> p (f b)"), sqkv[:, 0:24, :].rearrange("p f b -> p (f b)"),
                                    ALU.mult).then_inc(sm_dve, 1)
            dve.wait_ge(sm_pe, 2)
            nc.vector.tensor_copy(sbias, aux[0:ROWS, 1, 8:395])
            dve.wait_ge(sm_act, 1)
            step.step(nc.vector.reciprocal(rms, rms))
            for c in range(2):
                own = sqkv[:, 12 * c:12 * c + 12, :].rearrange("p f b -> p (f b)")
                step.step(nc.vector.scalar_tensor_tensor(own, own, gqk[:, 6 * c:6 * c + 1], rms[:, 96 * c:96 * c + 96], ALU.mult, ALU.mult))
            qmv = qm.rearrange("p (f b h) -> p f b h", b=NB, h=2)
            for h in range(2):
                step.step(nc.vector.tensor_scalar(qmv[:, :, :, h], sqkv[:, 0:12, :], hsel[:, h:h + 1], None, ALU.mult))
            nc.vector.tensor_tensor(pm.rearrange("p (f b h) -> p f b h", b=NB, h=2), qmv,
                                    sqkv[:, 12:24, :].unsqueeze(3).broadcast_to([P, 12, NB, 2]), ALU.mult).then_inc(sm_dve, 1)
            dve.wait_ge(sm_pe, 3)
            nc.vector.tensor_copy(sqs[:, 0:128], aux[:, 0, 0:128])
            nc.vector.tensor_copy(sqs[0:64, 128:192], aux[0:64, 0, 128:192]).then_inc(sm_dve, 1)
            dve.wait_ge(sm_pe, 4)
            for g in range(NG):
                n, skip = NKEY[g], 2 if g == 2 else 1
                nc.vector.scalar_tensor_tensor(srow[:, g * P:g * P + n], ups[0:ROWS, 0, 0, g * P:g * P + n], SCALE,
                                               sbias[:, 129 * g + skip:129 * g + n * skip + 1:skip][:, ::-1], ALU.mult, ALU.add)
            step.step(nc.vector.scalar_tensor_tensor(srow[:, 320:323], aux[0:ROWS, 1, 0:3], SCALE,
                                                     sbias.rearrange("p (g n) -> p g n", g=NG)[:, :, 0], ALU.mult, ALU.add))
            step.step(nc.vector.tensor_reduce(sstat[:, 0:1], srow, AX_X, ALU.max))
            nc.vector.tensor_scalar(sstat[:, 1:2], sstat[:, 0:1], -1.0, None, ALU.mult).then_inc(sm_max, 1)
            dve.wait_ge(sm_act, 2)
            step.step(nc.vector.reciprocal(sstat[:, 3:4], sstat[:, 2:3]))
            step.step(nc.vector.tensor_scalar(srow, srow, sstat[:, 3:4], None, ALU.mult))
            for g in range(NG):
                ins = nc.vector.tensor_scalar(r3[:, 32 * g:32 * g + 32], dsel, srow[:, 320 + g:321 + g], None, ALU.mult)
            ins.then_inc(sm_dve, 1)
            dve.wait_ge(sm_pe, 5)
            nc.vector.tensor_copy(pts[:, 0:128], aux[:, 0, 0:128])
            nc.vector.tensor_copy(pts[0:64, 128:192], aux[0:64, 0, 128:192]).then_inc(sm_dve, 1)
            step.step(nc.vector.tensor_tensor(rms[:, 0:96], aux[:, 1, 0:96], sqkv[:, 24:36, :].rearrange("p f b -> p (f b)"), ALU.mult))
            step.step(nc.vector.tensor_tensor(osum, rms[:, 0:32], rms[:, 32:64], ALU.add))
            step.step(nc.vector.tensor_tensor(osum, osum, rms[:, 64:96], ALU.add))
            dve.wait_ge(sm_pe, 8)
            dve.wait_ge(out_done, 48)
            for h in range(2):
                hr = slice(h * HD, (h + 1) * HD)
                ins = nc.vector.tensor_tensor(osam[hr], osum.rearrange("p (f b) -> p f b", f=4)[hr],
                                              ups[hr, 1, 0, 0:64].rearrange("p (f b h) -> p f b h", f=4, h=2)[:, :, :, h], ALU.add)
            ins.then_inc(sm_dve, 1)

            nc.vector.memset(VTOK[:, :, :, HD:HD + 1], 1.0)
            for s, n in ((att_free, 1), (sa_done, 2), (pt_mm, 2), (pv_mm, 2), (o_ev, 1)):
                dve.sem_inc(s, n)
            stores = 1
            for g in range(NG):
                per = 2 if g == 1 else 1
                with dve.Fori(0, 4) as i:
                    dve.wait_ge(qkv_ld, i * 64 + 64 * (4 * g + 1))
                    dve.wait_ge(o_stored, i * (16 * per) + 16 * stores)
                    step.loop(i, 8)
                    for n in range(10):
                        if n < 8:
                            hh, bp = n // 4, n % 4
                            dve.wait_ge(s_mm, i * 8 + (32 * g + n + 1))
                            dve.wait_ge(pt_mm, i * 8 + (32 * g + n + 1))
                            for m in range(2):
                                nk = nkeys(g, 2 * bp + m)
                                cols = slice(256 * m + 256 - P * nk, 256 * m + 256)
                                ins = nc.vector.scalar_tensor_tensor(SB[n % 2][:, cols], s_bank[n % 2][:, cols], SCALE,
                                                                     BT[:, hh, 0:P * nk][:, ::-1], ALU.mult, ALU.add)
                            ins.then_inc(sa_done, 1)
                            dve.wait_ge(sa_done, i * 8 + (32 * g + n + 3))
                            for m in range(2):
                                cols = slice(256 * m + 256 - P * nkeys(g, 2 * bp + m), 256 * m + 256)
                                ins = nc.vector.tensor_reduce(OT[:, 2 * bp + m, hh, HD + 1:HD + 2], SB[n % 2][:, cols], AX_X, ALU.max)
                            step.step(ins)
                            ins = nc.vector.tensor_scalar(NM[:, 2 * (n % 2):2 * (n % 2) + 2], OT[:, 2 * bp:2 * bp + 2, hh, HD + 1],
                                                          -1.0, None, ALU.mult).then_inc(nm_done, 1)
                        if n >= 2:
                            q = n - 2
                            hh, bp = q // 4, q % 4
                            dve.wait_ge(pv_mm, i * 8 + (32 * g + q + 3))
                            ins = nc.vector.tensor_copy(OT[:, 2 * bp:2 * bp + 2, hh, 0:HD + 1],
                                                        o_bank[:, 0:2 * (HD + 1)].rearrange("p (m e) -> p m e", m=2)).then_inc(o_ev, 1)
                    dve.wait_ge(o_ev, i * 8 + (32 * g + 9))
                    dve.sem_inc(att_free, 1)
                step.end(4)
                stores += 4 * per

            for n in range(8):
                o = OL[n % 2]
                dve.wait_ge(ol_ld[n % 2], 16 * (n // 2 + 1))
                mx = [o[:, g, :, HD + 1] for g in range(NG)]
                step.step(nc.vector.tensor_tensor(mt, mx[0], mx[1], ALU.max))
                step.step(nc.vector.tensor_tensor(mt, mt, mx[2], ALU.max))
                nc.vector.tensor_tensor(ce, o[:, :, :, HD + 1], mt.unsqueeze(1).broadcast_to([P, NG, HG]), ALU.subtract).then_inc(dm_done, 1)
                dve.wait_ge(ce_done, n + 1)
                step.step(nc.vector.tensor_tensor(cl, ce, o[:, :, :, HD], ALU.mult))
                step.step(nc.vector.tensor_tensor(den, cl[:, 0], cl[:, 1], ALU.add))
                step.step(nc.vector.tensor_tensor(den, den, cl[:, 2], ALU.add))
                step.step(nc.vector.reciprocal(den, den))
                step.step(nc.vector.tensor_tensor(cc, ce, den.unsqueeze(1).broadcast_to([P, NG, HG]), ALU.mult))
                if n:
                    dve.wait_ge(ot_mm, n)
                for g in range(NG):
                    cb = cc[:, g].unsqueeze(2).broadcast_to([P, HG, HD])
                    if g == 0:
                        step.step(nc.vector.tensor_tensor(oacc, o[:, g, :, 0:HD], cb, ALU.mult))
                    else:
                        step.step(nc.vector.tensor_tensor(oprod, o[:, g, :, 0:HD], cb, ALU.mult))
                        if g == 1:
                            step.step(nc.vector.tensor_tensor(oacc, oacc, oprod, ALU.add))
                        else:
                            nc.vector.tensor_tensor(oacc, oacc, oprod, ALU.add).then_inc(on_done, 1)
                nc.vector.tensor_copy(mt, mt).then_inc(cb_free[n % 2], 1)
                dve.wait_ge(ot_mm, n + 1)
                hi, lo = (big2[:, a, 0:4, n * P:(n + 1) * P] for a in range(2))
                src = aux[:, 0, :].rearrange("p (k t) -> p k t", k=4)
                step.step(nc.vector.tensor_copy(hi, src))
                nc.vector.tensor_tensor(lo, src, hi.bitcast(F32), ALU.subtract).then_inc(ot_done, 1)
            hi, lo = (big2[:, a, 0:4, SEQ:NT] for a in range(2))
            step.step(nc.vector.tensor_copy(hi, osam))
            nc.vector.tensor_tensor(lo, osam, hi.bitcast(F32), ALU.subtract).then_inc(ot_done, 1)

            dve.wait_ge(ot_done, 9)
            for s in (*mrg_done, *xr_free, sg_free):
                dve.sem_inc(s, 1)
            with dve.Fori(0, 4) as i:
                step.loop(i, 4)
                for j in range(2):
                    gl, ga, yl = (tmp(3 * j + n) for n in range(3))
                    dve.wait_ge(side_ld[j], i * 48 + 48)
                    step.step(nc.vector.scalar_tensor_tensor(gl, gl, 1.0, yl, ALU.add, ALU.mult))
                    dve.wait_ge(unit_done[j], i + (T0["merge"] + 2))
                    step.step(nc.vector.scalar_tensor_tensor(chunks(ga), chunks(ga), 1.0, ups_v[j], ALU.add, ALU.mult))
                    nc.vector.tensor_tensor(gl, gl, ga, ALU.add).then_inc(mrg_sum[j], 1)
                    dve.sem_inc(ps_free[j], 1)
                    dve.wait_ge(mrg_hi[j], i + 1)
                    nc.vector.scalar_tensor_tensor(big1[:, 1, ds(i * 2 + j, 1), :], gl, 0.5, big1[:, 0, ds(i * 2 + j, 1), :].bitcast(F32),
                                                   ALU.mult, ALU.subtract).then_inc(mrg_done[j], 1)
            step.end(4)
            with dve.Fori(0, 4) as i:
                for j in range(2):
                    dve.wait_ge(xr_ld[j], i * 16 + 16)
                    dve.wait_ge(unit_done[j], i + (T0["wo"] + 2))
                    apart(dve)
                    nc.vector.tensor_tensor(x1[:, ds(i * 2 + j, 1), :].rearrange("p a (c n) -> p (a c) n", c=NCH), ups_v[j],
                                            chunks(ext[:, 3 * j, 0:NT]), ALU.add).then_inc(wo_done, 1)
                    dve.wait_ge(wo_done, i * 2 + (j + 1))
                    dve.sem_inc(ps_free[j], 1)
                    dve.sem_inc(xr_free[j], 1)
            norm(1, gffn)
            for n, (f0, nf) in enumerate(PARTS):
                if n:
                    for j in range(2):
                        dve.wait_ge(unit_done[j], T0[f"up{n}"] + 1)
                with dve.Fori(0, nf) as i:
                    step.loop(i, 3)
                    dve.wait_ge(ps_free[0], i + (T0[f"up{n}"] + 2 - 12))
                    dve.wait_ge(unit_done[1], i + (T0[f"up{n}"] + 2))
                    step.step(nc.vector.tensor_tensor(chunks(ext[:, 1, 0:NT]), chunks(ext[:, 0, 0:NT]), ups_v[1], ALU.mult))
                    dve.sem_inc(ps_free[1], 1)
                    dve.sem_inc(sg_free, 1)
                    step.step(nc.vector.tensor_copy(big2[:, 0, ds(i, 1), :], ext[:, 1, 0:NT]))
                    step.step(nc.vector.tensor_tensor(big2[:, 1, ds(i, 1), :], ext[:, 1, 0:NT], big2[:, 0, ds(i, 1), :].bitcast(F32), ALU.subtract))
                    dve.sem_inc(h_done, 1)
                step.end(nf)
                with dve.Fori(0, 4) as i:
                    for j in range(2):
                        dve.wait_ge(unit_done[j], i + (T0[f"down{n}"] + 2))
                        own = x1[:, ds(i * 2 + j, 1), :].rearrange("p a (c n) -> p (a c) n", c=NCH)
                        apart(dve)
                        nc.vector.tensor_tensor(own, ups_v[j], own, ALU.add).then_inc(ps_free[j], 1)



_IN = ["x_prompt", "x_sample", "cache_kv_g0", "cache_kv_g1", "cache_kv_g2", "state_conv", "state_h", "rel_bias", "norm_mix",
       "w_in", "w_conv", "b_conv", "w_rg_a", "b_rg_a", "w_rg_x", "b_rg_x", "lru_lambda", "q_gain", "k_gain", "w_merge",
       "b_merge", "w_branch_lru", "w_branch_att", "w_o", "norm_ffn", "w_ffn_in", "w_ffn_out"]
_OUT = [("y_T", (KT, P, NT)), ("qkv", (36, P, SEQ)), ("sqkv", (P, 36, NB)), ("lru_out", (P, KT, 20)), ("state_out", (P, KT, 4 * NB))]


def kernel(**inputs):
    import concourse.bacc as bacc
    from concourse.bass_utils import run_bass_kernel_spmd as run

    nc = bacc.Bacc("TRN2", target_bir_lowering=False, num_devices=1)
    a = {name: np.ascontiguousarray(inputs[name]) for name in _IN}

    def tiles(v):
        return np.ascontiguousarray(v.reshape(-1, KT, P).transpose(2, 1, 0))

    def weights(w):
        k, n = w.shape
        return np.ascontiguousarray(w.reshape(k // P, P, n // P, P).transpose(2, 1, 0, 3))

    hsel = np.zeros((P, 2), np.float32)
    hsel[:HD, 0] = hsel[HD:, 1] = 1.0
    arrays = dict(c_ident=np.eye(P, dtype=np.float32), c_hsel=hsel, c_one=np.ones((1, NG * HG), np.float32),
                  c_bones=np.kron(np.eye(2, dtype=np.float32), np.ones((HD, HD), np.float32)), c_lines=bucket_lines(),
                  rel_bias=a["rel_bias"], w_rg_a=a["w_rg_a"], w_rg_x=a["w_rg_x"])
    for n in ("w_in", "w_merge", "w_branch_lru", "w_branch_att", "w_o", "w_ffn_in", "w_ffn_out"):
        arrays[n] = weights(a[n][0])
    x = np.concatenate([a["x_prompt"][0], a["x_sample"][:, 0]])
    arrays["x_T"] = np.ascontiguousarray(x.T.reshape(KT, P, NT))
    arrays["c_par"] = tiles(np.concatenate([a["w_conv"][0], a["b_conv"], a["b_rg_a"], a["b_rg_x"], a["lru_lambda"]]))
    arrays["c_state"] = tiles(np.concatenate([a["state_conv"][0].reshape(-1, D), a["state_h"][0]]))
    arrays["c_gains"] = np.ascontiguousarray(np.stack([np.tile(a[n][0], 2) for n in ("q_gain", "k_gain")], axis=1))
    for n in ("norm_mix", "norm_ffn"):
        arrays["c_" + n] = tiles(a[n])[:, :, 0].copy()
    arrays["c_b_merge"] = np.ascontiguousarray(a["b_merge"].reshape(16, P).T)
    for g in range(NG):
        kv = a[f"cache_kv_g{g}"][0, :, ::DIL[g]]
        n = kv.shape[1]
        assert n == NKEY[g]
        arrays[f"kc{g}"] = np.ascontiguousarray(kv[:, :, 0].reshape(NB, n, 4, P).transpose(3, 0, 2, 1))
        arrays[f"vc{g}"] = np.ascontiguousarray(kv[:, :, 1].reshape(NB, n, 512).transpose(1, 0, 2))
    row = np.arange(NB * HG)
    arrays["c_hm"] = (row[:, None] % 2 == np.arange(P)[None] // HD).astype(np.float32)
    arrays["c_dsel"] = (row[:, None] // 2 == np.arange(32)[None]).astype(np.float32)
    arrays["c_rsel"] = (np.arange(HG)[:, None] == (2 * (row // 16) + row % 2)[None]).astype(np.float32)
    A = {n: nc.dram_tensor(n, v.shape, F32, kind="ExternalInput").ap() for n, v in arrays.items()}
    O = {n: nc.dram_tensor("out_" + n, shape, F32, kind="ExternalOutput").ap() for n, shape in _OUT}
    build(nc, A, O)
    r = run(nc, [arrays], core_ids=[0]).results[0]
    y = r["out_y_T"].reshape(D, NT).T
    qkv = r["out_qkv"].reshape(3, NG, HG * HD, SEQ)[1:].transpose(1, 3, 0, 2).reshape(NG, SEQ, 2, HG, HD)
    sqkv = r["out_sqkv"].transpose(1, 0, 2).reshape(3, NG, HG * HD, NB)[1:].transpose(1, 3, 0, 2).reshape(NG, NB, 2, HG, HD)
    lru = r["out_lru_out"].transpose(2, 1, 0).reshape(20, D)
    state = r["out_state_out"].transpose(2, 1, 0).reshape(4 * NB, D)[:3 * NB].reshape(NB, 3, D)
    conv_s = np.concatenate([state[:, 1:], lru[3:11, None]], axis=1)[None]
    return (y[None, :SEQ].copy(), y[SEQ:, None].copy(), *(qkv[g, None, None, SEQ - n:].copy() for g, n in enumerate((128, 512, 1024))),
            lru[None, None, 0:3].copy(), lru[None, 11:12].copy(), *(sqkv[g, None, :, None].copy() for g in range(NG)),
            conv_s, lru[None, 12:20].copy())
```

```python
import math
from contextlib import ExitStack

import numpy as np

import concourse.bass as bass
from concourse import mybir

F32 = mybir.dt.float32
F32R = mybir.dt.float32r
ALU = mybir.AluOpType
ACT = mybir.ActivationFunctionType
AX_X = mybir.AxisListType.X
ds = bass.ds

P = 128
D = 1024
SEQ = 1024
NB = 8
NT = SEQ + NB
NCH = 3
CH = NT // NCH
KT = D // P
HD = 64
HG = 8
NG = 3
DIL = (1, 4, 16)
NKEY = (128, 128, 64)
ATT = NG * HG * HD
DFF = 2816
FT = DFF // P
PARTS = ((0, 8), (8, 8), (16, 6))
EPS = 1e-6
NEG = -1e30
SCALE = HD ** -0.5
NBK = 32
UL = 384


def bucket_lines():
    out = np.zeros((NG, NBK + 1, UL), np.float32)
    out[:, NBK] = NEG
    for g in range(NG):
        skip = 2 if g == 2 else 1
        at = np.arange(127, 256, skip)
        dist = np.arange(len(at)) * DIL[g]
        d_f = np.maximum(dist, 1).astype(np.float32)
        large = 16 + (np.log(d_f / np.float32(16)) / np.float32(math.log(2048 / 16)) * np.float32(16)).astype(np.int32)
        bucket = np.where(dist < 16, dist, np.minimum(large, NBK - 1))
        out[g, NBK, at] = 0.0
        out[g, bucket, at] = 1.0
    return out


class Chain:

    def __init__(self, eng, sem):
        self.eng, self.sem, self.base, self.n, self.i, self.per = eng, sem, 0, 0, 0, 0

    def loop(self, i, per, first=0):
        self.base += self.n - first * per
        self.i, self.per, self.n, self.first = i, per, 0, first

    def end(self, iterations):
        assert self.n == self.per, (self.n, self.per)
        self.base += self.per * (iterations + self.first)
        self.i = self.per = self.n = 0

    def step(self, ins):
        self.n += 1
        ins.then_inc(self.sem, 1)
        self.eng.wait_ge(self.sem, self.i * self.per + (self.base + self.n) if self.per else self.base + self.n)


def build(nc, A, O):
    with ExitStack() as ctx:
        def sb(name, shape, dt=F32):
            return ctx.enter_context(nc.sbuf_tensor(name, shape, dt))

        def sem(name):
            return ctx.enter_context(nc.semaphore(name))

        def dram(name, shape):
            return nc.dram_tensor(name, shape, F32, kind="Internal").ap()

        with nc.sbuf_tensor("big1_f32", [P, 2, KT, NT], F32) as big1_f32, nc.sbuf_tensor("big2_f32", [P, 2, KT, NT], F32) as big2_f32:
            pass
        big1 = sb("big1", [P, 2, KT, NT], F32R)
        big2 = sb("big2", [P, 2, KT, NT], F32R)
        x1 = sb("x1", [P, KT, NT])
        wraw = sb("wraw", [P, 2, KT, P])
        wsp = sb("wsp", [P, 2, 2, KT, P], F32R)
        ext = sb("ext", [P, 4, NT + 3])
        ident = sb("ident", [P, P])
        hsel = sb("hsel", [P, 2])
        ones = sb("ones", [P, P])
        par = sb("par", [P, KT, 8])
        cdec = sb("cdec", [P, 2, KT])
        lamt = sb("lamt", [P, 4, KT])
        gmix = sb("gmix", [P, KT])
        gffn = sb("gffn", [P, KT])
        bones = sb("bones", [P, P])
        gq2 = sb("gq2", [P, 2])
        relx = sb("relx", [NBK + 1, NG * HG])
        gqk = sb("gqk", [P, 12])
        bmrg = sb("bmrg", [P, 16])
        bd = sb("bd", [P, 2, P])
        sqkv = sb("sqkv", [P, 36, NB])
        stc = sb("stc", [P, KT, 4 * NB])
        sout = sb("sout", [P, KT, 20])
        st = sb("st", [P, 2, 32])
        epst = sb("epst", [P, 1])
        lines = big2_f32[0:NBK + 1, 0, 0:2, :].rearrange("p a n -> p (a n)")[:, 0:NG * UL]
        u_lines = big2_f32[0:HG, 1, 6:8, :].rearrange("p a n -> p (a n)")[:, 0:NG * UL].rearrange("p (g n) -> p g n", g=NG)
        sums, rrms = big1_f32[:, 1, KT - 1, :], ext[:, 0, 0:NT]
        normed = [ext[:, 1 + n, 0:NT] for n in range(3)]
        POOL_LOW = (1, 4, 7)

        def tmp(n):
            return x1[:, n, :]

        ups = ctx.enter_context(nc.psum_tensor("ups", [P, 2, NCH, 512], F32))
        aux = ctx.enter_context(nc.psum_tensor("aux", [P, 2, 512], F32))

        qkv_s = O["qkv"]
        gate_s = dram("gate_s", [24, P, NT])
        o_s = dram("o_s", [NG, SEQ, HG, HD + 2])
        u_s = dram("u_s", [NG * HG, UL])
        bt_s = dram("bt_s", [NG * HG, P, 2 * P])

        stream = [
            ("lru", 8, KT, A["w_in"], 0, 8, 1, 0),
            ("qk", 12, KT, A["w_in"], 16, 17, 2, 0),
            ("v", 2, KT, A["w_in"], 40, 41, 2, 0),
            ("att0", 4, KT, A["w_in"], 44, 45, 2, 0),
            ("att1", 4, KT, A["w_merge"], 0, 1, 2, 0),
            ("att2", 4, KT, A["w_merge"], 8, 9, 2, 0),
            ("ylru", 4, KT, A["w_branch_lru"], 0, 1, 2, 0),
            ("merge", 4, 4, A["w_branch_att"], 0, 1, 2, 0),
            ("wo", 4, KT, A["w_o"], 0, 1, 2, 0),
        ]
        for n, (f0, nf) in enumerate(PARTS):
            stream.append((f"up{n}", nf, KT, A["w_ffn_in"], f0, FT + f0, 1, 0))
            stream.append((f"down{n}", 4, nf, A["w_ffn_out"], 0, 1, 2, f0))
        T0, t = {}, 0
        for s in stream:
            T0[s[0]] = t
            t += s[1]

        def two(name):
            return [sem(f"{name}{j}") for j in range(2)]

        w_loaded, w_split, unit_done, ps_free = two("w_loaded"), two("w_split"), two("unit_done"), two("ps_free")
        w_hi, ticks = sem("w_hi"), sem("ticks")
        s_dve, s_act, s_pool = sem("s_dve"), sem("s_act"), sem("s_pool")
        const_ld = sem("const_ld")
        bd_zero = sem("bd_zero")
        x_loaded = [sem(f"x_loaded{k}") for k in range(KT)]
        ones_done, nsq_done, nadd_done, nst_mm, nrt_done = (sem(n) for n in ("ones_done", "nsq_done", "nadd_done", "nst_mm", "nrt_done"))
        nf_done, nhi_done, nlo_dve, nlo_pool = sem("nf_done"), sem("nhi_done"), sem("nlo_dve"), sem("nlo_pool")
        u_ps, u_sb, u_stored = sem("u_ps"), sem("u_sb"), sem("u_stored")
        lam_act, lam_dve = sem("lam_act"), sem("lam_dve")

        bd_loaded, xc0_done, xc_done = sem("bd_loaded"), sem("xc0_done"), sem("xc_done")
        conv_done, u_done, z_done = sem("conv_done"), sem("u_done"), sem("z_done")
        gate_mm, gate_ev, ath_done, m2_done, sqrt_done = sem("gate_mm"), sem("gate_ev"), sem("ath_done"), sem("m2_done"), sem("sqrt_done")
        out_done, lru_done = sem("out_done"), sem("lru_done")
        qsq_done, st_done, rt_done, qn_done = two("qsq_done"), two("st_done"), two("rt_done"), two("qn_done")
        qn_stored = two("qn_stored")
        sqc_done = sem("sqc_done")
        v_stored = two("v_stored")

        bt_fill = sem("bt_fill")
        sm_ld, sm_dve, sm_pe, sm_act, sm_max = sem("sm_ld"), sem("sm_dve"), sem("sm_pe"), sem("sm_act"), sem("sm_max")
        kv_ld, kv_used = two("kv_ld"), two("kv_used")
        v_ld, qk_ld, au_mm, au_ev, g_stored, o_stored = sem("v_ld"), sem("qk_ld"), sem("au_mm"), sem("au_ev"), two("g_stored"), sem("o_stored")
        vt_mm, vt_ev, s_mm, sa_done, nm_done, exp_done, pt_mm, pt_ev, pv_mm, o_ev = (
            sem(n) for n in ("vt_mm", "vt_ev", "s_mm", "sa_done", "nm_done", "exp_done", "pt_mm", "pt_ev", "pv_mm", "o_ev"))
        ol_ld, cb_free, dm_done, ce_done, on_done, ot_mm, ot_done = (
            two("ol_ld"), two("cb_free"), sem("dm_done"), sem("ce_done"), sem("on_done"), sem("ot_mm"), sem("ot_done"))
        side_ld, mrg_sum, mrg_hi, mrg_done = two("side_ld"), two("mrg_sum"), two("mrg_hi"), two("mrg_done")
        xr_ld, xr_free, wo_done = two("xr_ld"), two("xr_free"), sem("wo_done")
        sg_free, h_done, y_stored = sem("sg_free"), sem("h_done"), sem("y_stored")

        kv = [big1_f32[:, a, 4:8, :].rearrange("p a n -> p (a n)") for a in range(2)]
        kc = [kv[g % 2][:, 0:NB * 4 * n].rearrange("p (b f n) -> p b f n", b=NB, f=4) for g, n in enumerate(NKEY)]
        vc = [kv[(g + 1) % 2][0:n, 0:NB * 512].rearrange("p (b f) -> p b f", b=NB) for g, n in enumerate(NKEY)]
        small = ext[:, 1:3, :].rearrange("p a n -> p (a n)")
        ROWS = NB * HG

        def part(a, n, p=P):
            return small[0:p, a:a + n]

        qm, pm, sqs, rms = (part(192 * n, 192) for n in range(4))
        srow, sbias = part(768, 323, ROWS), part(1091, 387, ROWS)
        pts, hm, dsel = part(1478, 192), part(1670, P, ROWS), part(1798, 32, ROWS)
        r3, rsel, ul8 = part(1830, 96, ROWS), part(1926, ROWS, HG), part(768, 387, HG)
        osum = part(1990, 32)
        sstat = st[0:ROWS, 0, 0:4]
        osam = stc[:, 0:4, 0:NB]

        QT, KTT, VT = tmp(0)[:, 0:SEQ], tmp(1)[:, 0:SEQ], tmp(2)[:, 0:SEQ]
        SB = [tmp(3)[:, 512 * n:512 * n + 512] for n in range(2)]
        PTS = [tmp(4)[:, 512 * n:512 * n + 512] for n in range(2)]
        OT = x1[:, 5:7, :].rearrange("p a n -> p (a n)")[:, 0:16 * (HD + 2)].rearrange("p (b h e) -> p b h e", b=8, h=2)
        VTOK = ext[:, 1:3, :].rearrange("p a n -> p (a n)")[:, 0:16 * (HD + 1)].rearrange("p (b h e) -> p b h e", b=8, h=2)
        BT = ext[:, 0, 0:512].rearrange("p (h n) -> p h n", h=2)
        NM = ext[:, 0, 512:516]
        GT = [tmp(7), ext[:, 3, 0:NT]]
        s_bank = [ups[:, 1, 0, :], ups[:, 1, 1, :]]
        pt_bank = [ups[:, 1, 2, :], aux[:, 0, :]]
        o_bank = aux[:, 1, :]

        def toks(ap, g, b, n=1):
            if g == 0:
                return ap[:, (b + 1 - n) * P:(b + 1) * P]
            if g == 1:
                return ap.rearrange("p (m d) -> p d m", d=4)[:, b // 2, (b % 2 + 1 - n) * P:(b % 2 + 1) * P]
            return ap.rearrange("p (m d) -> p d m", d=8)[:, b]

        def nkeys(g, b):
            return (2 if b else 1, 1 + b % 2, 1)[g]

        OL = [x1[:, 2 * n:2 * n + 2, :].rearrange("p a n -> p (a n)")[:, 0:NG * HG * (HD + 2)]
              .rearrange("p (g h e) -> p g h e", g=NG, h=HG) for n in range(2)]
        mt = tmp(4)[:, 0:8]
        ce, cl, cc = (tmp(4)[:, 32 * n:32 * n + 24].rearrange("p (g h) -> p g h", g=NG) for n in range(1, 4))
        den = tmp(4)[:, 128:136]
        oacc, oprod = (tmp(5 + n)[:, 0:512].rearrange("p (h e) -> p h e", h=HG) for n in range(2))

        ups_v = [ups[:, j, :, 0:CH] for j in range(2)]

        def apart(eng):
            eng.sem_inc(ticks, 1)

        def tile_split(eng, r, k):
            if k in POOL_LOW:
                eng.wait_ge(nlo_pool, len(POOL_LOW) * r + POOL_LOW.index(k) + 1)
            else:
                eng.wait_ge(nlo_dve, (KT - len(POOL_LOW)) * r + k + 1 - sum(n < k for n in POOL_LOW))

        def chunks(ap):
            return ap.rearrange("p (c n) -> p c n", c=NCH)

        consts = [
            (ident[:], A["c_ident"]), (hsel[:], A["c_hsel"]), (relx[0:NBK, :], A["rel_bias"]),
            (relx[NBK:NBK + 1, :], A["c_one"]),
            (lines.rearrange("p (g n) -> p g n", g=NG), A["c_lines"].rearrange("g b n -> b g n")),
            (stc[:], A["c_state"]), (bones[:], A["c_bones"]),
            (gmix[:], A["c_norm_mix"]), (gffn[:], A["c_norm_ffn"]), (bmrg[:], A["c_b_merge"]),
            (par[:], A["c_par"]), (gq2[:], A["c_gains"]),
        ]
        CONSTS = 16 * len(consts)
        kv_loads = [(kc[g], A[f"kc{g}"]) for g in range(NG)] + [(vc[g], A[f"vc{g}"]) for g in range(NG)]
        sm_loads = [(hm, A["c_hm"]), (dsel, A["c_dsel"]), (rsel, A["c_rsel"]),
                     (ul8.rearrange("h (g n) -> h g n", g=NG), u_s.rearrange("(g h) n -> h g n", g=NG)[:, :, 127:256])]
        SM_LD = 16 * len(sm_loads)
        O_STORES = 16 * (1 + 4 + 8 + 4)
        block = ctx.enter_context(nc.Block())

        @block.sync
        def _(sp):
            for k in range(KT):
                sp.dma_start(tmp(k), A["x_T"][k]).then_inc(x_loaded[k], 16)
            for name, iters, nk, src, f0, f1, step, k0 in stream:

                def weights(i, slot):
                    f = (f0, f1)[slot]
                    sp.wait_ge(w_split[slot], i + (T0[name] + 1))
                    sp.dma_start(wraw[:, slot, 0:nk, :],
                                 src[ds(i * step + f, 1), :, k0:k0 + nk, :].rearrange("a p k n -> p (a k) n")).then_inc(w_loaded[slot], 16)

                if name == "ylru":
                    def outputs(n):
                        if n >= 2:
                            sp.wait_ge(cb_free[n % 2], n // 2)
                        sp.dma_start(OL[n % 2], o_s[:, n * P:(n + 1) * P].rearrange("g t h e -> t g h e")).then_inc(ol_ld[n % 2], 16)

                    def cache(n):
                        if n >= 2:
                            sp.wait_ge(kv_used[n % 2], n // 2)
                        sp.dma_start(*kv_loads[n]).then_inc(kv_ld[n % 2], 16)

                    weights(0, 0)
                    weights(0, 1)
                    for j in range(2):
                        sp.wait_ge(unit_done[j], T0["ylru"] + 1)
                    cache(0)
                    sp.wait_ge(o_stored, O_STORES)
                    outputs(0)
                    outputs(1)
                    cache(1)
                    weights(1, 0)
                    weights(1, 1)
                    outputs(2)
                    cache(2)
                    weights(2, 0)
                    outputs(3)
                    cache(3)
                    weights(2, 1)
                    outputs(4)
                    cache(4)
                    weights(3, 0)
                    outputs(5)
                    weights(3, 1)
                    outputs(6)
                    outputs(7)
                    cache(5)
                    continue
                with sp.Fori(0, iters) as i:
                    for slot in range(2):
                        weights(i, slot)
                    if name.startswith("att"):
                        g = int(name[3])
                        for j in range(2):
                            if g == 0:
                                sp.wait_ge(qn_stored[j], 16 * 13)
                                sp.wait_ge(v_stored[j], 16 * 3)
                                sp.wait_ge(bt_fill, 16)
                            else:
                                sp.wait_ge(g_stored[j], 16 * (2 * g + 1))
                        sp.wait_ge(sa_done, 2)
                        sp.wait_ge(vt_mm, i + (4 * g + 1))
                        sp.dma_start(VT, qkv_s[ds(i + (24 + 4 * g), 1)].rearrange("a p t -> p (a t)")).then_inc(v_ld, 16)
                        sp.wait_ge(sa_done, i * 8 + (32 * g + 2))
                        for n, t in enumerate((QT, KTT)):
                            sp.dma_start(t, qkv_s[ds(i + (12 * n + 4 * g), 1)].rearrange("a p t -> p (a t)")).then_inc(qk_ld, 16)
                        sp.dma_start(BT, bt_s[ds(i * 2 + 8 * g, 2)].rearrange("h p n -> p h n")).then_inc(qk_ld, 16)
                    if name == "merge":
                        for j in range(2):
                            sp.wait_ge(g_stored[j], 16 * 17)
                            sp.wait_ge(mrg_sum[j], i + 1)
                            for n in range(3):
                                sp.dma_start(tmp(3 * j + n), gate_s[ds(i * 2 + (8 * n + j), 1)].rearrange("a p t -> p (a t)"))\
                                    .then_inc(side_ld[j], 16)
                    if name == "wo":
                        for j in range(2):
                            sp.wait_ge(xr_free[j], i + 1)
                            sp.dma_start(ext[:, 3 * j, 0:NT], A["x_T"][ds(i * 2 + j, 1)].rearrange("a p t -> p (a t)")).then_inc(xr_ld[j], 16)

        @block.gpsimd
        def _(pool):
            nc.gpsimd.memset(bd[:], 0.0).then_inc(bd_zero, 1)
            for j in range(2):
                pool.sem_inc(w_split[j], 1)

            def split(name, nk, i, slot):
                pool.wait_ge(w_loaded[slot], i * 16 + 16 * (T0[name] + 1))
                pool.wait_ge(unit_done[slot], i + (T0[name] + 1))
                apart(pool)
                raw, hi, lo = wraw[:, slot, 0:nk, :], wsp[:, slot, 0, 0:nk, :], wsp[:, slot, 1, 0:nk, :]
                nc.gpsimd.tensor_copy(hi, raw).then_inc(w_hi, 1)
                pool.wait_ge(w_hi, i * 2 + (2 * T0[name] + slot + 1))
                nc.gpsimd.tensor_tensor(lo, raw, hi.bitcast(F32), ALU.subtract).then_inc(w_split[slot], 1)

            for name, iters, nk, *_ in stream:
                first = 0
                if name in ("lru", "up0"):
                    first, r = 1, int(name == "up0")
                    split(name, nk, 0, 0)
                    for k in POOL_LOW:
                        pool.wait_ge(nhi_done, KT * r + k + 1)
                        nc.gpsimd.tensor_tensor(big1[:, 1, k, :], normed[k % 3], big1[:, 0, k, :].bitcast(F32),
                                                ALU.subtract).then_inc(nlo_pool, 1)
                    split(name, nk, 0, 1)
                with pool.Fori(first, iters) as i:
                    for slot in range(2):
                        split(name, nk, i, slot)

        @block.tensor
        def _(pe):
            def unit(name, i, slot, src, nk=KT, parts=(0, 1, 2), norm=None, hidden=0):
                if 0 in parts:
                    pe.wait_ge(w_split[slot], i + (T0[name] + 2))
                    pe.wait_ge(ps_free[slot], i + (T0[name] + 1 - (12 if T0[name] >= T0["ylru"] else 0)))
                for c in parts:
                    for k in range(nk):
                        if norm is not None and c == 0:
                            tile_split(pe, norm, k)
                        if hidden and c == 0 and k == nk - 1:
                            pe.wait_ge(h_done, hidden)
                        for w, a in ((0, 0), (0, 1), (1, 0)):
                            ins = nc.tensor.matmul(ups[:, slot, c, 0:CH], wsp[:, slot, w, k, :], src[:, a, k, c * CH:(c + 1) * CH],
                                                   start=(k == 0 and w + a == 0), stop=(k == nk - 1 and w == 1))
                if NCH - 1 in parts:
                    ins.then_inc(unit_done[slot], 1)

            for j in range(2):
                pe.sem_inc(unit_done[j], 1)
            def norm_sums(r):
                pe.wait_ge(nadd_done, (KT + 1) * (r + 1))
                for c in range(NCH):
                    ins = nc.tensor.matmul(ups[:, 0, c, 0:CH], ones[:], sums[:, c * CH:(c + 1) * CH], start=True, stop=True)
                ins.then_inc(nst_mm, 1)

            pe.wait_ge(ones_done, 1)
            norm_sums(0)
            pe.wait_ge(const_ld, CONSTS)
            for g in range(NG):
                ins = nc.tensor.matmul(ups[0:HG, 1, g, 0:UL], relx[:, g * HG:(g + 1) * HG], lines[:, g * UL:(g + 1) * UL], start=True, stop=True)
            ins.then_inc(u_ps, 1)

            pe.sem_inc(gate_mm, 1)

            def gates(i, c):
                if c == 0:
                    pe.wait_ge(bd_loaded, i * 64 + 64)
                    pe.wait_ge(xc_done, i + 1)
                pe.wait_ge(gate_ev, i * NCH + (c + 1))
                for a in range(2):
                    ins = nc.tensor.matmul(aux[:, a, 0:CH], bd[:, a, :], tmp(0)[:, c * CH:(c + 1) * CH], start=True, stop=True)
                ins.then_inc(gate_mm, 1)

            def lru(i, first):
                for c in range(NCH):
                    unit("lru", i, 0, big1, parts=(c,), norm=0 if first else None)
                    if c < 2 and not first:
                        gates(i - 1, c + 1)
                if first:
                    pe.wait_ge(u_sb, 1)
                unit("lru", i, 1, big1)
                gates(i, 0)

            lru(0, True)
            with pe.Fori(1, KT) as i:
                lru(i, False)
            gates(KT - 1, 1)
            gates(KT - 1, 2)
            pe.wait_ge(gate_ev, KT * NCH + 1)
            def stats(j, i):
                pe.wait_ge(qsq_done[j], i + 1)
                pe.wait_ge(rt_done[1 - j], i + 1)
                for c in range(2):
                    ins = nc.tensor.matmul(aux[:, c, :], bones[:], tmp(2 + j)[:, c * 512:(c + 1) * 512], start=True, stop=True)
                ins.then_inc(st_done[j], 1)

            def qk(i, first):
                for j in range(2):
                    unit("qk", i, j, big1, parts=(0,))
                    if j:
                        stats(0, i)
                    elif not first:
                        stats(1, i - 1)
                    unit("qk", i, j, big1, parts=(1, 2))

            pe.sem_inc(rt_done[1], 1)
            qk(0, True)
            with pe.Fori(1, 12) as i:
                qk(i, False)
            stats(1, 11)
            with pe.Fori(0, 2) as i:
                unit("v", i, 0, big1)
                unit("v", i, 1, big1)

            pe.wait_ge(ps_free[0], T0["att0"] + 1)
            pe.wait_ge(ps_free[1], T0["att0"] + 1)
            pe.wait_ge(rt_done[1], 13)
            pe.sem_inc(vt_mm, 1)
            for g in range(NG):
                with pe.Fori(0, 4) as i:
                    def pieces(a, b):
                        for n in range(a, b):
                            slot, c, k = n // 24, n // 8 % 3, n % 8
                            if n % 24 == 0:
                                pe.wait_ge(w_split[slot], i + (T0[f"att{g}"] + 2))
                            if n % 8 == 0:
                                pe.wait_ge(au_ev, i * 6 + (24 * g + n // 8 + 1))
                            for w, a2 in ((0, 0), (0, 1), (1, 0)):
                                ins = nc.tensor.matmul(ups[:, 0, c, 0:CH], wsp[:, slot, w, k, :], big1[:, a2, k, c * CH:(c + 1) * CH],
                                                       start=(k == 0 and w + a2 == 0), stop=(k == KT - 1 and w == 1))
                            if n % 8 == 7:
                                ins.then_inc(au_mm if c < NCH - 1 else unit_done[slot], 1)

                    pe.wait_ge(v_ld, i * 16 + 16 * (4 * g + 1))
                    pe.wait_ge(pt_ev, i * 8 + (32 * g + 2))
                    for b in range(8):
                        ins = nc.tensor.transpose(pt_bank[b // 4][:, (b % 4) * P:(b % 4 + 1) * P], toks(VT, g, b), ident[:])
                    ins.then_inc(vt_mm, 1)
                    pieces(0, 8)
                    pe.wait_ge(qk_ld, i * 48 + 48 * (4 * g + 1))
                    for n in range(10):
                        if n < 8:
                            hh, bp = n // 4, n % 4
                            hr = slice(hh * HD, (hh + 1) * HD)
                            pe.wait_ge(sa_done, i * 8 + (32 * g + n + 1))
                            for m in range(2):
                                b = 2 * bp + m
                                nk = nkeys(g, b)
                                ins = nc.tensor.matmul(s_bank[n % 2][:, 256 * m + 256 - P * nk:256 * m + 256], toks(QT, g, b)[hr],
                                                       toks(KTT, g, b, nk)[hr], start=True, stop=True)
                            ins.then_inc(s_mm, 1)
                        if 1 <= n <= 8:
                            q = n - 1
                            pe.wait_ge(exp_done, i * 8 + (32 * g + q + 1))
                            pe.wait_ge(pt_ev, i * 8 + (32 * g + q + 1))
                            if q == 0:
                                pe.wait_ge(vt_ev, i + (4 * g + 1))
                            for m in range(2):
                                for c in range(256 * m + 256 - P * nkeys(g, 2 * (q % 4) + m), 256 * m + 256, P):
                                    ins = nc.tensor.transpose(pt_bank[q % 2][:, c:c + P], SB[q % 2][:, c:c + P], ident[:])
                            ins.then_inc(pt_mm, 1)
                        if n >= 2:
                            q = n - 2
                            hh, bp = q // 4, q % 4
                            pe.wait_ge(pt_ev, i * 8 + (32 * g + q + 3))
                            pe.wait_ge(o_ev, i * 8 + (32 * g + q + 1))
                            for m in range(2):
                                b = 2 * bp + m
                                nk = nkeys(g, b)
                                for k in range(nk):
                                    c = 256 * m + 256 - P * (nk - k)
                                    ins = nc.tensor.matmul(o_bank[:, m * (HD + 1):(m + 1) * (HD + 1)], PTS[q % 2][:, c:c + P],
                                                           VTOK[:, b + 1 - nk + k, hh, :], start=(k == 0), stop=(k == nk - 1))
                            ins.then_inc(pv_mm, 1)
                        pieces(8 + 4 * n, 12 + 4 * n)

            def head_squares():
                pe.wait_ge(sm_dve, 1)
                nc.tensor.matmul(aux[:, 1, 0:192], bones[:], sqs, start=True, stop=True).then_inc(sm_pe, 1)

            def bias_rows():
                pe.wait_ge(sm_ld, SM_LD)
                pe.wait_ge(sm_act, 1)
                nc.tensor.matmul(aux[0:ROWS, 1, 0:387], rsel, ul8, start=True, stop=True).then_inc(sm_pe, 1)

            def scores(g):
                pe.wait_ge(kv_ld[g % 2], 16 * (g // 2 + 1))
                pe.wait_ge(sm_dve, 2)
                nc.tensor.matmul(aux[0:ROWS, 1, 400 + g:401 + g], pm[:, 64 * g:64 * g + 64], ones[:, 0:1], start=True, stop=True)
                for f in range(4):
                    for b in range(NB):
                        at = 64 * g + 16 * f + 2 * b
                        ins = nc.tensor.matmul(aux[0:NKEY[g], 1, at:at + 2], kc[g][:, b, f, :], qm[:, at:at + 2], start=True, stop=True)
                ins.then_inc(kv_used[g % 2], 1)

            def score_rows():
                pe.wait_ge(sm_dve, 3)
                for g in range(NG):
                    ins = nc.tensor.transpose(aux[0:ROWS, 1, g * P:g * P + NKEY[g]], sqs[0:NKEY[g], 64 * g:64 * g + 64],
                                              ident[0:NKEY[g], 0:NKEY[g]])
                ins.then_inc(sm_pe, 1)

            def prob_columns():
                pe.wait_ge(sm_dve, 4)
                for g in range(NG):
                    nc.tensor.transpose(aux[0:NKEY[g], 1, 64 * g:64 * g + 64], srow[:, g * P:g * P + NKEY[g]], ident[0:ROWS, 0:ROWS])
                nc.tensor.matmul(aux[:, 1, 192:288], hm, r3, start=True, stop=True).then_inc(sm_pe, 1)

            def values(g):
                pe.wait_ge(kv_ld[(g + 1) % 2], 16 * ((g + 3) // 2 + 1))
                pe.wait_ge(sm_dve, 5)
                for f in range(4):
                    for b in range(NB):
                        at = 16 * f + 2 * b
                        ins = nc.tensor.matmul(aux[:, 1, 448 + at:450 + at], vc[g][:, b, f * P:(f + 1) * P],
                                               pts[0:NKEY[g], 64 * g + at:64 * g + at + 2],
                                               start=(g + f + b == 0), stop=(g == NG - 1), skip_group_check=True)
                ins.then_inc(kv_used[(g + 1) % 2], 1)

            def turn(n):
                pe.wait_ge(on_done, n + 1)
                if n:
                    pe.wait_ge(ot_done, n)
                for k in range(4):
                    ins = nc.tensor.transpose(aux[:, 0, k * P:(k + 1) * P], tmp(5)[:, k * P:(k + 1) * P], ident[:])
                ins.then_inc(ot_mm, 1)

            pe.wait_ge(lru_done, KT)
            pe.wait_ge(au_ev, 12 * 6 + NCH)
            pe.wait_ge(sa_done, 98)
            pe.wait_ge(pt_ev, 98)
            pe.wait_ge(o_ev, 97)
            beside = {0: [head_squares], 1: [bias_rows], 4: [(turn, 0)], 5: [(scores, 0)], 6: [(turn, 1)], 7: [(scores, 1)],
                      9: [(turn, 2), (scores, 2)], 12: [(turn, 3), score_rows], 14: [(turn, 4)], 15: [prob_columns], 17: [(turn, 5)],
                      18: [(values, 0)], 19: [(values, 1)], 20: [(turn, 6)], 22: [(values, 2)], 23: [(turn, 7)]}
            for n in range(8):
                for c in range(NCH):
                    unit("ylru", n // 2, n % 2, big2, parts=(c,))
                    for do in beside.get(n * NCH + c, []):
                        do() if callable(do) else do[0](do[1])
            pe.wait_ge(ot_done, 9)
            with pe.Fori(0, 4) as i:
                unit("merge", i, 0, big1, nk=4)
                unit("merge", i, 1, big1, nk=4)
            for j in range(2):
                pe.wait_ge(mrg_done[j], 4)
            with pe.Fori(0, 4) as i:
                unit("wo", i, 0, big2)
                unit("wo", i, 1, big2)
            norm_sums(1)
            for n, (f0, nf) in enumerate(PARTS):
                with pe.Fori(0, nf) as i:
                    unit(f"up{n}", i, 0, big1, norm=None if n else 1)
                    unit(f"up{n}", i, 1, big1)
                pe.wait_ge(h_done, f0 + nf - 1)
                with pe.Fori(0, 4) as i:
                    unit(f"down{n}", i, 0, big2, nk=nf, hidden=f0 + nf)
                    unit(f"down{n}", i, 1, big2, nk=nf)


        @block.scalar
        def _(act):
            step = Chain(act, s_act)
            for dst, src in consts:
                act.dma_start(dst, src).then_inc(const_ld, 16)
            def square(r, k, at):
                if isinstance(k, int):
                    act.wait_ge(x_loaded[k], 16)
                    if k:
                        act.wait_ge(nadd_done, k)
                    nc.scalar.activation(ext[:, 1 + at, 0:NT], tmp(k), ACT.Square).then_inc(nsq_done, 1)
                else:
                    act.wait_ge(wo_done, k + 1)
                    act.wait_ge(nadd_done, k + (KT + 1))
                    apart(act)
                    nc.scalar.activation(ext[:, 1 + at, 0:NT], x1[:, ds(k, 1), :].rearrange("p a n -> p (a n)"), ACT.Square).then_inc(nsq_done, 1)

            def norm(r):
                act.wait_ge(nst_mm, r + 1)
                nc.scalar.activation(chunks(rrms), ups_v[0], ACT.Sqrt, scale=1.0 / D, bias=epst[:]).then_inc(nrt_done, 1)
                for k in range(KT):
                    act.wait_ge(nf_done, KT * r + k + 1)
                    nc.scalar.activation(big1[:, 0, k, :], normed[k % 3], ACT.Copy).then_inc(nhi_done, 1)

            for k in range(KT):
                square(0, k, k % 2)
            norm(0)
            act.wait_ge(u_sb, 1)
            act.dma_start(u_s.rearrange("(g h) n -> h g n", g=NG), u_lines).then_inc(u_stored, 16)
            act.wait_ge(lam_dve, 1)
            nc.scalar.activation(lamt[:, 1, :], lamt[:, 0, :], ACT.Exp, scale=-1.0).then_inc(lam_act, 1)
            act.wait_ge(lam_dve, 2)
            nc.scalar.activation(lamt[:, 3, :], lamt[:, 2, :], ACT.Ln).then_inc(lam_act, 1)

            act.wait_ge(nlo_dve, KT - len(POOL_LOW))
            act.wait_ge(nlo_pool, len(POOL_LOW))
            act.sem_inc(gate_ev, 1)
            XC, GE, R, I, AD, M2, U, H = (tmp(n) for n in range(8))
            LX = ext[:, 0, :]

            def col(i, n):
                return par[:, ds(i, 1), n]

            def front(i):
                act.wait_ge(gate_mm, i * NCH + 1)
                for a, wn in enumerate(("w_rg_a", "w_rg_x")):
                    src = A[wn][0].rearrange("n i j -> (n i) j")
                    for h in range(2):
                        act.dma_start(bd[h * HD:(h + 1) * HD, a, h * HD:(h + 1) * HD],
                                      src[ds(i * P + h * HD, HD), :]).then_inc(bd_loaded, 16)
                act.wait_ge(unit_done[0], i + (T0["lru"] + 2))
                act.wait_ge(conv_done, i + 1)
                nc.scalar.activation(chunks(LX[:, 3:3 + NT]), ups_v[0], ACT.Copy).then_inc(ps_free[0], 1)
                act.wait_ge(ps_free[0], i + (T0["lru"] + 2))
                act.wait_ge(u_done, i + 1)
                apart(act)
                nc.scalar.activation(XC[:, 0:SEQ], LX[:, 0:SEQ], ACT.Identity, bias=col(i, 4), scale=col(i, 0))
                nc.scalar.activation(XC[:, SEQ:NT], LX[:, SEQ + 3:NT + 3], ACT.Identity, bias=col(i, 4), scale=col(i, 3)).then_inc(xc0_done, 1)

            def gate(i, c):
                act.wait_ge(gate_mm, i * NCH + (c + 2))
                apart(act)
                nc.scalar.activation(R[:, c * CH:(c + 1) * CH], aux[:, 0, 0:CH], ACT.Sigmoid, bias=col(i, 5))
                nc.scalar.activation(I[:, c * CH:(c + 1) * CH], aux[:, 1, 0:CH], ACT.Sigmoid, bias=col(i, 6)).then_inc(gate_ev, 1)

            def side(i):
                gate(i, 1)
                act.wait_ge(unit_done[1], i + (T0["lru"] + 2))
                act.wait_ge(z_done, i + 1)
                nc.scalar.activation(chunks(GE), ups_v[1], ACT.Gelu_apprx_tanh).then_inc(ps_free[1], 1)
                gate(i, 2)

            def decay(i):
                act.wait_ge(gate_ev, i * NCH + (NCH + 1))
                apart(act)
                step.step(nc.scalar.activation(AD, R, ACT.Exp, scale=cdec[:, 0, ds(i, 1)]))
                apart(act)
                nc.scalar.activation(R, R, ACT.Tanh, scale=cdec[:, 1, ds(i, 1)]).then_inc(ath_done, 1)
                act.wait_ge(m2_done, i + 1)
                nc.scalar.activation(M2, M2, ACT.Sqrt).then_inc(sqrt_done, 1)

            front(0)
            gate(0, 0)
            with act.Fori(1, KT) as i:
                step.loop(i, 1, 1)
                side(i - 1)
                front(i)
                decay(i - 1)
                gate(i, 0)
            step.end(KT - 1)
            side(KT - 1)
            decay(KT - 1)
            act.wait_ge(lru_done, KT)
            act.dma_start(O["lru_out"], sout[:]).then_inc(out_done, 16)
            act.dma_start(O["state_out"], stc[:]).then_inc(out_done, 16)
            act.wait_ge(u_stored, 16)
            act.dma_start(bt_s, bass.AP(tensor=u_s.tensor, offset=0, ap=[[UL, NG * HG], [1, P], [1, 2 * P]])).then_inc(bt_fill, 16)
            for j in range(2):
                act.sem_inc(qn_stored[j], 16)
                act.sem_inc(v_stored[j], 16)

            def evac(i, j):
                act.wait_ge(unit_done[j], i + (T0["qk"] + 2))
                act.wait_ge(qn_done[j], i + 1)
                nc.scalar.activation(chunks(tmp(j)), ups_v[j], ACT.Copy).then_inc(ps_free[j], 1)
                act.wait_ge(ps_free[j], i + (T0["qk"] + 2))
                nc.scalar.activation(tmp(2 + j)[:, 0:SEQ], tmp(j)[:, 0:SEQ], ACT.Square).then_inc(qsq_done[j], 1)
                nc.scalar.activation(sqkv[:, ds(i * 2 + j, 1), :], tmp(j)[:, SEQ:NT], ACT.Copy).then_inc(sqc_done, 1)

            def store(i, j):
                act.wait_ge(qn_done[j], i + 2)
                act.dma_start(qkv_s[ds(i * 2 + j, 1), :, :].rearrange("a p t -> p a t"), tmp(6 + j)[:, 0:SEQ]).then_inc(qn_stored[j], 16)

            def root(i, j):
                act.wait_ge(st_done[j], i + 1)
                act.wait_ge(qn_done[j], i + 1)
                nc.scalar.activation(tmp(4 + j)[:, 0:SEQ], aux[:].rearrange("p b n -> p (b n)"), ACT.Sqrt, scale=1.0 / HD, bias=epst[:])\
                    .then_inc(rt_done[j], 1)

            def qk(i, first):
                evac(i, 0)
                if not first:
                    root(i - 1, 1)
                    store(i - 1, 0)
                evac(i, 1)
                root(i, 0)
                if not first:
                    store(i - 1, 1)

            qk(0, True)
            with act.Fori(1, 12) as i:
                qk(i, False)
            root(11, 1)
            store(11, 0)
            store(11, 1)
            with act.Fori(0, 2) as i:
                for j in range(2):
                    act.wait_ge(unit_done[j], i + (T0["v"] + 2))
                    act.wait_ge(v_stored[j], i * 16 + 16)
                    nc.scalar.activation(chunks(tmp(j)), ups_v[j], ACT.Copy).then_inc(ps_free[j], 1)
                    act.wait_ge(ps_free[j], i + (T0["v"] + 2))
                    nc.scalar.activation(sqkv[:, ds(i * 2 + (24 + j), 1), :], tmp(j)[:, SEQ:NT], ACT.Copy).then_inc(sqc_done, 1)
                    act.dma_start(qkv_s[ds(i * 2 + (24 + j), 1), :, :].rearrange("a p t -> p a t"), tmp(j)[:, 0:SEQ]).then_inc(v_stored[j], 16)
            for j in range(2):
                act.wait_ge(v_stored[j], 16 * 3)
                act.wait_ge(qn_stored[j], 16 * 13)
            act.sem_inc(pt_ev, 2)
            act.sem_inc(au_ev, NCH)
            act.sem_inc(o_stored, 16)
            for j in range(2):
                act.sem_inc(g_stored[j], 16)
            for g in range(NG):
                with act.Fori(0, 4) as i:
                    def evac(n):
                        j, c = n // NCH, n % NCH
                        if c < NCH - 1:
                            act.wait_ge(au_mm, i * 4 + (16 * g + 2 * j + c + 1))
                        else:
                            act.wait_ge(unit_done[j], i + (T0[f"att{g}"] + 2))
                        if c == 0:
                            act.wait_ge(g_stored[j], i * 16 + (64 * g + 16))
                        apart(act)
                        to = GT[j][:, c * CH:(c + 1) * CH]
                        if g:
                            nc.scalar.activation(to, ups[:, 0, c, 0:CH], ACT.Tanh, scale=0.5,
                                                 bias=bmrg[:, ds(i * 2 + (8 * g - 8 + j), 1)]).then_inc(au_ev, 1)
                        else:
                            nc.scalar.activation(to, ups[:, 0, c, 0:CH], ACT.Copy).then_inc(au_ev, 1)
                        if c < NCH - 1:
                            return
                        act.wait_ge(au_ev, i * 6 + (24 * g + n + NCH + 1))
                        if g:
                            act.dma_start(gate_s[ds(i * 2 + (8 * g - 8 + j), 1)].rearrange("a p t -> p (a t)"), GT[j]).then_inc(g_stored[j], 16)
                        else:
                            nc.scalar.activation(sqkv[:, ds(i * 2 + (28 + j), 1), :], GT[j][:, SEQ:NT], ACT.Copy).then_inc(sqc_done, 1)
                            act.dma_start(qkv_s[ds(i * 2 + (28 + j), 1)].rearrange("a p t -> p (a t)"), GT[j][:, 0:SEQ]).then_inc(g_stored[j], 16)

                    act.wait_ge(vt_mm, i + (4 * g + 2))
                    act.wait_ge(pv_mm, i * 8 + (32 * g + 2))
                    for n in range(2):
                        ins = nc.scalar.activation(VTOK[:, 4 * n:4 * n + 4, :, 0:HD],
                                                   pt_bank[n].rearrange("p (b h e) -> p b h e", b=4, h=2), ACT.Copy)
                    ins.then_inc(vt_ev, 1)
                    for n in range(9):
                        if n >= 1:
                            q = n - 1
                            act.wait_ge(pt_mm, i * 8 + (32 * g + q + 3))
                            act.wait_ge(pv_mm, i * 8 + (32 * g + q + 1))
                            lo = 256 - P * nkeys(g, 2 * (q % 4))
                            if g < 2:
                                ins = nc.scalar.activation(PTS[q % 2][:, lo:512], pt_bank[q % 2][:, lo:512], ACT.Copy)
                            else:
                                ins = nc.scalar.activation(PTS[q % 2].rearrange("p (m c) -> p m c", m=2)[:, :, P:2 * P],
                                                           pt_bank[q % 2].rearrange("p (m c) -> p m c", m=2)[:, :, P:2 * P], ACT.Copy)
                            ins.then_inc(pt_ev, 1)
                        if n < 8:
                            act.wait_ge(nm_done, i * 8 + (32 * g + n + 1))
                            for m in range(2):
                                cols = slice(256 * m + 256 - P * nkeys(g, 2 * (n % 4) + m), 256 * m + 256)
                                ins = nc.scalar.activation(SB[n % 2][:, cols], SB[n % 2][:, cols], ACT.Exp,
                                                           bias=NM[:, 2 * (n % 2) + m:2 * (n % 2) + m + 1])
                            ins.then_inc(exp_done, 1)
                        if n in (0, 2, 4, 6, 8):
                            evac(n // 2)
                    evac(5)
                    act.wait_ge(o_ev, i * 8 + (32 * g + 9))
                    pair = o_s[g].rearrange("t (f h) e -> t f h e", h=2)[:, ds(i, 1)].rearrange("t a h e -> t (a h e)")
                    if g == 0:
                        act.dma_start(pair.rearrange("(b p) e -> p b e", p=P), OT.rearrange("p b h e -> p b (h e)")).then_inc(o_stored, 16)
                    elif g == 1:
                        for c in range(2):
                            act.dma_start(pair.rearrange("(c p r) e -> c p r e", c=2, r=4)[c],
                                          OT.rearrange("p (r c) h e -> p r c (h e)", c=2)[:, :, c]).then_inc(o_stored, 16)
                    else:
                        act.dma_start(pair.rearrange("(m b) e -> m b e", b=8), OT.rearrange("p b h e -> p b (h e)")).then_inc(o_stored, 16)
            for dst, src in sm_loads:
                act.dma_start(dst, src).then_inc(sm_ld, 16)

            def weigh(n):
                act.wait_ge(dm_done, n + 1)
                nc.scalar.activation(ce, ce, ACT.Exp).then_inc(ce_done, 1)

            def y_lru(n):
                i, j = n // 2, n % 2
                act.wait_ge(unit_done[j], T0["ylru"] + 2 + i)
                act.wait_ge(g_stored[j], 16 * (13 + i))
                nc.scalar.activation(chunks(GT[j]), ups_v[j], ACT.Copy).then_inc(ps_free[j], 1)
                act.wait_ge(ps_free[j], T0["ylru"] + 2 + i - 12)
                act.dma_start(gate_s[16 + n], GT[j]).then_inc(g_stored[j], 16)

            act.wait_ge(sm_pe, 1)
            nc.scalar.activation(rms, aux[:, 1, 0:192], ACT.Sqrt, scale=1.0 / HD, bias=epst[:]).then_inc(sm_act, 1)
            weigh(0)
            y_lru(0)
            act.wait_ge(sm_dve, 2)
            act.dma_start(O["sqkv"], sqkv[:]).then_inc(out_done, 16)
            for n in range(1, 4):
                weigh(n)
                y_lru(n)
            act.wait_ge(sm_max, 1)
            nc.scalar.activation(srow, srow, ACT.Exp, bias=sstat[:, 1:2], accum_out=sstat[:, 2:3]).then_inc(sm_act, 1)
            for n in range(4, 8):
                weigh(n)
                y_lru(n)

            with act.Fori(0, 4) as i:
                for j in range(2):
                    act.wait_ge(mrg_sum[j], i + 2)
                    apart(act)
                    nc.scalar.activation(big2[:, 0, ds(i * 2 + j, 1), :], ext[:, 1 + j, 0:NT], ACT.Copy, scale=0.5).then_inc(mrg_hi[j], 1)
            with act.Fori(0, 4) as i:
                for j in range(2):
                    square(1, i * 2 + j, j)
            norm(1)
            for n, (f0, nf) in enumerate(PARTS):
                with act.Fori(0, nf) as i:
                    act.wait_ge(unit_done[0], i + (T0[f"up{n}"] + 2))
                    act.wait_ge(sg_free, i + (f0 + 1))
                    nc.scalar.activation(chunks(ext[:, 0, 0:NT]), ups_v[0], ACT.Silu).then_inc(ps_free[0], 1)
            with act.Fori(0, 4) as i:
                for j in range(2):
                    act.wait_ge(ps_free[j], i + (T0["down2"] + 2 - 12))
                    act.dma_start(O["y_T"][ds(i * 2 + j, 1)].rearrange("a p t -> p (a t)"), x1[:, ds(i * 2 + j, 1), :].rearrange("p a t -> p (a t)"))\
                        .then_inc(y_stored, 16)
            act.wait_ge(y_stored, 16 * KT)
            act.wait_ge(out_done, 48)
            act.wait_ge(o_stored, O_STORES)
            for j in range(2):
                act.wait_ge(g_stored[j], 16 * 17)


        @block.vector
        def _(dve):
            step = Chain(dve, s_dve)
            nc.vector.memset(epst[:], EPS)
            nc.vector.memset(ones[:], 1.0).then_inc(ones_done, 1)

            def norm_add(k, r, at):
                dve.wait_ge(nsq_done, k + 1)
                dve.wait_ge(nadd_done, k + (r + 1))
                nc.vector.tensor_tensor(sums, sums, ext[:, 1 + at, 0:NT], ALU.add).then_inc(nadd_done, 1)

            def norm(r, gain):
                def low(k):
                    if k in POOL_LOW:
                        return
                    dve.wait_ge(nhi_done, KT * r + k + 1)
                    nc.vector.tensor_tensor(big1[:, 1, k, :], normed[k % 3], big1[:, 0, k, :].bitcast(F32), ALU.subtract).then_inc(nlo_dve, 1)

                dve.wait_ge(nrt_done, r + 1)
                step.step(nc.vector.reciprocal(rrms, rrms))
                for k in range(KT):
                    if k >= 3:
                        tile_split(dve, r, k - 3)
                    nc.vector.scalar_tensor_tensor(normed[k % 3], tmp(k), gain[:, k:k + 1], rrms, ALU.mult, ALU.mult).then_inc(nf_done, 1)
                    if k >= 1:
                        low(k - 1)
                low(KT - 1)

            nc.vector.memset(sums, 0.0).then_inc(nadd_done, 1)
            for k in range(KT):
                norm_add(k, 0, k % 2)
            dve.wait_ge(const_ld, CONSTS)
            norm(0, gmix)
            dve.wait_ge(u_ps, 1)
            nc.vector.tensor_copy(u_lines, ups[0:HG, 1, :, 0:UL]).then_inc(u_sb, 1)
            for c in range(2):
                nc.vector.tensor_copy(gqk[:, 6 * c:6 * c + 6], gq2[:, c:c + 1].broadcast_to([P, 6]))
            step.step(nc.vector.tensor_scalar(bmrg[:], bmrg[:], 0.5, None, ALU.mult))
            lam = par[:, :, 7]
            step.step(nc.vector.tensor_scalar(lamt[:, 0, :], lam, -1.0, None, ALU.mult))
            nc.vector.tensor_tensor(lamt[:, 0, :], lamt[:, 0, :], lam, ALU.max).then_inc(lam_dve, 1)
            dve.wait_ge(lam_act, 1)
            nc.vector.tensor_scalar(lamt[:, 2, :], lamt[:, 1, :], 1.0, None, ALU.add).then_inc(lam_dve, 1)
            dve.wait_ge(lam_act, 2)
            step.step(nc.vector.tensor_scalar(lamt[:, 2, :], lamt[:, 2, :], -1.0, None, ALU.add))
            step.step(nc.vector.tensor_scalar(cdec[:, 0, :], lamt[:, 2, :], 0.0, None, ALU.is_equal))
            step.step(nc.vector.tensor_tensor(lamt[:, 2, :], lamt[:, 2, :], cdec[:, 0, :], ALU.add))
            step.step(nc.vector.tensor_tensor(lamt[:, 3, :], lamt[:, 3, :], cdec[:, 0, :], ALU.add))
            step.step(nc.vector.reciprocal(lamt[:, 2, :], lamt[:, 2, :]))
            step.step(nc.vector.tensor_tensor(lamt[:, 3, :], lamt[:, 3, :], lamt[:, 2, :], ALU.mult))
            step.step(nc.vector.tensor_tensor(lamt[:, 3, :], lamt[:, 3, :], lamt[:, 1, :], ALU.mult))
            step.step(nc.vector.tensor_scalar(lamt[:, 0, :], lam, -1.0, 0.0, ALU.mult, ALU.max))
            step.step(nc.vector.tensor_tensor(lamt[:, 3, :], lamt[:, 3, :], lamt[:, 0, :], ALU.add))
            step.step(nc.vector.tensor_scalar(cdec[:, 0, :], lamt[:, 3, :], -8.0, None, ALU.mult))
            step.step(nc.vector.tensor_scalar(cdec[:, 1, :], lamt[:, 3, :], 8.0, None, ALU.mult))
            dve.wait_ge(nlo_pool, len(POOL_LOW))
            dve.wait_ge(u_stored, 16)
            step.step(nc.vector.memset(ext[:, 0, 0:3], 0.0))

            for s in (ps_free[0], ps_free[1], conv_done, u_done, z_done):
                dve.sem_inc(s, 1)
            XC, GE, R, I, AD, M2, U, H = (tmp(n) for n in range(8))
            LX, GI = ext[:, 0, :], ext[:, 1, 0:NT]

            def gated(i):
                dve.wait_ge(gate_ev, i * NCH + (NCH + 1))
                nc.vector.tensor_tensor(GI, I, XC, ALU.mult).then_inc(u_done, 1)

            def conv(i):
                dve.wait_ge(xc0_done, i + 1)
                for k in range(1, 4):
                    step.step(nc.vector.scalar_tensor_tensor(XC[:, 0:SEQ], LX[:, k:k + SEQ], par[:, ds(i, 1), k], XC[:, 0:SEQ], ALU.mult, ALU.add))
                for k in range(3):
                    prev = stc[:, ds(i, 1), 0:3 * NB].rearrange("p a (b c) -> p a b c", c=3)[:, :, :, k]
                    ins = nc.vector.scalar_tensor_tensor(XC[:, SEQ:NT], prev, par[:, ds(i, 1), k], XC[:, SEQ:NT], ALU.mult, ALU.add)
                    if k < 2:
                        step.step(ins)
                ins.then_inc(xc_done, 1)
                nc.vector.tensor_copy(sout[:, ds(i, 1), 0:11], LX[:, SEQ:SEQ + 11]).then_inc(conv_done, 1)

            def recur(i):
                dve.wait_ge(ath_done, i + 1)
                step.step(nc.vector.tensor_tensor(M2, AD, AD, ALU.mult))
                nc.vector.scalar_tensor_tensor(M2, M2, 1.0, R, ALU.add, ALU.mult).then_inc(m2_done, 1)
                dve.wait_ge(sqrt_done, i + 1)
                step.step(nc.vector.memset(M2[:, 0:1], 1.0))
                dve.wait_ge(u_done, i + 2)
                step.step(nc.vector.tensor_tensor(U, M2, GI, ALU.mult))
                step.step(nc.vector.tensor_tensor_scan(H[:, 0:SEQ], AD[:, 0:SEQ], U[:, 0:SEQ], 0.0, ALU.mult, ALU.add))
                step.step(nc.vector.tensor_tensor(H[:, SEQ:NT], AD[:, SEQ:NT], stc[:, ds(i, 1), 3 * NB:4 * NB], ALU.mult))
                step.step(nc.vector.tensor_tensor(H[:, SEQ:NT], H[:, SEQ:NT], U[:, SEQ:NT], ALU.add))
                nc.vector.tensor_copy(sout[:, ds(i, 1), 11:20], H[:, SEQ - 1:NT])
                step.step(nc.vector.tensor_tensor(U, H, GE, ALU.mult))
                dve.sem_inc(z_done, 1)
                step.step(nc.vector.tensor_copy(big2[:, 0, ds(i, 1), :], U))
                step.step(nc.vector.tensor_tensor(big2[:, 1, ds(i, 1), :], U, big2[:, 0, ds(i, 1), :].bitcast(F32), ALU.subtract))
                dve.sem_inc(lru_done, 1)

            conv(0)
            with dve.Fori(1, KT) as i:
                step.loop(i, 14, 1)
                gated(i - 1)
                conv(i)
                recur(i - 1)
            step.end(KT - 1)
            gated(KT - 1)
            recur(KT - 1)

            for j in range(2):
                dve.sem_inc(qn_done[j], 1)
            with dve.Fori(0, 12) as i:
                step.loop(i, 2)
                for j in range(2):
                    rms_t = tmp(4 + j)[:, 0:SEQ]
                    dve.wait_ge(rt_done[j], i + (1 + j))
                    step.step(nc.vector.reciprocal(rms_t, rms_t))
                    dve.wait_ge(qn_stored[j], i * 16 + 16)
                    nc.vector.scalar_tensor_tensor(tmp(6 + j)[:, 0:SEQ], tmp(j)[:, 0:SEQ], gqk[:, ds(i, 1)],
                                                   rms_t, ALU.mult, ALU.mult).then_inc(qn_done[j], 1)
            step.end(12)

            dve.wait_ge(sqc_done, 28)
            dve.wait_ge(qn_stored[0], 16 * 13)
            nc.vector.memset(VTOK[:, :, :, HD:HD + 1], 1.0)
            for s, n in ((sa_done, 2), (pt_mm, 2), (pv_mm, 2), (o_ev, 1)):
                dve.sem_inc(s, n)
            stores = 1
            for g in range(NG):
                per = 2 if g == 1 else 1
                with dve.Fori(0, 4) as i:
                    dve.wait_ge(qk_ld, i * 48 + 48 * (4 * g + 1))
                    dve.wait_ge(o_stored, i * (16 * per) + 16 * stores)
                    step.loop(i, 8)
                    for n in range(10):
                        if n < 8:
                            hh, bp = n // 4, n % 4
                            dve.wait_ge(s_mm, i * 8 + (32 * g + n + 1))
                            dve.wait_ge(pt_mm, i * 8 + (32 * g + n + 1))
                            for m in range(2):
                                nk = nkeys(g, 2 * bp + m)
                                cols = slice(256 * m + 256 - P * nk, 256 * m + 256)
                                ins = nc.vector.scalar_tensor_tensor(SB[n % 2][:, cols], s_bank[n % 2][:, cols], SCALE,
                                                                     BT[:, hh, 0:P * nk][:, ::-1], ALU.mult, ALU.add)
                            ins.then_inc(sa_done, 1)
                            dve.wait_ge(sa_done, i * 8 + (32 * g + n + 3))
                            for m in range(2):
                                cols = slice(256 * m + 256 - P * nkeys(g, 2 * bp + m), 256 * m + 256)
                                ins = nc.vector.tensor_reduce(OT[:, 2 * bp + m, hh, HD + 1:HD + 2], SB[n % 2][:, cols], AX_X, ALU.max)
                            step.step(ins)
                            ins = nc.vector.tensor_scalar(NM[:, 2 * (n % 2):2 * (n % 2) + 2], OT[:, 2 * bp:2 * bp + 2, hh, HD + 1],
                                                          -1.0, None, ALU.mult).then_inc(nm_done, 1)
                        if n >= 2:
                            q = n - 2
                            hh, bp = q // 4, q % 4
                            dve.wait_ge(pv_mm, i * 8 + (32 * g + q + 3))
                            ins = nc.vector.tensor_copy(OT[:, 2 * bp:2 * bp + 2, hh, 0:HD + 1],
                                                        o_bank[:, 0:2 * (HD + 1)].rearrange("p (m e) -> p m e", m=2)).then_inc(o_ev, 1)
                step.end(4)
                stores += 4 * per

            def s_squares():
                dve.wait_ge(sqc_done, 36)
                nc.vector.tensor_tensor(sqs, sqkv[:, 0:24, :].rearrange("p f b -> p (f b)"), sqkv[:, 0:24, :].rearrange("p f b -> p (f b)"),
                                        ALU.mult).then_inc(sm_dve, 1)

            def s_norm():
                dve.wait_ge(sm_ld, SM_LD)
                dve.wait_ge(sm_pe, 2)
                nc.vector.tensor_copy(sbias, aux[0:ROWS, 1, 0:387])
                step.step(nc.vector.reciprocal(rms, rms))
                for c in range(2):
                    own = sqkv[:, 12 * c:12 * c + 12, :].rearrange("p f b -> p (f b)")
                    step.step(nc.vector.scalar_tensor_tensor(own, own, gqk[:, 6 * c:6 * c + 1], rms[:, 96 * c:96 * c + 96], ALU.mult, ALU.mult))
                qmv = qm.rearrange("p (f b h) -> p f b h", b=NB, h=2)
                for h in range(2):
                    step.step(nc.vector.tensor_scalar(qmv[:, :, :, h], sqkv[:, 0:12, :], hsel[:, h:h + 1], None, ALU.mult))
                nc.vector.tensor_tensor(pm.rearrange("p (f b h) -> p f b h", b=NB, h=2), qmv,
                                        sqkv[:, 12:24, :].unsqueeze(3).broadcast_to([P, 12, NB, 2]), ALU.mult).then_inc(sm_dve, 1)

            def s_scores():
                dve.wait_ge(kv_used[0], 2)
                nc.vector.tensor_copy(sqs[:, 0:128], aux[:, 1, 0:128])
                nc.vector.tensor_copy(sqs[0:64, 128:192], aux[0:64, 1, 128:192]).then_inc(sm_dve, 1)

            def s_bias():
                dve.wait_ge(sm_pe, 3)
                for g in range(NG):
                    n, skip = NKEY[g], 2 if g == 2 else 1
                    nc.vector.scalar_tensor_tensor(srow[:, g * P:g * P + n], aux[0:ROWS, 1, g * P:g * P + n], SCALE,
                                                   sbias[:, 129 * g + skip:129 * g + n * skip + 1:skip][:, ::-1], ALU.mult, ALU.add)
                step.step(nc.vector.scalar_tensor_tensor(srow[:, 320:323], aux[0:ROWS, 1, 400:403], SCALE,
                                                         sbias.rearrange("p (g n) -> p g n", g=NG)[:, :, 0], ALU.mult, ALU.add))
                step.step(nc.vector.tensor_reduce(sstat[:, 0:1], srow, AX_X, ALU.max))
                nc.vector.tensor_scalar(sstat[:, 1:2], sstat[:, 0:1], -1.0, None, ALU.mult).then_inc(sm_max, 1)

            def s_probs():
                dve.wait_ge(sm_act, 2)
                step.step(nc.vector.reciprocal(sstat[:, 3:4], sstat[:, 2:3]))
                step.step(nc.vector.tensor_scalar(srow, srow, sstat[:, 3:4], None, ALU.mult))
                for g in range(NG):
                    ins = nc.vector.tensor_scalar(r3[:, 32 * g:32 * g + 32], dsel, srow[:, 320 + g:321 + g], None, ALU.mult)
                ins.then_inc(sm_dve, 1)

            def s_own():
                dve.wait_ge(sm_pe, 4)
                step.step(nc.vector.tensor_tensor(rms[:, 0:96], aux[:, 1, 192:288], sqkv[:, 24:36, :].rearrange("p f b -> p (f b)"), ALU.mult))
                nc.vector.tensor_copy(pts[:, 0:128], aux[:, 1, 0:128])
                nc.vector.tensor_copy(pts[0:64, 128:192], aux[0:64, 1, 128:192]).then_inc(sm_dve, 1)
                step.step(nc.vector.tensor_tensor(osum, rms[:, 0:32], rms[:, 32:64], ALU.add))
                step.step(nc.vector.tensor_tensor(osum, osum, rms[:, 64:96], ALU.add))

            def s_output():
                dve.wait_ge(kv_used[1], 3)
                dve.wait_ge(out_done, 48)
                for h in range(2):
                    hr = slice(h * HD, (h + 1) * HD)
                    ins = nc.vector.tensor_tensor(osam[hr], osum.rearrange("p (f b) -> p f b", f=4)[hr],
                                                  aux[hr, 1, 448:512].rearrange("p (f b h) -> p f b h", f=4, h=2)[:, :, :, h], ALU.add)
                step.step(ins)
                hi, lo = (big1[:, a, 0:4, SEQ:NT] for a in range(2))
                step.step(nc.vector.tensor_copy(hi, osam))
                nc.vector.tensor_tensor(lo, osam, hi.bitcast(F32), ALU.subtract).then_inc(ot_done, 1)

            def split_turned(n):
                dve.wait_ge(ot_mm, n + 1)
                hi, lo = (big1[:, a, 0:4, n * P:(n + 1) * P] for a in range(2))
                src = aux[:, 0, :].rearrange("p (k t) -> p k t", k=4)
                step.step(nc.vector.tensor_copy(hi, src))
                nc.vector.tensor_tensor(lo, src, hi.bitcast(F32), ALU.subtract).then_inc(ot_done, 1)

            def combine(n):
                o = OL[n % 2]
                dve.wait_ge(ol_ld[n % 2], 16 * (n // 2 + 1))
                mx = [o[:, g, :, HD + 1] for g in range(NG)]
                step.step(nc.vector.tensor_tensor(mt, mx[0], mx[1], ALU.max))
                step.step(nc.vector.tensor_tensor(mt, mt, mx[2], ALU.max))
                nc.vector.tensor_tensor(ce, o[:, :, :, HD + 1], mt.unsqueeze(1).broadcast_to([P, NG, HG]), ALU.subtract).then_inc(dm_done, 1)
                dve.wait_ge(ce_done, n + 1)
                step.step(nc.vector.tensor_tensor(cl, ce, o[:, :, :, HD], ALU.mult))
                step.step(nc.vector.tensor_tensor(den, cl[:, 0], cl[:, 1], ALU.add))
                step.step(nc.vector.tensor_tensor(den, den, cl[:, 2], ALU.add))
                step.step(nc.vector.reciprocal(den, den))
                step.step(nc.vector.tensor_tensor(cc, ce, den.unsqueeze(1).broadcast_to([P, NG, HG]), ALU.mult))
                if n:
                    split_turned(n - 1)
                for g in range(NG):
                    cb = cc[:, g].unsqueeze(2).broadcast_to([P, HG, HD])
                    if g == 0:
                        step.step(nc.vector.tensor_tensor(oacc, o[:, g, :, 0:HD], cb, ALU.mult))
                    else:
                        step.step(nc.vector.tensor_tensor(oprod, o[:, g, :, 0:HD], cb, ALU.mult))
                        if g == 1:
                            step.step(nc.vector.tensor_tensor(oacc, oacc, oprod, ALU.add))
                        else:
                            dve.sem_inc(cb_free[n % 2], 1)
                            nc.vector.tensor_tensor(oacc, oacc, oprod, ALU.add).then_inc(on_done, 1)

            s_squares()
            for j in range(2):
                dve.wait_ge(unit_done[j], T0["ylru"] + 1)
            combine(0)
            s_norm()
            combine(1)
            combine(2)
            s_scores()
            combine(3)
            s_bias()
            combine(4)
            s_probs()
            combine(5)
            s_own()
            combine(6)
            combine(7)
            s_output()
            split_turned(7)

            dve.wait_ge(ot_done, 9)
            for s in (*mrg_sum, *xr_free, sg_free):
                dve.sem_inc(s, 1)
            with dve.Fori(0, 4) as i:
                step.loop(i, 4)
                for j in range(2):
                    gl, ga, yl, both = *(tmp(3 * j + n) for n in range(3)), ext[:, 1 + j, 0:NT]
                    dve.wait_ge(side_ld[j], i * 48 + 48)
                    step.step(nc.vector.scalar_tensor_tensor(gl, gl, 1.0, yl, ALU.add, ALU.mult))
                    dve.wait_ge(unit_done[j], i + (T0["merge"] + 2))
                    step.step(nc.vector.scalar_tensor_tensor(chunks(ga), chunks(ga), 1.0, ups_v[j], ALU.add, ALU.mult))
                    dve.sem_inc(ps_free[j], 1)
                    nc.vector.tensor_tensor(both, gl, ga, ALU.add).then_inc(mrg_sum[j], 1)
                    dve.wait_ge(mrg_hi[j], i + 1)
                    nc.vector.scalar_tensor_tensor(big2[:, 1, ds(i * 2 + j, 1), :], both, 0.5, big2[:, 0, ds(i * 2 + j, 1), :].bitcast(F32),
                                                   ALU.mult, ALU.subtract).then_inc(mrg_done[j], 1)
            step.end(4)
            nc.vector.memset(sums, 0.0).then_inc(nadd_done, 1)
            with dve.Fori(0, 4) as i:
                for j in range(2):
                    dve.wait_ge(xr_ld[j], i * 16 + 16)
                    dve.wait_ge(unit_done[j], i + (T0["wo"] + 2))
                    apart(dve)
                    nc.vector.tensor_tensor(x1[:, ds(i * 2 + j, 1), :].rearrange("p a (c n) -> p (a c) n", c=NCH), ups_v[j],
                                            chunks(ext[:, 3 * j, 0:NT]), ALU.add).then_inc(wo_done, 1)
                    dve.wait_ge(wo_done, i * 2 + (j + 1))
                    dve.sem_inc(ps_free[j], 1)
                    dve.sem_inc(xr_free[j], 1)
                    norm_add(i * 2 + (j + KT), 1, j)
            norm(1, gffn)
            for n, (f0, nf) in enumerate(PARTS):
                if n:
                    for j in range(2):
                        dve.wait_ge(unit_done[j], T0[f"up{n}"] + 1)
                with dve.Fori(0, nf) as i:
                    step.loop(i, 3)
                    dve.wait_ge(ps_free[0], i + (T0[f"up{n}"] + 2 - 12))
                    dve.wait_ge(unit_done[1], i + (T0[f"up{n}"] + 2))
                    step.step(nc.vector.tensor_tensor(chunks(ext[:, 1, 0:NT]), chunks(ext[:, 0, 0:NT]), ups_v[1], ALU.mult))
                    dve.sem_inc(ps_free[1], 1)
                    dve.sem_inc(sg_free, 1)
                    step.step(nc.vector.tensor_copy(big2[:, 0, ds(i, 1), :], ext[:, 1, 0:NT]))
                    step.step(nc.vector.tensor_tensor(big2[:, 1, ds(i, 1), :], ext[:, 1, 0:NT], big2[:, 0, ds(i, 1), :].bitcast(F32), ALU.subtract))
                    dve.sem_inc(h_done, 1)
                step.end(nf)
                with dve.Fori(0, 4) as i:
                    for j in range(2):
                        dve.wait_ge(unit_done[j], i + (T0[f"down{n}"] + 2))
                        own = x1[:, ds(i * 2 + j, 1), :].rearrange("p a (c n) -> p (a c) n", c=NCH)
                        apart(dve)
                        nc.vector.tensor_tensor(own, ups_v[j], own, ALU.add).then_inc(ps_free[j], 1)



_IN = ["x_prompt", "x_sample", "cache_kv_g0", "cache_kv_g1", "cache_kv_g2", "state_conv", "state_h", "rel_bias", "norm_mix",
       "w_in", "w_conv", "b_conv", "w_rg_a", "b_rg_a", "w_rg_x", "b_rg_x", "lru_lambda", "q_gain", "k_gain", "w_merge",
       "b_merge", "w_branch_lru", "w_branch_att", "w_o", "norm_ffn", "w_ffn_in", "w_ffn_out"]
_OUT = [("y_T", (KT, P, NT)), ("qkv", (36, P, SEQ)), ("sqkv", (P, 36, NB)), ("lru_out", (P, KT, 20)), ("state_out", (P, KT, 4 * NB))]


def kernel(**inputs):
    import concourse.bacc as bacc
    from concourse.bass_utils import run_bass_kernel_spmd as run

    nc = bacc.Bacc("TRN2", target_bir_lowering=False, num_devices=1)
    a = {name: np.ascontiguousarray(inputs[name]) for name in _IN}

    def tiles(v):
        return np.ascontiguousarray(v.reshape(-1, KT, P).transpose(2, 1, 0))

    def weights(w):
        k, n = w.shape
        return np.ascontiguousarray(w.reshape(k // P, P, n // P, P).transpose(2, 1, 0, 3))

    hsel = np.zeros((P, 2), np.float32)
    hsel[:HD, 0] = hsel[HD:, 1] = 1.0
    arrays = dict(c_ident=np.eye(P, dtype=np.float32), c_hsel=hsel, c_one=np.ones((1, NG * HG), np.float32),
                  c_bones=np.kron(np.eye(2, dtype=np.float32), np.ones((HD, HD), np.float32)), c_lines=bucket_lines(),
                  rel_bias=a["rel_bias"], w_rg_a=a["w_rg_a"], w_rg_x=a["w_rg_x"])
    for n in ("w_in", "w_merge", "w_branch_lru", "w_branch_att", "w_o", "w_ffn_in", "w_ffn_out"):
        arrays[n] = weights(a[n][0])
    x = np.concatenate([a["x_prompt"][0], a["x_sample"][:, 0]])
    arrays["x_T"] = np.ascontiguousarray(x.T.reshape(KT, P, NT))
    arrays["c_par"] = tiles(np.concatenate([a["w_conv"][0], a["b_conv"], a["b_rg_a"], a["b_rg_x"], a["lru_lambda"]]))
    arrays["c_state"] = tiles(np.concatenate([a["state_conv"][0].reshape(-1, D), a["state_h"][0]]))
    arrays["c_gains"] = np.ascontiguousarray(np.stack([np.tile(a[n][0], 2) for n in ("q_gain", "k_gain")], axis=1))
    for n in ("norm_mix", "norm_ffn"):
        arrays["c_" + n] = tiles(a[n])[:, :, 0].copy()
    arrays["c_b_merge"] = np.ascontiguousarray(a["b_merge"].reshape(16, P).T)
    for g in range(NG):
        kv = a[f"cache_kv_g{g}"][0, :, ::DIL[g]]
        n = kv.shape[1]
        assert n == NKEY[g]
        arrays[f"kc{g}"] = np.ascontiguousarray(kv[:, :, 0].reshape(NB, n, 4, P).transpose(3, 0, 2, 1))
        arrays[f"vc{g}"] = np.ascontiguousarray(kv[:, :, 1].reshape(NB, n, 512).transpose(1, 0, 2))
    row = np.arange(NB * HG)
    arrays["c_hm"] = (row[:, None] % 2 == np.arange(P)[None] // HD).astype(np.float32)
    arrays["c_dsel"] = (row[:, None] // 2 == np.arange(32)[None]).astype(np.float32)
    arrays["c_rsel"] = (np.arange(HG)[:, None] == (2 * (row // 16) + row % 2)[None]).astype(np.float32)
    A = {n: nc.dram_tensor(n, v.shape, F32, kind="ExternalInput").ap() for n, v in arrays.items()}
    O = {n: nc.dram_tensor("out_" + n, shape, F32, kind="ExternalOutput").ap() for n, shape in _OUT}
    build(nc, A, O)
    r = run(nc, [arrays], core_ids=[0]).results[0]
    y = r["out_y_T"].reshape(D, NT).T
    qkv = r["out_qkv"].reshape(3, NG, HG * HD, SEQ)[1:].transpose(1, 3, 0, 2).reshape(NG, SEQ, 2, HG, HD)
    sqkv = r["out_sqkv"].transpose(1, 0, 2).reshape(3, NG, HG * HD, NB)[1:].transpose(1, 3, 0, 2).reshape(NG, NB, 2, HG, HD)
    lru = r["out_lru_out"].transpose(2, 1, 0).reshape(20, D)
    state = r["out_state_out"].transpose(2, 1, 0).reshape(4 * NB, D)[:3 * NB].reshape(NB, 3, D)
    conv_s = np.concatenate([state[:, 1:], lru[3:11, None]], axis=1)[None]
    return (y[None, :SEQ].copy(), y[SEQ:, None].copy(), *(qkv[g, None, None, SEQ - n:].copy() for g, n in enumerate((128, 512, 1024))),
            lru[None, None, 0:3].copy(), lru[None, 11:12].copy(), *(sqkv[g, None, :, None].copy() for g in range(NG)),
            conv_s, lru[None, 12:20].copy())
```

```python
import math
from contextlib import ExitStack
from functools import partial

import numpy as np

import concourse.bass as bass
from concourse import mybir

F32 = mybir.dt.float32
F32R = mybir.dt.float32r
ALU = mybir.AluOpType
ACT = mybir.ActivationFunctionType
AX_X = mybir.AxisListType.X
ds = bass.ds

P = 128
D = 1024
SEQ = 1024
NB = 8
NT = SEQ + NB
NCH = 3
CH = NT // NCH
KT = D // P
HD = 64
HG = 8
NG = 3
DIL = (1, 4, 16)
NKEY = (128, 128, 64)
DFF = 2816
FT = DFF // P
PARTS = ((0, 8), (8, 8), (16, 6))
EPS = 1e-6
NEG = -1e30
SCALE = HD ** -0.5
NBK = 32
UL = 384


def bucket_lines():
    out = np.zeros((NG, NBK + 1, UL), np.float32)
    out[:, NBK] = NEG
    for g in range(NG):
        skip = 2 if g == 2 else 1
        at = np.arange(127, 256, skip)
        dist = np.arange(len(at)) * DIL[g]
        d_f = np.maximum(dist, 1).astype(np.float32)
        large = 16 + (np.log(d_f / np.float32(16)) / np.float32(math.log(2048 / 16)) * np.float32(16)).astype(np.int32)
        bucket = np.where(dist < 16, dist, np.minimum(large, NBK - 1))
        out[g, NBK, at] = 0.0
        out[g, bucket, at] = 1.0
    return out


class Chain:

    def __init__(self, eng, sem):
        self.eng, self.sem, self.base, self.n, self.i, self.per = eng, sem, 0, 0, 0, 0

    def loop(self, i, per, first=0):
        self.base += self.n - first * per
        self.i, self.per, self.n, self.first = i, per, 0, first

    def end(self, iterations):
        assert self.n == self.per, (self.n, self.per)
        self.base += self.per * (iterations + self.first)
        self.i = self.per = self.n = 0

    def step(self, ins):
        self.n += 1
        ins.then_inc(self.sem, 1)
        self.eng.wait_ge(self.sem, self.i * self.per + (self.base + self.n) if self.per else self.base + self.n)


def build(nc, A, O):
    with ExitStack() as ctx:
        def sb(name, shape, dt=F32):
            return ctx.enter_context(nc.sbuf_tensor(name, shape, dt))

        def sem(name):
            return ctx.enter_context(nc.semaphore(name))

        def dram(name, shape):
            return nc.dram_tensor(name, shape, F32, kind="Internal").ap()

        with nc.sbuf_tensor("big1_f32", [P, 2, KT, NT], F32) as big1_f32:
            pass
        big1 = sb("big1", [P, 2, KT, NT], F32R)
        big2 = sb("big2", [P, 2, KT, NT], F32R)
        x1 = sb("x1", [P, KT, NT])
        wraw = sb("wraw", [P, 2, KT, P])
        wsp = sb("wsp", [P, 2, 2, KT, P], F32R)
        with nc.sbuf_tensor("ext_r", [P, 4, NT + 3], F32R) as ext_r:
            pass
        ext = sb("ext", [P, 4, NT + 3])
        ident = sb("ident", [P, P])
        hsel = sb("hsel", [P, 2])
        ones = sb("ones", [P, P])
        par = sb("par", [P, KT, 8])
        cdec = sb("cdec", [P, 2, KT])
        gmix = sb("gmix", [P, KT])
        gffn = sb("gffn", [P, KT])
        bones = sb("bones", [P, P])
        bones_r = sb("bones_r", [P, P], F32R)
        gq2 = sb("gq2", [P, 2])
        gqk = sb("gqk", [P, 12])
        bmrg = sb("bmrg", [P, 16])
        bd = sb("bd", [P, 2, P])
        sqkv = sb("sqkv", [P, 36, NB])
        stc = sb("stc", [P, KT, 4 * NB])
        sout = sb("sout", [P, KT, 20])
        lamt = sout.rearrange("p a n -> p (a n)")[:, 0:4 * KT].rearrange("p (a n) -> p a n", a=4)
        st = sb("st", [P, 4])
        epst = sb("epst", [P, 1])
        lines, relx = (ext[0:NBK + 1, 2:4, :].rearrange("p a n -> p (a n)")[:, c] for c in
                       (slice(0, NG * UL), slice(NG * UL, NG * UL + NG * HG)))
        u_lines = ext[0:HG, 0:2, :].rearrange("p a n -> p (a n)")[:, 0:NG * UL].rearrange("p (g n) -> p g n", g=NG)
        sums, rrms = big1_f32[:, 1, KT - 1, :], ext[:, 0, 0:NT]
        normed = [ext[:, 1 + n, 0:NT] for n in range(3)]
        POOL_LOW = (1, 4, 7)

        sq_parts = [ext_r[:, a, 0:SEQ] for a in range(2)]

        def tmp(n):
            return x1[:, n, :]

        ups = ctx.enter_context(nc.psum_tensor("ups", [P, 2, NCH, 512], F32))
        aux = ctx.enter_context(nc.psum_tensor("aux", [P, 2, 512], F32))

        qkv_s = O["qkv"]
        gate_s = dram("gate_s", [16, P, NT])
        o_s = dram("o_s", [NG, SEQ, HG, HD + 2])
        u_s = dram("u_s", [NG * HG, UL])
        bt_s = dram("bt_s", [NG * HG, P, 2 * P])

        stream = [
            ("lru", 8, KT, A["w_in"], 0, 8, 1, 0),
            ("qk", 12, KT, A["w_in"], 16, 17, 2, 0),
            ("v", 2, KT, A["w_in"], 40, 41, 2, 0),
            ("att0", 4, KT, A["w_in"], 44, 45, 2, 0),
            ("att1", 4, KT, A["w_merge"], 0, 1, 2, 0),
            ("att2", 4, KT, A["w_merge"], 8, 9, 2, 0),
            ("ylru", 4, KT, A["w_branch_lru"], 0, 1, 2, 0),
            ("merge", 4, 4, A["w_branch_att"], 0, 1, 2, 0),
            ("wo", 4, KT, A["w_o"], 0, 1, 2, 0),
        ]
        for n, (f0, nf) in enumerate(PARTS):
            stream.append((f"up{n}", nf, KT, A["w_ffn_in"], f0, FT + f0, 1, 0))
            stream.append((f"down{n}", 4, nf, A["w_ffn_out"], 0, 1, 2, f0))
        T0, t = {}, 0
        for s in stream:
            T0[s[0]] = t
            t += s[1]

        def two(name):
            return [sem(f"{name}{j}") for j in range(2)]

        w_loaded, w_split, unit_done, ps_free = two("w_loaded"), two("w_split"), two("unit_done"), two("ps_free")
        w_hi, ticks = sem("w_hi"), sem("ticks")
        s_dve, s_act = sem("s_dve"), sem("s_act")
        const_ld = sem("const_ld")
        bd_zero = sem("bd_zero")
        x_loaded = [sem(f"x_loaded{k}") for k in range(KT)]
        ones_done, nsq_done, nadd_done, nst_mm, nrt_done = (sem(n) for n in ("ones_done", "nsq_done", "nadd_done", "nst_mm", "nrt_done"))
        nf_done, nhi_done, nlo_dve, nlo_pool = sem("nf_done"), sem("nhi_done"), sem("nlo_dve"), sem("nlo_pool")
        lines_ld, u_ps, u_sb, u_stored = sem("lines_ld"), sem("u_ps"), sem("u_sb"), sem("u_stored")
        lam_act, lam_dve = sem("lam_act"), sem("lam_dve")

        bd_loaded, xc0_done, xc_done = sem("bd_loaded"), sem("xc0_done"), sem("xc_done")
        conv_done, u_done, z_done = sem("conv_done"), sem("u_done"), sem("z_done")
        gate_mm, gate_ev, ath_done, m2_done, sqrt_done = sem("gate_mm"), sem("gate_ev"), sem("ath_done"), sem("m2_done"), sem("sqrt_done")
        out_done, lru_done = sem("out_done"), sem("lru_done")
        qsq_done, st_done, rt_done, qn_done = two("qsq_done"), two("st_done"), two("rt_done"), two("qn_done")
        qsh_done, qsl_done = two("qsh_done"), two("qsl_done")
        qn_stored = two("qn_stored")
        sqc_done = sem("sqc_done")
        v_stored = two("v_stored")

        bt_fill = sem("bt_fill")
        sm_ld, sm_dve, sm_pe, sm_act, sm_max = sem("sm_ld"), sem("sm_dve"), sem("sm_pe"), sem("sm_act"), sem("sm_max")
        kv_ld, kv_used = two("kv_ld"), two("kv_used")
        v_ld, qk_ld, au_mm, au_ev, g_stored, o_stored = sem("v_ld"), sem("qk_ld"), sem("au_mm"), sem("au_ev"), two("g_stored"), sem("o_stored")
        vt_mm, vt_ev, s_mm, sa_done, nm_done, exp_done, pt_mm, pt_ev, pv_mm, o_ev = (
            sem(n) for n in ("vt_mm", "vt_ev", "s_mm", "sa_done", "nm_done", "exp_done", "pt_mm", "pt_ev", "pv_mm", "o_ev"))
        gl_ld = two("gl_ld")
        ol_ld, cb_free, dm_done, ce_done, on_done, ot_mm, ot_done = (
            two("ol_ld"), two("cb_free"), sem("dm_done"), sem("ce_done"), sem("on_done"), sem("ot_mm"), sem("ot_done"))
        side_ld, mrg_sum, mrg_hi, mrg_done = two("side_ld"), two("mrg_sum"), two("mrg_hi"), two("mrg_done")
        xr_ld, xr_free, wo_done = two("xr_ld"), two("xr_free"), sem("wo_done")
        sg_free, h_done, y_stored = sem("sg_free"), sem("h_done"), sem("y_stored")

        kv = [big1_f32[:, a, 4:8, :].rearrange("p a n -> p (a n)") for a in range(2)]
        kc = [kv[g % 2][:, 0:NB * 4 * n].rearrange("p (b f n) -> p b f n", b=NB, f=4) for g, n in enumerate(NKEY)]
        vc = [kv[(g + 1) % 2][0:n, 0:NB * 512].rearrange("p (b f) -> p b f", b=NB) for g, n in enumerate(NKEY)]
        small = ext[:, 1:3, :].rearrange("p a n -> p (a n)")
        ROWS = NB * HG

        def spart(a, n, p=P):
            return small[0:p, a:a + n]

        qm, pm, sqs, rms = (spart(192 * n, 192) for n in range(4))
        srow, sbias = spart(768, 323, ROWS), spart(1091, 387, ROWS)
        pts, hm, dsel = spart(1478, 192), spart(1670, P, ROWS), spart(1798, 32, ROWS)
        r3, rsel, ul8 = spart(1830, 96, ROWS), spart(1926, ROWS, HG), spart(768, 387, HG)
        osum = spart(1990, 32)
        sstat = st[0:ROWS]
        osam = stc[:, 0:4, 0:NB]

        QT, KTT, VT = tmp(0)[:, 0:SEQ], tmp(1)[:, 0:SEQ], tmp(2)[:, 0:SEQ]
        SB = [tmp(3)[:, 512 * n:512 * n + 512] for n in range(2)]
        PTS = [tmp(4)[:, 512 * n:512 * n + 512] for n in range(2)]
        OT = x1[:, 5:7, :].rearrange("p a n -> p (a n)")[:, 0:16 * (HD + 2)].rearrange("p (b h e) -> p b h e", b=8, h=2)
        VTOK = ext[:, 1:3, :].rearrange("p a n -> p (a n)")[:, 0:16 * (HD + 1)].rearrange("p (b h e) -> p b h e", b=8, h=2)
        BT = ext[:, 0, 0:512].rearrange("p (h n) -> p h n", h=2)
        NM = ext[:, 0, 512:516]
        GT = [tmp(7), ext[:, 3, 0:NT]]
        s_bank = [ups[:, 1, 0, :], ups[:, 1, 1, :]]
        pt_bank = [ups[:, 1, 2, :], aux[:, 0, :]]
        o_bank = aux[:, 1, :]

        def toks(ap, g, b, n=1):
            if g == 0:
                return ap[:, (b + 1 - n) * P:(b + 1) * P]
            if g == 1:
                return ap.rearrange("p (m d) -> p d m", d=4)[:, b // 2, (b % 2 + 1 - n) * P:(b % 2 + 1) * P]
            return ap.rearrange("p (m d) -> p d m", d=8)[:, b]

        def nkeys(g, b):
            return (2 if b else 1, 1 + b % 2, 1)[g]

        PIECES = (8, 15, 20, 24, 28, 32, 36, 39, 42, 45, 48)

        OL = [x1[:, 2 * n:2 * n + 2, :].rearrange("p a n -> p (a n)")[:, 0:NG * HG * (HD + 2)]
              .rearrange("p (g h e) -> p g h e", g=NG, h=HG) for n in range(2)]
        mt = tmp(4)[:, 0:8]
        ce, cl, cc = (tmp(4)[:, 32 * n:32 * n + 24].rearrange("p (g h) -> p g h", g=NG) for n in range(1, 4))
        den = tmp(4)[:, 128:136]
        oacc, oprod = (tmp(5 + n)[:, 0:512].rearrange("p (h e) -> p h e", h=HG) for n in range(2))

        ups_v = [ups[:, j, :, 0:CH] for j in range(2)]

        def apart(eng):
            eng.sem_inc(ticks, 1)

        def part(ap, c):
            return ap[:, c * CH:(c + 1) * CH]

        def by_pool(c, k):
            return c > 0 and k in POOL_LOW

        def wait_split(eng, r, c, k):
            done = [by_pool(*divmod(n, KT)) for n in range(c * KT + k + 1)]
            every = [by_pool(*divmod(n, KT)) for n in range(NCH * KT)]
            eng.wait_ge(nlo_pool if done[-1] else nlo_dve, r * every.count(done[-1]) + done.count(done[-1]))

        def chunks(ap):
            return ap.rearrange("p (c n) -> p c n", c=NCH)

        consts = [
            (ident[:], A["c_ident"]), (hsel[:], A["c_hsel"]),
            (stc[:], A["c_state"]), (bones[:], A["c_bones"]),
            (gmix[:], A["c_norm_mix"]), (gffn[:], A["c_norm_ffn"]), (bmrg[:], A["c_b_merge"]),
            (par[:], A["c_par"]), (gq2[:], A["c_gains"]),
        ]
        CONSTS = 16 * len(consts)
        kv_loads = [(kc[g], A[f"kc{g}"]) for g in range(NG)] + [(vc[g], A[f"vc{g}"]) for g in range(NG)]
        sm_loads = [(hm, A["c_hm"]), (dsel, A["c_dsel"]), (rsel, A["c_rsel"]),
                     (ul8.rearrange("h (g n) -> h g n", g=NG), u_s.rearrange("(g h) n -> h g n", g=NG)[:, :, 127:256])]
        SM_LD = 16 * len(sm_loads)
        O_STORES = 16 * (1 + 4 + 8 + 4)
        block = ctx.enter_context(nc.Block())

        @block.sync
        def _(sp):
            for k in range(KT):
                sp.dma_start(tmp(k), A["x_T"][k]).then_inc(x_loaded[k], 16)
            for name, iters, nk, src, f0, f1, step, k0 in stream:
                first = 0

                def weights(i, slot):
                    f = (f0, f1)[slot]
                    sp.wait_ge(w_split[slot], i + (T0[name] + 1))
                    sp.dma_start(wraw[:, slot, 0:nk, :],
                                 src[ds(i * step + f, 1), :, k0:k0 + nk, :].rearrange("a p k n -> p (a k) n")).then_inc(w_loaded[slot], 16)

                if name == "ylru":
                    def outputs(n):
                        if n >= 2:
                            sp.wait_ge(cb_free[n % 2], n // 2)
                        sp.dma_start(OL[n % 2], o_s[:, n * P:(n + 1) * P].rearrange("g t h e -> t g h e")).then_inc(ol_ld[n % 2], 16)

                    def cache(n):
                        if n >= 2:
                            sp.wait_ge(kv_used[n % 2], n // 2)
                        sp.dma_start(*kv_loads[n]).then_inc(kv_ld[n % 2], 16)

                    weights(0, 0)
                    weights(0, 1)
                    for j in range(2):
                        sp.wait_ge(unit_done[j], T0["ylru"] + 1)
                    cache(0)
                    sp.wait_ge(o_stored, O_STORES)
                    outputs(0)
                    outputs(1)
                    cache(1)
                    weights(1, 0)
                    weights(1, 1)
                    outputs(2)
                    cache(2)
                    weights(2, 0)
                    outputs(3)
                    cache(3)
                    weights(2, 1)
                    outputs(4)
                    cache(4)
                    weights(3, 0)
                    outputs(5)
                    weights(3, 1)
                    outputs(6)
                    outputs(7)
                    cache(5)
                    continue
                if name == "lru":
                    first = 1
                    weights(0, 0)
                    weights(0, 1)
                    for dst, con in consts:
                        sp.dma_start(dst, con).then_inc(const_ld, 16)
                with sp.Fori(first, iters) as i:
                    for slot in range(2):
                        weights(i, slot)
                    if name.startswith("att"):
                        g = int(name[3])
                        for j in range(2):
                            if g == 0:
                                sp.wait_ge(qn_stored[j], 16 * 13)
                                sp.wait_ge(v_stored[j], 16 * 3)
                                sp.wait_ge(bt_fill, 16)
                            else:
                                sp.wait_ge(g_stored[j], 16 * (2 * g + 1))
                        sp.wait_ge(sa_done, 2)
                        sp.wait_ge(vt_mm, i + (4 * g + 1))
                        sp.dma_start(VT, qkv_s[ds(i + (24 + 4 * g), 1)].rearrange("a p t -> p (a t)")).then_inc(v_ld, 16)
                        sp.wait_ge(sa_done, i * 8 + (32 * g + 2))
                        for n, t in enumerate((QT, KTT)):
                            sp.dma_start(t, qkv_s[ds(i + (12 * n + 4 * g), 1)].rearrange("a p t -> p (a t)")).then_inc(qk_ld, 16)
                        sp.dma_start(BT, bt_s[ds(i * 2 + 8 * g, 2)].rearrange("h p n -> p h n")).then_inc(qk_ld, 16)
                    if name == "merge":
                        for j in range(2):
                            sp.wait_ge(g_stored[j], 16 * 17)
                            sp.wait_ge(mrg_sum[j], i + 1)
                            for n in range(2):
                                sp.dma_start(tmp(3 * j + n), gate_s[ds(i * 2 + (8 * n + j), 1)].rearrange("a p t -> p (a t)"))\
                                    .then_inc(side_ld[j], 16)
                    if name == "wo":
                        for j in range(2):
                            sp.wait_ge(xr_free[j], i + 1)
                            sp.dma_start(ext[:, 3 * j, 0:NT], A["x_T"][ds(i * 2 + j, 1)].rearrange("a p t -> p (a t)")).then_inc(xr_ld[j], 16)

        @block.gpsimd
        def _(pool):
            nc.gpsimd.memset(bd[:], 0.0).then_inc(bd_zero, 1)
            for j in range(2):
                pool.sem_inc(w_split[j], 1)

            def split(name, nk, i, slot):
                pool.wait_ge(w_loaded[slot], i * 16 + 16 * (T0[name] + 1))
                pool.wait_ge(unit_done[slot], i + (T0[name] + 1))
                apart(pool)
                raw, hi, lo = wraw[:, slot, 0:nk, :], wsp[:, slot, 0, 0:nk, :], wsp[:, slot, 1, 0:nk, :]
                nc.gpsimd.tensor_copy(hi, raw).then_inc(w_hi, 1)
                pool.wait_ge(w_hi, i * 2 + (2 * T0[name] + slot + 1))
                nc.gpsimd.tensor_tensor(lo, raw, hi.bitcast(F32), ALU.subtract).then_inc(w_split[slot], 1)

            for name, iters, nk, *_ in stream:
                first = 0
                if name in ("lru", "up0"):
                    first, r = 1, int(name == "up0")
                    split(name, nk, 0, 0)
                    split(name, nk, 0, 1)
                    for c in range(1, NCH):
                        for k in POOL_LOW:
                            pool.wait_ge(nhi_done, KT * (NCH * r + c) + k + 1)
                            nc.gpsimd.tensor_tensor(part(big1[:, 1, k, :], c), part(normed[k % 3], c), part(big1[:, 0, k, :], c).bitcast(F32),
                                                    ALU.subtract).then_inc(nlo_pool, 1)
                with pool.Fori(first, iters) as i:
                    for slot in range(2):
                        split(name, nk, i, slot)

        @block.tensor
        def _(pe):
            def unit(name, i, slot, src, nk=KT, parts=(0, 1, 2), ready=None):
                if 0 in parts:
                    pe.wait_ge(w_split[slot], i + (T0[name] + 2))
                    pe.wait_ge(ps_free[slot], i + (T0[name] + 1 - (12 if T0[name] >= T0["ylru"] else 0)))
                for c in parts:
                    for k in range(nk):
                        if ready:
                            ready(c, k)
                        for w, a in ((0, 0), (0, 1), (1, 0)):
                            ins = nc.tensor.matmul(ups[:, slot, c, 0:CH], wsp[:, slot, w, k, :], src[:, a, k, c * CH:(c + 1) * CH],
                                                   start=(k == 0 and w + a == 0), stop=(k == nk - 1 and w == 1))
                if NCH - 1 in parts:
                    ins.then_inc(unit_done[slot], 1)

            for j in range(2):
                pe.sem_inc(unit_done[j], 1)
            pe.sem_inc(gate_mm, 1)
            def norm_sums(r):
                pe.wait_ge(nadd_done, (KT + 1) * (r + 1))
                for c in range(NCH):
                    nc.tensor.matmul(ups[:, 0, c, 0:CH], ones[:], part(sums, c), start=True, stop=True).then_inc(nst_mm, 1)

            pe.wait_ge(ones_done, 1)
            norm_sums(0)

            def gates(i, c):
                if c == 0:
                    pe.wait_ge(bd_loaded, i * 64 + 64)
                    pe.wait_ge(xc_done, i + 1)
                pe.wait_ge(gate_ev, i * NCH + (c + 1))
                for a in range(2):
                    ins = nc.tensor.matmul(aux[:, a, 0:CH], bd[:, a, :], tmp(0)[:, c * CH:(c + 1) * CH], start=True, stop=True)
                ins.then_inc(gate_mm, 1)

            def lru(i, first):
                for c in range(NCH):
                    unit("lru", i, 0, big1, parts=(c,), ready=partial(wait_split, pe, 0) if first else None)
                    if first:
                        unit("lru", i, 1, big1, parts=(c,))
                    elif c < 2:
                        gates(i - 1, c + 1)
                if not first:
                    unit("lru", i, 1, big1)
                gates(i, 0)

            lru(0, True)
            with pe.Fori(1, KT) as i:
                lru(i, False)
            gates(KT - 1, 1)
            gates(KT - 1, 2)
            pe.wait_ge(gate_ev, KT * NCH + 1)
            def stats(j, i):
                pe.wait_ge(qsl_done[j], i + 1)
                pe.wait_ge(rt_done[1 - j], i + 1)
                for c in range(2):
                    for a in range(2):
                        ins = nc.tensor.matmul(aux[:, c, :], bones_r[:], sq_parts[a][:, c * 512:(c + 1) * 512], start=(a == 0), stop=(a == 1))
                ins.then_inc(st_done[j], 1)

            def qk(i, first):
                for j in range(2):
                    unit("qk", i, j, big1, parts=(0, 1))
                    if j:
                        stats(0, i)
                    elif not first:
                        stats(1, i - 1)
                    unit("qk", i, j, big1, parts=(2,))

            pe.sem_inc(rt_done[1], 1)
            pe.sem_inc(st_done[1], 1)
            qk(0, True)
            with pe.Fori(1, 12) as i:
                qk(i, False)
            def bias_line(g):
                return nc.tensor.matmul(aux[0:HG, g % 2, 0:UL], relx[:, g * HG:(g + 1) * HG], lines[:, g * UL:(g + 1) * UL], start=True, stop=True)

            unit("v", 0, 0, big1, parts=(0, 1))
            stats(1, 11)
            unit("v", 0, 0, big1, parts=(2,))
            pe.wait_ge(rt_done[1], 13)
            pe.wait_ge(lines_ld, 48)
            bias_line(0)
            bias_line(1).then_inc(u_ps, 1)
            unit("v", 0, 1, big1)
            pe.wait_ge(u_sb, 1)
            bias_line(2).then_inc(u_ps, 1)
            unit("v", 1, 0, big1)
            unit("v", 1, 1, big1)
            pe.wait_ge(ps_free[0], T0["att0"] + 1)
            pe.wait_ge(ps_free[1], T0["att0"] + 1)
            pe.wait_ge(u_sb, 2)

            pe.sem_inc(vt_mm, 1)
            for g in range(NG):
                with pe.Fori(0, 4) as i:
                    def pieces(a, b):
                        for n in range(a, b):
                            slot, c, k = n // 24, n // 8 % 3, n % 8
                            if n % 24 == 0:
                                pe.wait_ge(w_split[slot], i + (T0[f"att{g}"] + 2))
                            if n % 8 == 0:
                                pe.wait_ge(au_ev, i * 6 + (24 * g + n // 8 + 1))
                            for w, a2 in ((0, 0), (0, 1), (1, 0)):
                                ins = nc.tensor.matmul(ups[:, 0, c, 0:CH], wsp[:, slot, w, k, :], big1[:, a2, k, c * CH:(c + 1) * CH],
                                                       start=(k == 0 and w + a2 == 0), stop=(k == KT - 1 and w == 1))
                            if n % 8 == 7:
                                ins.then_inc(au_mm if c < NCH - 1 else unit_done[slot], 1)

                    pieces(0, 8)
                    pe.wait_ge(v_ld, i * 16 + 16 * (4 * g + 1))
                    pe.wait_ge(pt_ev, i * 8 + (32 * g + 2))
                    for b in range(8):
                        ins = nc.tensor.transpose(pt_bank[b // 4][:, (b % 4) * P:(b % 4 + 1) * P], toks(VT, g, b), ident[:])
                    ins.then_inc(vt_mm, 1)
                    pe.wait_ge(qk_ld, i * 48 + 48 * (4 * g + 1))
                    for n in range(10):
                        if n < 8:
                            hh, bp = n // 4, n % 4
                            hr = slice(hh * HD, (hh + 1) * HD)
                            pe.wait_ge(sa_done, i * 8 + (32 * g + n + 1))
                            for m in range(2):
                                b = 2 * bp + m
                                nk = nkeys(g, b)
                                ins = nc.tensor.matmul(s_bank[n % 2][:, 256 * m + 256 - P * nk:256 * m + 256], toks(QT, g, b)[hr],
                                                       toks(KTT, g, b, nk)[hr], start=True, stop=True)
                            ins.then_inc(s_mm, 1)
                        if 1 <= n <= 8:
                            q = n - 1
                            pe.wait_ge(exp_done, i * 8 + (32 * g + q + 1))
                            pe.wait_ge(pt_ev, i * 8 + (32 * g + q + 1))
                            if q == 0:
                                pe.wait_ge(vt_ev, i + (4 * g + 1))
                            for m in range(2):
                                for c in range(256 * m + 256 - P * nkeys(g, 2 * (q % 4) + m), 256 * m + 256, P):
                                    ins = nc.tensor.transpose(pt_bank[q % 2][:, c:c + P], SB[q % 2][:, c:c + P], ident[:])
                            ins.then_inc(pt_mm, 1)
                        if n >= 2:
                            q = n - 2
                            hh, bp = q // 4, q % 4
                            pe.wait_ge(pt_ev, i * 8 + (32 * g + q + 3))
                            pe.wait_ge(o_ev, i * 8 + (32 * g + q + 1))
                            for m in range(2):
                                b = 2 * bp + m
                                nk = nkeys(g, b)
                                for k in range(nk):
                                    c = 256 * m + 256 - P * (nk - k)
                                    ins = nc.tensor.matmul(o_bank[:, m * (HD + 1):(m + 1) * (HD + 1)], PTS[q % 2][:, c:c + P],
                                                           VTOK[:, b + 1 - nk + k, hh, :], start=(k == 0), stop=(k == nk - 1))
                            ins.then_inc(pv_mm, 1)
                        pieces(*PIECES[n:n + 2])

            def head_squares():
                pe.wait_ge(sm_dve, 1)
                nc.tensor.matmul(aux[:, 1, 0:192], bones[:], sqs, start=True, stop=True).then_inc(sm_pe, 1)

            def bias_rows():
                pe.wait_ge(sm_ld, SM_LD)
                pe.wait_ge(sm_act, 1)
                nc.tensor.matmul(aux[0:ROWS, 1, 0:387], rsel, ul8, start=True, stop=True).then_inc(sm_pe, 1)

            def scores(g):
                pe.wait_ge(kv_ld[g % 2], 16 * (g // 2 + 1))
                pe.wait_ge(sm_dve, 2)
                nc.tensor.matmul(aux[0:ROWS, 1, 400 + g:401 + g], pm[:, 64 * g:64 * g + 64], ones[:, 0:1], start=True, stop=True)
                for f in range(4):
                    for b in range(NB):
                        at = 64 * g + 16 * f + 2 * b
                        ins = nc.tensor.matmul(aux[0:NKEY[g], 1, at:at + 2], kc[g][:, b, f, :], qm[:, at:at + 2], start=True, stop=True)
                ins.then_inc(kv_used[g % 2], 1)

            def score_rows():
                pe.wait_ge(sm_dve, 3)
                for g in range(NG):
                    ins = nc.tensor.transpose(aux[0:ROWS, 1, g * P:g * P + NKEY[g]], sqs[0:NKEY[g], 64 * g:64 * g + 64],
                                              ident[0:NKEY[g], 0:NKEY[g]])
                ins.then_inc(sm_pe, 1)

            def prob_columns():
                pe.wait_ge(sm_dve, 4)
                for g in range(NG):
                    nc.tensor.transpose(aux[0:NKEY[g], 1, 64 * g:64 * g + 64], srow[:, g * P:g * P + NKEY[g]], ident[0:ROWS, 0:ROWS])
                nc.tensor.matmul(aux[:, 1, 192:288], hm, r3, start=True, stop=True).then_inc(sm_pe, 1)

            def values(g):
                pe.wait_ge(kv_ld[(g + 1) % 2], 16 * ((g + 3) // 2 + 1))
                pe.wait_ge(sm_dve, 5)
                for f in range(4):
                    for b in range(NB):
                        at = 16 * f + 2 * b
                        ins = nc.tensor.matmul(aux[:, 1, 448 + at:450 + at], vc[g][:, b, f * P:(f + 1) * P],
                                               pts[0:NKEY[g], 64 * g + at:64 * g + at + 2],
                                               start=(g + f + b == 0), stop=(g == NG - 1), skip_group_check=True)
                ins.then_inc(kv_used[(g + 1) % 2], 1)

            def turn(n):
                pe.wait_ge(on_done, n + 1)
                if n:
                    pe.wait_ge(ot_done, n)
                for k in range(4):
                    ins = nc.tensor.transpose(aux[:, 0, k * P:(k + 1) * P], tmp(5)[:, k * P:(k + 1) * P], ident[:])
                ins.then_inc(ot_mm, 1)

            pe.wait_ge(lru_done, KT)
            pe.wait_ge(au_ev, 12 * 6 + NCH)
            pe.wait_ge(sa_done, 98)
            pe.wait_ge(pt_ev, 98)
            pe.wait_ge(o_ev, 97)
            def y_chunks(a, b):
                for m in range(a, b):
                    unit("ylru", m // 6, m // NCH % 2, big2, parts=(m % NCH,))

            y_chunks(0, 1)
            head_squares()
            y_chunks(1, 2)
            bias_rows()
            y_chunks(2, 5)
            turn(0)
            y_chunks(5, 6)
            scores(0)
            y_chunks(6, 7)
            turn(1)
            y_chunks(7, 8)
            scores(1)
            y_chunks(8, 10)
            turn(2)
            scores(2)
            y_chunks(10, 13)
            turn(3)
            score_rows()
            y_chunks(13, 15)
            turn(4)
            y_chunks(15, 16)
            prob_columns()
            y_chunks(16, 18)
            turn(5)
            y_chunks(18, 19)
            values(0)
            y_chunks(19, 20)
            values(1)
            y_chunks(20, 21)
            turn(6)
            y_chunks(21, 23)
            values(2)
            y_chunks(23, 24)
            turn(7)
            pe.wait_ge(ot_done, 9)
            with pe.Fori(0, 4) as i:
                unit("merge", i, 0, big1, nk=4)
                unit("merge", i, 1, big1, nk=4)

            def merged_ready(c, k):
                if c == 0:
                    pe.wait_ge(mrg_done[k % 2], k // 2 + 1)

            with pe.Fori(0, 4) as i:
                unit("wo", i, 0, big2, ready=merged_ready)
                unit("wo", i, 1, big2)
            norm_sums(1)
            for n, (f0, nf) in enumerate(PARTS):
                if n == 0:
                    for c in range(NCH):
                        unit("up0", 0, 0, big1, parts=(c,), ready=partial(wait_split, pe, 1))
                        unit("up0", 0, 1, big1, parts=(c,))
                with pe.Fori(int(n == 0), nf) as i:
                    unit(f"up{n}", i, 0, big1)
                    unit(f"up{n}", i, 1, big1)
                pe.wait_ge(h_done, f0 + nf - 1)

                def hidden_ready(c, k):
                    if (c, k) == (0, nf - 1):
                        pe.wait_ge(h_done, f0 + nf)

                with pe.Fori(0, 4) as i:
                    unit(f"down{n}", i, 0, big2, nk=nf, ready=hidden_ready)
                    unit(f"down{n}", i, 1, big2, nk=nf)


        @block.scalar
        def _(act):
            step = Chain(act, s_act)
            def gate_weights(i):
                act.wait_ge(gate_mm, i * NCH + 1)
                for a, wn in enumerate(("w_rg_a", "w_rg_x")):
                    src = A[wn][0].rearrange("n i j -> (n i) j")
                    for h in range(2):
                        act.dma_start(bd[h * HD:(h + 1) * HD, a, h * HD:(h + 1) * HD],
                                      src[ds(i * P + h * HD, HD), :]).then_inc(bd_loaded, 16)

            def square(r, k, at):
                if isinstance(k, int):
                    act.wait_ge(x_loaded[k], 16)
                    if k:
                        act.wait_ge(nadd_done, k)
                    nc.scalar.activation(ext[:, 1 + at, 0:NT], tmp(k), ACT.Square).then_inc(nsq_done, 1)
                else:
                    act.wait_ge(wo_done, k + 1)
                    act.wait_ge(nadd_done, k + (KT + 1))
                    apart(act)
                    nc.scalar.activation(ext[:, 1 + at, 0:NT], x1[:, ds(k, 1), :].rearrange("p a n -> p (a n)"), ACT.Square).then_inc(nsq_done, 1)

            def norm(r):
                for c in range(NCH):
                    act.wait_ge(nst_mm, NCH * r + c + 1)
                    nc.scalar.activation(part(rrms, c), ups[:, 0, c, 0:CH], ACT.Sqrt, scale=1.0 / D, bias=epst[:]).then_inc(nrt_done, 1)
                for c in range(NCH):
                    for k in range(KT):
                        act.wait_ge(nf_done, KT * (NCH * r + c) + k + 1)
                        nc.scalar.activation(part(big1[:, 0, k, :], c), part(normed[k % 3], c), ACT.Copy).then_inc(nhi_done, 1)

            for k in range(KT):
                square(0, k, k % 2)
            act.wait_ge(bd_zero, 1)
            gate_weights(0)
            norm(0)
            act.wait_ge(lam_dve, 1)
            nc.scalar.activation(lamt[:, 1, :], lamt[:, 0, :], ACT.Exp, scale=-1.0).then_inc(lam_act, 1)
            act.wait_ge(lam_dve, 2)
            nc.scalar.activation(lamt[:, 3, :], lamt[:, 2, :], ACT.Ln).then_inc(lam_act, 1)

            wait_split(act, 0, 2, 6)
            wait_split(act, 0, 2, 7)
            act.dma_start(lines.rearrange("p (g n) -> p g n", g=NG), A["c_lines"].rearrange("g b n -> b g n")).then_inc(lines_ld, 16)
            act.dma_start(relx[0:NBK, :], A["rel_bias"]).then_inc(lines_ld, 16)
            act.dma_start(relx[NBK:NBK + 1, :], A["c_one"]).then_inc(lines_ld, 16)
            act.sem_inc(gate_ev, 1)
            XC, GE, R, I, AD, M2, U, H = (tmp(n) for n in range(8))
            LX = ext[:, 0, :]

            def col(i, n):
                return par[:, ds(i, 1), n]

            def front(i):
                act.wait_ge(unit_done[0], i + (T0["lru"] + 2))
                act.wait_ge(conv_done, i + 1)
                nc.scalar.activation(chunks(LX[:, 3:3 + NT]), ups_v[0], ACT.Copy).then_inc(ps_free[0], 1)
                act.wait_ge(ps_free[0], i + (T0["lru"] + 2))
                act.wait_ge(u_done, i + 1)
                apart(act)
                nc.scalar.activation(XC[:, 0:SEQ], LX[:, 0:SEQ], ACT.Identity, bias=col(i, 4), scale=col(i, 0))
                nc.scalar.activation(XC[:, SEQ:NT], LX[:, SEQ + 3:NT + 3], ACT.Identity, bias=col(i, 4), scale=col(i, 3)).then_inc(xc0_done, 1)

            def gate(i, c):
                act.wait_ge(gate_mm, i * NCH + (c + 2))
                apart(act)
                nc.scalar.activation(R[:, c * CH:(c + 1) * CH], aux[:, 0, 0:CH], ACT.Sigmoid, bias=col(i, 5))
                nc.scalar.activation(I[:, c * CH:(c + 1) * CH], aux[:, 1, 0:CH], ACT.Sigmoid, bias=col(i, 6)).then_inc(gate_ev, 1)

            def side(i):
                gate(i, 1)
                act.wait_ge(unit_done[1], i + (T0["lru"] + 2))
                act.wait_ge(z_done, i + 1)
                nc.scalar.activation(chunks(GE), ups_v[1], ACT.Gelu_apprx_tanh).then_inc(ps_free[1], 1)
                gate(i, 2)

            def decay(i):
                act.wait_ge(gate_ev, i * NCH + (NCH + 1))
                apart(act)
                step.step(nc.scalar.activation(AD, R, ACT.Exp, scale=cdec[:, 0, ds(i, 1)]))
                apart(act)
                nc.scalar.activation(R, R, ACT.Tanh, scale=cdec[:, 1, ds(i, 1)]).then_inc(ath_done, 1)
                act.wait_ge(m2_done, i + 1)
                nc.scalar.activation(M2, M2, ACT.Sqrt).then_inc(sqrt_done, 1)

            front(0)
            gate(0, 0)
            with act.Fori(1, KT) as i:
                step.loop(i, 1, 1)
                side(i - 1)
                gate_weights(i)
                front(i)
                decay(i - 1)
                gate(i, 0)
            step.end(KT - 1)
            side(KT - 1)
            decay(KT - 1)
            act.wait_ge(lru_done, KT)
            act.dma_start(O["lru_out"], sout[:]).then_inc(out_done, 16)
            act.dma_start(O["state_out"], stc[:]).then_inc(out_done, 16)
            for j in range(2):
                act.sem_inc(qn_stored[j], 16)
                act.sem_inc(v_stored[j], 16)

            def evac(i, j):
                act.wait_ge(unit_done[j], i + (T0["qk"] + 2))
                act.wait_ge(qn_done[j], i + 1)
                nc.scalar.activation(chunks(tmp(j)), ups_v[j], ACT.Copy).then_inc(ps_free[j], 1)
                act.wait_ge(ps_free[j], i + (T0["qk"] + 2))
                nc.scalar.activation(tmp(2 + j)[:, 0:SEQ], tmp(j)[:, 0:SEQ], ACT.Square).then_inc(qsq_done[j], 1)
                act.wait_ge(qsq_done[j], i + 1)
                act.wait_ge(st_done[1 - j], i + 1)
                nc.scalar.activation(sq_parts[0], tmp(2 + j)[:, 0:SEQ], ACT.Copy).then_inc(qsh_done[j], 1)
                nc.scalar.activation(sqkv[:, ds(i * 2 + j, 1), :], tmp(j)[:, SEQ:NT], ACT.Copy).then_inc(sqc_done, 1)

            def store(i, j):
                act.wait_ge(qn_done[j], i + 2)
                act.dma_start(qkv_s[ds(i * 2 + j, 1), :, :].rearrange("a p t -> p a t"), tmp(6 + j)[:, 0:SEQ]).then_inc(qn_stored[j], 16)

            def root(i, j):
                act.wait_ge(st_done[j], i + (1 + j))
                act.wait_ge(qn_done[j], i + 1)
                nc.scalar.activation(tmp(4 + j)[:, 0:SEQ], aux[:].rearrange("p b n -> p (b n)"), ACT.Sqrt, scale=1.0 / HD, bias=epst[:])\
                    .then_inc(rt_done[j], 1)

            def qk(i, first):
                if not first:
                    root(i - 1, 1)
                evac(i, 0)
                if not first:
                    store(i - 1, 0)
                root(i, 0)
                evac(i, 1)
                if not first:
                    store(i - 1, 1)

            qk(0, True)
            with act.Fori(1, 12) as i:
                qk(i, False)
            root(11, 1)
            store(11, 0)
            store(11, 1)
            for n in range(4):
                i, j = n // 2, n % 2
                act.wait_ge(unit_done[j], i + (T0["v"] + 2))
                act.wait_ge(v_stored[j], i * 16 + 16)
                nc.scalar.activation(chunks(tmp(j)), ups_v[j], ACT.Copy).then_inc(ps_free[j], 1)
                act.wait_ge(ps_free[j], i + (T0["v"] + 2))
                nc.scalar.activation(sqkv[:, 24 + n, :], tmp(j)[:, SEQ:NT], ACT.Copy).then_inc(sqc_done, 1)
                act.dma_start(qkv_s[24 + n], tmp(j)[:, 0:SEQ]).then_inc(v_stored[j], 16)
                if n == 1:
                    act.wait_ge(u_sb, 2)
                    act.dma_start(u_s.rearrange("(g h) n -> h g n", g=NG), u_lines).then_inc(u_stored, 16)
                if n == 2:
                    act.wait_ge(u_stored, 16)
                    act.dma_start(bt_s, bass.AP(tensor=u_s.tensor, offset=0, ap=[[UL, NG * HG], [1, P], [1, 2 * P]])).then_inc(bt_fill, 16)
            for j in range(2):
                act.wait_ge(v_stored[j], 16 * 3)
                act.wait_ge(qn_stored[j], 16 * 13)
            act.sem_inc(pt_ev, 2)
            act.sem_inc(au_ev, NCH)
            act.sem_inc(o_stored, 16)
            for j in range(2):
                act.sem_inc(g_stored[j], 16)
            for g in range(NG):
                with act.Fori(0, 4) as i:
                    def evac(n):
                        j, c = n // NCH, n % NCH
                        if c < NCH - 1:
                            act.wait_ge(au_mm, i * 4 + (16 * g + 2 * j + c + 1))
                        else:
                            act.wait_ge(unit_done[j], i + (T0[f"att{g}"] + 2))
                        if c == 0:
                            act.wait_ge(g_stored[j], i * 16 + (64 * g + 16))
                        apart(act)
                        to = GT[j][:, c * CH:(c + 1) * CH]
                        if g:
                            nc.scalar.activation(to, ups[:, 0, c, 0:CH], ACT.Tanh, scale=0.5,
                                                 bias=bmrg[:, ds(i * 2 + (8 * g - 8 + j), 1)]).then_inc(au_ev, 1)
                        else:
                            nc.scalar.activation(to, ups[:, 0, c, 0:CH], ACT.Copy).then_inc(au_ev, 1)
                        if c < NCH - 1:
                            return
                        act.wait_ge(au_ev, i * 6 + (24 * g + n + NCH + 1))
                        if g:
                            act.dma_start(gate_s[ds(i * 2 + (8 * g - 8 + j), 1)].rearrange("a p t -> p (a t)"), GT[j]).then_inc(g_stored[j], 16)
                        else:
                            nc.scalar.activation(sqkv[:, ds(i * 2 + (28 + j), 1), :], GT[j][:, SEQ:NT], ACT.Copy).then_inc(sqc_done, 1)
                            act.dma_start(qkv_s[ds(i * 2 + (28 + j), 1)].rearrange("a p t -> p (a t)"), GT[j][:, 0:SEQ]).then_inc(g_stored[j], 16)

                    act.wait_ge(vt_mm, i + (4 * g + 2))
                    act.wait_ge(pv_mm, i * 8 + (32 * g + 2))
                    for n in range(2):
                        ins = nc.scalar.activation(VTOK[:, 4 * n:4 * n + 4, :, 0:HD],
                                                   pt_bank[n].rearrange("p (b h e) -> p b h e", b=4, h=2), ACT.Copy)
                    ins.then_inc(vt_ev, 1)
                    for n in range(9):
                        if n >= 1:
                            q = n - 1
                            act.wait_ge(pt_mm, i * 8 + (32 * g + q + 3))
                            act.wait_ge(pv_mm, i * 8 + (32 * g + q + 1))
                            lo = 256 - P * nkeys(g, 2 * (q % 4))
                            if g < 2:
                                ins = nc.scalar.activation(PTS[q % 2][:, lo:512], pt_bank[q % 2][:, lo:512], ACT.Copy)
                            else:
                                ins = nc.scalar.activation(PTS[q % 2].rearrange("p (m c) -> p m c", m=2)[:, :, P:2 * P],
                                                           pt_bank[q % 2].rearrange("p (m c) -> p m c", m=2)[:, :, P:2 * P], ACT.Copy)
                            ins.then_inc(pt_ev, 1)
                        if n < 8:
                            act.wait_ge(nm_done, i * 8 + (32 * g + n + 1))
                            for m in range(2):
                                cols = slice(256 * m + 256 - P * nkeys(g, 2 * (n % 4) + m), 256 * m + 256)
                                ins = nc.scalar.activation(SB[n % 2][:, cols], SB[n % 2][:, cols], ACT.Exp,
                                                           bias=NM[:, 2 * (n % 2) + m:2 * (n % 2) + m + 1])
                            ins.then_inc(exp_done, 1)
                        if n in (0, 2, 4, 6, 8):
                            evac(n // 2)
                    evac(5)
                    act.wait_ge(o_ev, i * 8 + (32 * g + 9))
                    pair = o_s[g].rearrange("t (f h) e -> t f h e", h=2)[:, ds(i, 1)].rearrange("t a h e -> t (a h e)")
                    if g == 0:
                        act.dma_start(pair.rearrange("(b p) e -> p b e", p=P), OT.rearrange("p b h e -> p b (h e)")).then_inc(o_stored, 16)
                    elif g == 1:
                        for c in range(2):
                            act.dma_start(pair.rearrange("(c p r) e -> c p r e", c=2, r=4)[c],
                                          OT.rearrange("p (r c) h e -> p r c (h e)", c=2)[:, :, c]).then_inc(o_stored, 16)
                    else:
                        act.dma_start(pair.rearrange("(m b) e -> m b e", b=8), OT.rearrange("p b h e -> p b (h e)")).then_inc(o_stored, 16)
            for dst, src in sm_loads:
                act.dma_start(dst, src).then_inc(sm_ld, 16)

            def weigh(n):
                act.wait_ge(dm_done, n + 1)
                nc.scalar.activation(ce, ce, ACT.Exp).then_inc(ce_done, 1)

            def gate_load(n):
                j = n % 2
                act.wait_ge(g_stored[j], 16 * (13 + n // 2))
                act.dma_start(GT[j], gate_s[n]).then_inc(gl_ld[j], 16)

            def gate_store(n):
                act.wait_ge(ps_free[n % 2], T0["ylru"] + 2 + n // 2 - 12)
                act.dma_start(gate_s[n], GT[n % 2]).then_inc(g_stored[n % 2], 16)

            gate_load(0)
            gate_load(1)
            act.wait_ge(sm_pe, 1)
            nc.scalar.activation(rms, aux[:, 1, 0:192], ACT.Sqrt, scale=1.0 / HD, bias=epst[:]).then_inc(sm_act, 1)
            weigh(0)
            gate_store(0)
            act.wait_ge(sm_dve, 2)
            act.dma_start(O["sqkv"], sqkv[:]).then_inc(out_done, 16)
            for n in range(1, 4):
                weigh(n)
                gate_load(n + 1)
                gate_store(n)
            act.wait_ge(sm_max, 1)
            nc.scalar.activation(srow, srow, ACT.Exp, bias=sstat[:, 1:2], accum_out=sstat[:, 2:3]).then_inc(sm_act, 1)
            for n in range(4, 8):
                weigh(n)
                if n < 7:
                    gate_load(n + 1)
                gate_store(n)

            with act.Fori(0, 4) as i:
                for j in range(2):
                    act.wait_ge(mrg_sum[j], i + 2)
                    apart(act)
                    nc.scalar.activation(big2[:, 0, ds(i * 2 + j, 1), :], ext[:, 1 + j, 0:NT], ACT.Copy, scale=0.5).then_inc(mrg_hi[j], 1)
            with act.Fori(0, 4) as i:
                for j in range(2):
                    square(1, i * 2 + j, j)
            norm(1)
            for n, (f0, nf) in enumerate(PARTS):
                with act.Fori(0, nf) as i:
                    act.wait_ge(unit_done[0], i + (T0[f"up{n}"] + 2))
                    act.wait_ge(sg_free, i + (f0 + 1))
                    nc.scalar.activation(chunks(ext[:, 0, 0:NT]), ups_v[0], ACT.Silu).then_inc(ps_free[0], 1)
            with act.Fori(0, 4) as i:
                for j in range(2):
                    act.wait_ge(ps_free[j], i + (T0["down2"] + 2 - 12))
                    act.dma_start(O["y_T"][ds(i * 2 + j, 1)].rearrange("a p t -> p (a t)"), x1[:, ds(i * 2 + j, 1), :].rearrange("p a t -> p (a t)"))\
                        .then_inc(y_stored, 16)
            act.wait_ge(y_stored, 16 * KT)
            act.wait_ge(out_done, 48)
            act.wait_ge(o_stored, O_STORES)
            for j in range(2):
                act.wait_ge(g_stored[j], 16 * 17)


        @block.vector
        def _(dve):
            step = Chain(dve, s_dve)
            for s in (ps_free[0], ps_free[1], u_done, z_done):
                dve.sem_inc(s, 1)
            nc.vector.memset(epst[:], EPS)
            nc.vector.memset(ones[:], 1.0).then_inc(ones_done, 1)

            def norm_add(k, r, at):
                dve.wait_ge(nsq_done, k + 1)
                dve.wait_ge(nadd_done, k + (r + 1))
                nc.vector.tensor_tensor(sums, sums, ext[:, 1 + at, 0:NT], ALU.add).then_inc(nadd_done, 1)

            def norm(r, gain):
                def low(c, k):
                    if not by_pool(c, k):
                        dve.wait_ge(nhi_done, KT * (NCH * r + c) + k + 1)
                        nc.vector.tensor_tensor(part(big1[:, 1, k, :], c), part(normed[k % 3], c), part(big1[:, 0, k, :], c).bitcast(F32),
                                                ALU.subtract).then_inc(nlo_dve, 1)

                for c in range(NCH):
                    dve.wait_ge(nrt_done, NCH * r + c + 1)
                    step.step(nc.vector.reciprocal(part(rrms, c), part(rrms, c)))
                    for k in range(KT):
                        if k >= 3:
                            wait_split(dve, r, c, k - 3)
                        nc.vector.scalar_tensor_tensor(part(normed[k % 3], c), part(tmp(k), c), gain[:, k:k + 1], part(rrms, c),
                                                       ALU.mult, ALU.mult).then_inc(nf_done, 1)
                        if k >= 1:
                            low(c, k - 1)
                    low(c, KT - 1)

            nc.vector.memset(sums, 0.0).then_inc(nadd_done, 1)
            for k in range(KT):
                norm_add(k, 0, k % 2)
            dve.wait_ge(const_ld, CONSTS)
            norm(0, gmix)
            nc.vector.tensor_copy(bones_r[:], bones[:])
            for c in range(2):
                nc.vector.tensor_copy(gqk[:, 6 * c:6 * c + 6], gq2[:, c:c + 1].broadcast_to([P, 6]))
            step.step(nc.vector.tensor_scalar(bmrg[:], bmrg[:], 0.5, None, ALU.mult))
            lam = par[:, :, 7]
            step.step(nc.vector.tensor_scalar(lamt[:, 0, :], lam, -1.0, None, ALU.mult))
            nc.vector.tensor_tensor(lamt[:, 0, :], lamt[:, 0, :], lam, ALU.max).then_inc(lam_dve, 1)
            dve.wait_ge(lam_act, 1)
            nc.vector.tensor_scalar(lamt[:, 2, :], lamt[:, 1, :], 1.0, None, ALU.add).then_inc(lam_dve, 1)
            dve.wait_ge(lam_act, 2)
            step.step(nc.vector.tensor_scalar(lamt[:, 2, :], lamt[:, 2, :], -1.0, None, ALU.add))
            step.step(nc.vector.tensor_scalar(cdec[:, 0, :], lamt[:, 2, :], 0.0, None, ALU.is_equal))
            step.step(nc.vector.tensor_tensor(lamt[:, 2, :], lamt[:, 2, :], cdec[:, 0, :], ALU.add))
            step.step(nc.vector.tensor_tensor(lamt[:, 3, :], lamt[:, 3, :], cdec[:, 0, :], ALU.add))
            step.step(nc.vector.reciprocal(lamt[:, 2, :], lamt[:, 2, :]))
            step.step(nc.vector.tensor_tensor(lamt[:, 3, :], lamt[:, 3, :], lamt[:, 2, :], ALU.mult))
            step.step(nc.vector.tensor_tensor(lamt[:, 3, :], lamt[:, 3, :], lamt[:, 1, :], ALU.mult))
            step.step(nc.vector.tensor_scalar(lamt[:, 0, :], lam, -1.0, 0.0, ALU.mult, ALU.max))
            step.step(nc.vector.tensor_tensor(lamt[:, 3, :], lamt[:, 3, :], lamt[:, 0, :], ALU.add))
            step.step(nc.vector.tensor_scalar(cdec[:, 0, :], lamt[:, 3, :], -8.0, None, ALU.mult))
            step.step(nc.vector.tensor_scalar(cdec[:, 1, :], lamt[:, 3, :], 8.0, None, ALU.mult))
            wait_split(dve, 0, 2, 7)
            step.step(nc.vector.memset(ext[:, 0, 0:3], 0.0))

            dve.sem_inc(conv_done, 1)
            XC, GE, R, I, AD, M2, U, H = (tmp(n) for n in range(8))
            LX, GI = ext[:, 0, :], ext[:, 1, 0:NT]

            def gated(i):
                dve.wait_ge(gate_ev, i * NCH + (NCH + 1))
                nc.vector.tensor_tensor(GI, I, XC, ALU.mult).then_inc(u_done, 1)

            def conv(i):
                dve.wait_ge(xc0_done, i + 1)
                for k in range(1, 4):
                    step.step(nc.vector.scalar_tensor_tensor(XC[:, 0:SEQ], LX[:, k:k + SEQ], par[:, ds(i, 1), k], XC[:, 0:SEQ], ALU.mult, ALU.add))
                for k in range(3):
                    prev = stc[:, ds(i, 1), 0:3 * NB].rearrange("p a (b c) -> p a b c", c=3)[:, :, :, k]
                    ins = nc.vector.scalar_tensor_tensor(XC[:, SEQ:NT], prev, par[:, ds(i, 1), k], XC[:, SEQ:NT], ALU.mult, ALU.add)
                    if k < 2:
                        step.step(ins)
                ins.then_inc(xc_done, 1)
                nc.vector.tensor_copy(sout[:, ds(i, 1), 0:11], LX[:, SEQ:SEQ + 11]).then_inc(conv_done, 1)

            def recur(i):
                dve.wait_ge(ath_done, i + 1)
                step.step(nc.vector.tensor_tensor(M2, AD, AD, ALU.mult))
                nc.vector.scalar_tensor_tensor(M2, M2, 1.0, R, ALU.add, ALU.mult).then_inc(m2_done, 1)
                dve.wait_ge(sqrt_done, i + 1)
                step.step(nc.vector.memset(M2[:, 0:1], 1.0))
                dve.wait_ge(u_done, i + 2)
                step.step(nc.vector.tensor_tensor(U, M2, GI, ALU.mult))
                step.step(nc.vector.tensor_tensor_scan(H[:, 0:SEQ], AD[:, 0:SEQ], U[:, 0:SEQ], 0.0, ALU.mult, ALU.add))
                step.step(nc.vector.tensor_tensor(H[:, SEQ:NT], AD[:, SEQ:NT], stc[:, ds(i, 1), 3 * NB:4 * NB], ALU.mult))
                step.step(nc.vector.tensor_tensor(H[:, SEQ:NT], H[:, SEQ:NT], U[:, SEQ:NT], ALU.add))
                nc.vector.tensor_copy(sout[:, ds(i, 1), 11:20], H[:, SEQ - 1:NT])
                step.step(nc.vector.tensor_tensor(U, H, GE, ALU.mult))
                dve.sem_inc(z_done, 1)
                step.step(nc.vector.tensor_copy(big2[:, 0, ds(i, 1), :], U))
                step.step(nc.vector.tensor_tensor(big2[:, 1, ds(i, 1), :], U, big2[:, 0, ds(i, 1), :].bitcast(F32), ALU.subtract))
                dve.sem_inc(lru_done, 1)

            conv(0)
            with dve.Fori(1, KT) as i:
                step.loop(i, 14, 1)
                gated(i - 1)
                conv(i)
                recur(i - 1)
            step.end(KT - 1)
            gated(KT - 1)
            recur(KT - 1)

            for j in range(2):
                dve.sem_inc(qn_done[j], 1)
            def square_low(i, j):
                dve.wait_ge(qsh_done[j], i + 1)
                nc.vector.tensor_tensor(sq_parts[1], tmp(2 + j)[:, 0:SEQ], sq_parts[0].bitcast(F32), ALU.subtract).then_inc(qsl_done[j], 1)

            def normed_qk(i, j):
                rms_t = tmp(4 + j)[:, 0:SEQ]
                dve.wait_ge(rt_done[j], i + (1 + j))
                step.step(nc.vector.reciprocal(rms_t, rms_t))
                dve.wait_ge(qn_stored[j], i * 16 + 16)
                nc.vector.scalar_tensor_tensor(tmp(6 + j)[:, 0:SEQ], tmp(j)[:, 0:SEQ], gqk[:, ds(i, 1)],
                                               rms_t, ALU.mult, ALU.mult).then_inc(qn_done[j], 1)

            square_low(0, 0)
            with dve.Fori(0, 11) as i:
                step.loop(i, 2)
                normed_qk(i, 0)
                square_low(i, 1)
                normed_qk(i, 1)
                square_low(i + 1, 0)
            step.end(11)
            step.loop(11, 2, 11)
            normed_qk(11, 0)
            square_low(11, 1)
            normed_qk(11, 1)
            step.end(1)

            dve.wait_ge(u_ps, 1)
            nc.vector.tensor_copy(u_lines[:, 0:2, :], aux[0:HG, :, 0:UL]).then_inc(u_sb, 1)
            dve.wait_ge(u_ps, 2)
            nc.vector.tensor_copy(u_lines[:, 2, :], aux[0:HG, 0, 0:UL]).then_inc(u_sb, 1)

            dve.wait_ge(u_stored, 16)
            dve.wait_ge(sqc_done, 28)
            dve.wait_ge(qn_stored[0], 16 * 13)
            nc.vector.memset(VTOK[:, :, :, HD:HD + 1], 1.0)
            for s, n in ((sa_done, 2), (pt_mm, 2), (pv_mm, 2), (o_ev, 1)):
                dve.sem_inc(s, n)
            stores = 1
            for g in range(NG):
                per = 2 if g == 1 else 1
                with dve.Fori(0, 4) as i:
                    dve.wait_ge(qk_ld, i * 48 + 48 * (4 * g + 1))
                    dve.wait_ge(o_stored, i * (16 * per) + 16 * stores)
                    step.loop(i, 8)
                    for n in range(10):
                        if n < 8:
                            hh, bp = n // 4, n % 4
                            dve.wait_ge(s_mm, i * 8 + (32 * g + n + 1))
                            dve.wait_ge(pt_mm, i * 8 + (32 * g + n + 1))
                            for m in range(2):
                                nk = nkeys(g, 2 * bp + m)
                                cols = slice(256 * m + 256 - P * nk, 256 * m + 256)
                                ins = nc.vector.scalar_tensor_tensor(SB[n % 2][:, cols], s_bank[n % 2][:, cols], SCALE,
                                                                     BT[:, hh, 0:P * nk][:, ::-1], ALU.mult, ALU.add)
                            ins.then_inc(sa_done, 1)
                            dve.wait_ge(sa_done, i * 8 + (32 * g + n + 3))
                            for m in range(2):
                                cols = slice(256 * m + 256 - P * nkeys(g, 2 * bp + m), 256 * m + 256)
                                ins = nc.vector.tensor_reduce(OT[:, 2 * bp + m, hh, HD + 1:HD + 2], SB[n % 2][:, cols], AX_X, ALU.max)
                            step.step(ins)
                            ins = nc.vector.tensor_scalar(NM[:, 2 * (n % 2):2 * (n % 2) + 2], OT[:, 2 * bp:2 * bp + 2, hh, HD + 1],
                                                          -1.0, None, ALU.mult).then_inc(nm_done, 1)
                        if n >= 2:
                            q = n - 2
                            hh, bp = q // 4, q % 4
                            dve.wait_ge(pv_mm, i * 8 + (32 * g + q + 3))
                            ins = nc.vector.tensor_copy(OT[:, 2 * bp:2 * bp + 2, hh, 0:HD + 1],
                                                        o_bank[:, 0:2 * (HD + 1)].rearrange("p (m e) -> p m e", m=2)).then_inc(o_ev, 1)
                step.end(4)
                stores += 4 * per

            def s_squares():
                dve.wait_ge(sqc_done, 36)
                nc.vector.tensor_tensor(sqs, sqkv[:, 0:24, :].rearrange("p f b -> p (f b)"), sqkv[:, 0:24, :].rearrange("p f b -> p (f b)"),
                                        ALU.mult).then_inc(sm_dve, 1)

            def s_norm():
                dve.wait_ge(sm_ld, SM_LD)
                dve.wait_ge(sm_pe, 2)
                nc.vector.tensor_copy(sbias, aux[0:ROWS, 1, 0:387])
                step.step(nc.vector.reciprocal(rms, rms))
                for c in range(2):
                    own = sqkv[:, 12 * c:12 * c + 12, :].rearrange("p f b -> p (f b)")
                    step.step(nc.vector.scalar_tensor_tensor(own, own, gqk[:, 6 * c:6 * c + 1], rms[:, 96 * c:96 * c + 96], ALU.mult, ALU.mult))
                qmv = qm.rearrange("p (f b h) -> p f b h", b=NB, h=2)
                for h in range(2):
                    step.step(nc.vector.tensor_scalar(qmv[:, :, :, h], sqkv[:, 0:12, :], hsel[:, h:h + 1], None, ALU.mult))
                nc.vector.tensor_tensor(pm.rearrange("p (f b h) -> p f b h", b=NB, h=2), qmv,
                                        sqkv[:, 12:24, :].unsqueeze(3).broadcast_to([P, 12, NB, 2]), ALU.mult).then_inc(sm_dve, 1)

            def s_scores():
                dve.wait_ge(kv_used[0], 2)
                nc.vector.tensor_copy(sqs[:, 0:128], aux[:, 1, 0:128])
                nc.vector.tensor_copy(sqs[0:64, 128:192], aux[0:64, 1, 128:192]).then_inc(sm_dve, 1)

            def s_bias():
                dve.wait_ge(sm_pe, 3)
                for g in range(NG):
                    n, skip = NKEY[g], 2 if g == 2 else 1
                    nc.vector.scalar_tensor_tensor(srow[:, g * P:g * P + n], aux[0:ROWS, 1, g * P:g * P + n], SCALE,
                                                   sbias[:, 129 * g + skip:129 * g + n * skip + 1:skip][:, ::-1], ALU.mult, ALU.add)
                step.step(nc.vector.scalar_tensor_tensor(srow[:, 320:323], aux[0:ROWS, 1, 400:403], SCALE,
                                                         sbias.rearrange("p (g n) -> p g n", g=NG)[:, :, 0], ALU.mult, ALU.add))
                step.step(nc.vector.tensor_reduce(sstat[:, 0:1], srow, AX_X, ALU.max))
                nc.vector.tensor_scalar(sstat[:, 1:2], sstat[:, 0:1], -1.0, None, ALU.mult).then_inc(sm_max, 1)

            def s_probs():
                dve.wait_ge(sm_act, 2)
                step.step(nc.vector.reciprocal(sstat[:, 3:4], sstat[:, 2:3]))
                step.step(nc.vector.tensor_scalar(srow, srow, sstat[:, 3:4], None, ALU.mult))
                for g in range(NG):
                    ins = nc.vector.tensor_scalar(r3[:, 32 * g:32 * g + 32], dsel, srow[:, 320 + g:321 + g], None, ALU.mult)
                ins.then_inc(sm_dve, 1)

            def s_own():
                dve.wait_ge(sm_pe, 4)
                step.step(nc.vector.tensor_tensor(rms[:, 0:96], aux[:, 1, 192:288], sqkv[:, 24:36, :].rearrange("p f b -> p (f b)"), ALU.mult))
                nc.vector.tensor_copy(pts[:, 0:128], aux[:, 1, 0:128])
                nc.vector.tensor_copy(pts[0:64, 128:192], aux[0:64, 1, 128:192]).then_inc(sm_dve, 1)
                step.step(nc.vector.tensor_tensor(osum, rms[:, 0:32], rms[:, 32:64], ALU.add))
                step.step(nc.vector.tensor_tensor(osum, osum, rms[:, 64:96], ALU.add))

            def s_output():
                dve.wait_ge(kv_used[1], 3)
                dve.wait_ge(out_done, 48)
                for h in range(2):
                    hr = slice(h * HD, (h + 1) * HD)
                    ins = nc.vector.tensor_tensor(osam[hr], osum.rearrange("p (f b) -> p f b", f=4)[hr],
                                                  aux[hr, 1, 448:512].rearrange("p (f b h) -> p f b h", f=4, h=2)[:, :, :, h], ALU.add)
                step.step(ins)
                hi, lo = (big1[:, a, 0:4, SEQ:NT] for a in range(2))
                step.step(nc.vector.tensor_copy(hi, osam))
                nc.vector.tensor_tensor(lo, osam, hi.bitcast(F32), ALU.subtract).then_inc(ot_done, 1)

            def split_turned(n):
                dve.wait_ge(ot_mm, n + 1)
                hi, lo = (big1[:, a, 0:4, n * P:(n + 1) * P] for a in range(2))
                src = aux[:, 0, :].rearrange("p (k t) -> p k t", k=4)
                step.step(nc.vector.tensor_copy(hi, src))
                nc.vector.tensor_tensor(lo, src, hi.bitcast(F32), ALU.subtract).then_inc(ot_done, 1)

            def combine(n):
                o = OL[n % 2]
                dve.wait_ge(ol_ld[n % 2], 16 * (n // 2 + 1))
                mx = [o[:, g, :, HD + 1] for g in range(NG)]
                step.step(nc.vector.tensor_tensor(mt, mx[0], mx[1], ALU.max))
                step.step(nc.vector.tensor_tensor(mt, mt, mx[2], ALU.max))
                nc.vector.tensor_tensor(ce, o[:, :, :, HD + 1], mt.unsqueeze(1).broadcast_to([P, NG, HG]), ALU.subtract).then_inc(dm_done, 1)
                dve.wait_ge(ce_done, n + 1)
                step.step(nc.vector.tensor_tensor(cl, ce, o[:, :, :, HD], ALU.mult))
                step.step(nc.vector.tensor_tensor(den, cl[:, 0], cl[:, 1], ALU.add))
                step.step(nc.vector.tensor_tensor(den, den, cl[:, 2], ALU.add))
                step.step(nc.vector.reciprocal(den, den))
                step.step(nc.vector.tensor_tensor(cc, ce, den.unsqueeze(1).broadcast_to([P, NG, HG]), ALU.mult))
                if n:
                    split_turned(n - 1)
                for g in range(NG):
                    cb = cc[:, g].unsqueeze(2).broadcast_to([P, HG, HD])
                    if g == 0:
                        step.step(nc.vector.tensor_tensor(oacc, o[:, g, :, 0:HD], cb, ALU.mult))
                    else:
                        step.step(nc.vector.tensor_tensor(oprod, o[:, g, :, 0:HD], cb, ALU.mult))
                        if g == 1:
                            step.step(nc.vector.tensor_tensor(oacc, oacc, oprod, ALU.add))
                        else:
                            dve.sem_inc(cb_free[n % 2], 1)
                            nc.vector.tensor_tensor(oacc, oacc, oprod, ALU.add).then_inc(on_done, 1)

            def y_lru(n):
                j = n % 2
                dve.wait_ge(gl_ld[j], 16 * (n // 2 + 1))
                dve.wait_ge(unit_done[j], T0["ylru"] + 2 + n // 2)
                nc.vector.scalar_tensor_tensor(chunks(GT[j]), chunks(GT[j]), 1.0, ups_v[j], ALU.add, ALU.mult).then_inc(ps_free[j], 1)

            s_squares()
            for j in range(2):
                dve.wait_ge(unit_done[j], T0["ylru"] + 1)
            def tokens(n):
                combine(n)
                y_lru(n)

            tokens(0)
            s_norm()
            tokens(1)
            tokens(2)
            s_scores()
            tokens(3)
            s_bias()
            tokens(4)
            s_probs()
            tokens(5)
            s_own()
            tokens(6)
            tokens(7)
            s_output()
            split_turned(7)

            dve.wait_ge(ot_done, 9)
            for s in (*mrg_sum, *xr_free, sg_free):
                dve.sem_inc(s, 1)
            with dve.Fori(0, 4) as i:
                step.loop(i, 2)
                for j in range(2):
                    gl, ga, both = tmp(3 * j), tmp(3 * j + 1), ext[:, 1 + j, 0:NT]
                    dve.wait_ge(side_ld[j], i * 32 + 32)
                    dve.wait_ge(unit_done[j], i + (T0["merge"] + 2))
                    step.step(nc.vector.scalar_tensor_tensor(chunks(ga), chunks(ga), 1.0, ups_v[j], ALU.add, ALU.mult))
                    dve.sem_inc(ps_free[j], 1)
                    nc.vector.tensor_tensor(both, gl, ga, ALU.add).then_inc(mrg_sum[j], 1)
                    dve.wait_ge(mrg_hi[j], i + 1)
                    nc.vector.scalar_tensor_tensor(big2[:, 1, ds(i * 2 + j, 1), :], both, 0.5, big2[:, 0, ds(i * 2 + j, 1), :].bitcast(F32),
                                                   ALU.mult, ALU.subtract).then_inc(mrg_done[j], 1)
            step.end(4)
            nc.vector.memset(sums, 0.0).then_inc(nadd_done, 1)
            with dve.Fori(0, 4) as i:
                for j in range(2):
                    dve.wait_ge(xr_ld[j], i * 16 + 16)
                    dve.wait_ge(unit_done[j], i + (T0["wo"] + 2))
                    apart(dve)
                    nc.vector.tensor_tensor(x1[:, ds(i * 2 + j, 1), :].rearrange("p a (c n) -> p (a c) n", c=NCH), ups_v[j],
                                            chunks(ext[:, 3 * j, 0:NT]), ALU.add).then_inc(wo_done, 1)
                    dve.wait_ge(wo_done, i * 2 + (j + 1))
                    dve.sem_inc(ps_free[j], 1)
                    dve.sem_inc(xr_free[j], 1)
                    norm_add(i * 2 + (j + KT), 1, j)
            norm(1, gffn)
            for n, (f0, nf) in enumerate(PARTS):
                if n:
                    for j in range(2):
                        dve.wait_ge(unit_done[j], T0[f"up{n}"] + 1)
                with dve.Fori(0, nf) as i:
                    step.loop(i, 3)
                    dve.wait_ge(ps_free[0], i + (T0[f"up{n}"] + 2 - 12))
                    dve.wait_ge(unit_done[1], i + (T0[f"up{n}"] + 2))
                    step.step(nc.vector.tensor_tensor(chunks(ext[:, 1, 0:NT]), chunks(ext[:, 0, 0:NT]), ups_v[1], ALU.mult))
                    dve.sem_inc(ps_free[1], 1)
                    dve.sem_inc(sg_free, 1)
                    step.step(nc.vector.tensor_copy(big2[:, 0, ds(i, 1), :], ext[:, 1, 0:NT]))
                    step.step(nc.vector.tensor_tensor(big2[:, 1, ds(i, 1), :], ext[:, 1, 0:NT], big2[:, 0, ds(i, 1), :].bitcast(F32), ALU.subtract))
                    dve.sem_inc(h_done, 1)
                step.end(nf)
                with dve.Fori(0, 4) as i:
                    for j in range(2):
                        dve.wait_ge(unit_done[j], i + (T0[f"down{n}"] + 2))
                        own = x1[:, ds(i * 2 + j, 1), :].rearrange("p a (c n) -> p (a c) n", c=NCH)
                        apart(dve)
                        nc.vector.tensor_tensor(own, ups_v[j], own, ALU.add).then_inc(ps_free[j], 1)



_IN = ["x_prompt", "x_sample", "cache_kv_g0", "cache_kv_g1", "cache_kv_g2", "state_conv", "state_h", "rel_bias", "norm_mix",
       "w_in", "w_conv", "b_conv", "w_rg_a", "b_rg_a", "w_rg_x", "b_rg_x", "lru_lambda", "q_gain", "k_gain", "w_merge",
       "b_merge", "w_branch_lru", "w_branch_att", "w_o", "norm_ffn", "w_ffn_in", "w_ffn_out"]
_OUT = [("y_T", (KT, P, NT)), ("qkv", (36, P, SEQ)), ("sqkv", (P, 36, NB)), ("lru_out", (P, KT, 20)), ("state_out", (P, KT, 4 * NB))]


def kernel(**inputs):
    import concourse.bacc as bacc
    from concourse.bass_utils import run_bass_kernel_spmd as run

    nc = bacc.Bacc("TRN2", target_bir_lowering=False, num_devices=1)
    a = {name: np.ascontiguousarray(inputs[name]) for name in _IN}

    def tiles(v):
        return np.ascontiguousarray(v.reshape(-1, KT, P).transpose(2, 1, 0))

    def weights(w):
        k, n = w.shape
        return np.ascontiguousarray(w.reshape(k // P, P, n // P, P).transpose(2, 1, 0, 3))

    hsel = np.zeros((P, 2), np.float32)
    hsel[:HD, 0] = hsel[HD:, 1] = 1.0
    arrays = dict(c_ident=np.eye(P, dtype=np.float32), c_hsel=hsel, c_one=np.ones((1, NG * HG), np.float32),
                  c_bones=np.kron(np.eye(2, dtype=np.float32), np.ones((HD, HD), np.float32)), c_lines=bucket_lines(),
                  rel_bias=a["rel_bias"], w_rg_a=a["w_rg_a"], w_rg_x=a["w_rg_x"])
    for n in ("w_in", "w_merge", "w_branch_lru", "w_branch_att", "w_o", "w_ffn_in", "w_ffn_out"):
        arrays[n] = weights(a[n][0])
    x = np.concatenate([a["x_prompt"][0], a["x_sample"][:, 0]])
    arrays["x_T"] = np.ascontiguousarray(x.T.reshape(KT, P, NT))
    arrays["c_par"] = tiles(np.concatenate([a["w_conv"][0], a["b_conv"], a["b_rg_a"], a["b_rg_x"], a["lru_lambda"]]))
    arrays["c_state"] = tiles(np.concatenate([a["state_conv"][0].reshape(-1, D), a["state_h"][0]]))
    arrays["c_gains"] = np.ascontiguousarray(np.stack([np.tile(a[n][0], 2) for n in ("q_gain", "k_gain")], axis=1))
    for n in ("norm_mix", "norm_ffn"):
        arrays["c_" + n] = tiles(a[n])[:, :, 0].copy()
    arrays["c_b_merge"] = np.ascontiguousarray(a["b_merge"].reshape(16, P).T)
    for g in range(NG):
        kv = a[f"cache_kv_g{g}"][0, :, ::DIL[g]]
        n = kv.shape[1]
        assert n == NKEY[g]
        arrays[f"kc{g}"] = np.ascontiguousarray(kv[:, :, 0].reshape(NB, n, 4, P).transpose(3, 0, 2, 1))
        arrays[f"vc{g}"] = np.ascontiguousarray(kv[:, :, 1].reshape(NB, n, 512).transpose(1, 0, 2))
    row = np.arange(NB * HG)
    arrays["c_hm"] = (row[:, None] % 2 == np.arange(P)[None] // HD).astype(np.float32)
    arrays["c_dsel"] = (row[:, None] // 2 == np.arange(32)[None]).astype(np.float32)
    arrays["c_rsel"] = (np.arange(HG)[:, None] == (2 * (row // 16) + row % 2)[None]).astype(np.float32)
    A = {n: nc.dram_tensor(n, v.shape, F32, kind="ExternalInput").ap() for n, v in arrays.items()}
    O = {n: nc.dram_tensor("out_" + n, shape, F32, kind="ExternalOutput").ap() for n, shape in _OUT}
    build(nc, A, O)
    r = run(nc, [arrays], core_ids=[0]).results[0]
    y = r["out_y_T"].reshape(D, NT).T
    qkv = r["out_qkv"].reshape(3, NG, HG * HD, SEQ)[1:].transpose(1, 3, 0, 2).reshape(NG, SEQ, 2, HG, HD)
    sqkv = r["out_sqkv"].transpose(1, 0, 2).reshape(3, NG, HG * HD, NB)[1:].transpose(1, 3, 0, 2).reshape(NG, NB, 2, HG, HD)
    lru = r["out_lru_out"].transpose(2, 1, 0).reshape(20, D)
    state = r["out_state_out"].transpose(2, 1, 0).reshape(4 * NB, D)[:3 * NB].reshape(NB, 3, D)
    conv_s = np.concatenate([state[:, 1:], lru[3:11, None]], axis=1)[None]
    return (y[None, :SEQ].copy(), y[SEQ:, None].copy(), *(qkv[g, None, None, SEQ - n:].copy() for g, n in enumerate((128, 512, 1024))),
            lru[None, None, 0:3].copy(), lru[None, 11:12].copy(), *(sqkv[g, None, :, None].copy() for g in range(NG)),
            conv_s, lru[None, 12:20].copy())
```
